# Optimizing a Trainium2 kernel written in Bass

```python
import math
import jax, jax.numpy as jnp
from jax import lax
import numpy as np

D_MODEL = 1024
BATCH = 1
SEQ = 256
DEPTH = 2

N_MIXERS = 2
HEAD_DIM = 64
N_HEADS = D_MODEL // HEAD_DIM
N_RWKV = (DEPTH + 1) // 2
N_MOBA = DEPTH // 2
DECAY_LORA = max(32, int(round(1.8 * D_MODEL ** 0.5 / 32)) * 32)
AAA_LORA = max(32, int(round(1.8 * D_MODEL ** 0.5 / 32)) * 32)
GATE_LORA = max(32, int(round(0.6 * D_MODEL ** 0.8 / 32)) * 32)
GN_EPS = HEAD_DIM * 1e-5
MOBA_BLOCK = 256
MOBA_TOPK = 3
Q_CHUNK = 128
ROPE_THETA = 10000.0
D_FF = -(-8 * D_MODEL // (3 * 256)) * 256
ALPHA = (2 * DEPTH) ** 0.25
BETA = (8 * DEPTH) ** -0.25
LN_EPS = 1e-5


def layer_norm(x, g, b):
    xf = x.astype(jnp.float32)
    mu = xf.mean(-1, keepdims=True)
    var = jnp.square(xf - mu).mean(-1, keepdims=True)
    return ((xf - mu) * lax.rsqrt(var + LN_EPS) * g + b).astype(x.dtype)

def swiglu_ffn(x, w_in, w_down):
    gate, up = jnp.split(x @ w_in, 2, axis=-1)
    return (jax.nn.silu(gate) * up) @ w_down

def time_shift(x):
    return jnp.pad(x, ((0, 0), (1, 0), (0, 0)))[:, :-1, :]

def rwkv7_time_mix(x, mu, w_rkv, w0, w1, w2, a0, a1, a2, g1, g2, k_k, k_a, r_k, gn_g, gn_b, w_o):
    B, T, C = x.shape
    H, N = N_HEADS, HEAD_DIM
    f32 = jnp.float32
    xx = time_shift(x) - x
    xr, xw, xk, xv, xa, xg = [x + xx * mu[n] for n in range(6)]
    r, k, v = jnp.einsum('nbtc,ncd->nbtd', jnp.stack([xr, xk, xv]), w_rkv)
    w = -jax.nn.softplus(-(w0 + jnp.tanh(xw @ w1) @ w2)) - 0.5
    a = jax.nn.sigmoid(a0 + (xa @ a1) @ a2)
    g = jax.nn.sigmoid(xg @ g1) @ g2
    heads = lambda t: t.reshape(B, T, H, N).astype(f32)
    kk = heads(k * k_k)
    kk = kk / jnp.maximum(jnp.sqrt(jnp.sum(kk * kk, -1, keepdims=True)), 1e-12)
    k = k * (1 + (a - 1) * k_a)
    rh, kh, vh, ah = heads(r), heads(k), heads(v), heads(a)
    decay = jnp.exp(-jnp.exp(heads(w)))

    def step(S, inp):
        r_t, w_t, k_t, v_t, kk_t, b_t = inp
        sa = jnp.einsum('bhvk,bhk->bhv', S, -kk_t)
        S = S * w_t[:, :, None, :] + sa[..., None] * b_t[:, :, None, :] + v_t[..., None] * k_t[:, :, None, :]
        return S, jnp.einsum('bhvk,bhk->bhv', S, r_t)

    to_time = lambda t: jnp.swapaxes(t, 0, 1)
    S0 = jnp.zeros((B, H, N, N), f32)
    _, y = lax.scan(step, S0, tuple(to_time(t) for t in (rh, decay, kh, vh, kk, kk * ah)))
    y = to_time(y)
    mean = y.mean(-1, keepdims=True)
    var = jnp.square(y - mean).mean(-1, keepdims=True)
    y = ((y - mean) * lax.rsqrt(var + GN_EPS)).reshape(B, T, C) * gn_g + gn_b
    bonus = jnp.sum(rh * kh * r_k, -1, keepdims=True) * vh
    y = (y + bonus.reshape(B, T, C)).astype(x.dtype)
    return (y * g) @ w_o

def rope_tables(T):
    inv = ROPE_THETA ** (-jnp.arange(0, HEAD_DIM, 2, dtype=jnp.float32) / HEAD_DIM)
    ang = jnp.arange(T, dtype=jnp.float32)[:, None] * inv[None, :]
    return jnp.cos(ang), jnp.sin(ang)

def apply_rope(t, cos, sin):
    t1, t2 = jnp.split(t, 2, axis=-1)
    return jnp.concatenate([t1 * cos - t2 * sin, t2 * cos + t1 * sin], axis=-1)

def moba_attention(x, w_qkv, w_o):
    B, T, C = x.shape
    H, Dh = N_HEADS, HEAD_DIM
    f32 = jnp.float32
    qkv = (x @ w_qkv).reshape(B, T, 3, H, Dh)
    q, k, v = [jnp.transpose(qkv[:, :, n], (0, 2, 1, 3)).astype(f32) for n in range(3)]
    cos, sin = rope_tables(T)
    q = apply_rope(q, cos, sin) * (Dh ** -0.5)
    k = apply_rope(k, cos, sin)
    NB = -(-T // MOBA_BLOCK)
    K = min(MOBA_TOPK, NB)
    pad = NB * MOBA_BLOCK - T
    kb = jnp.pad(k, ((0, 0), (0, 0), (0, pad), (0, 0))).reshape(B, H, NB, MOBA_BLOCK, Dh)
    vb = jnp.pad(v, ((0, 0), (0, 0), (0, pad), (0, 0))).reshape(B, H, NB, MOBA_BLOCK, Dh)
    k_mean = kb.mean(axis=3)
    bi = jnp.arange(B)[:, None, None, None]
    hi = jnp.arange(H)[None, :, None, None]
    blk_ids = jnp.arange(NB)
    key_off = jnp.arange(MOBA_BLOCK)
    q_off = jnp.arange(Q_CHUNK)

    def attend_chunk(c):
        q0 = c * Q_CHUNK
        own = q0 // MOBA_BLOCK
        q_c = lax.dynamic_slice_in_dim(q, q0, Q_CHUNK, axis=2)
        gate = jnp.einsum('bhqd,bhnd->bhqn', q_c, k_mean)
        gate = jnp.where(blk_ids < own, gate, -jnp.inf)
        _, sel = lax.top_k(gate, K)
        valid = sel < own
        k_sel = kb[bi, hi, sel]
        v_sel = vb[bi, hi, sel]
        s_sel = jnp.einsum('bhqd,bhqksd->bhqks', q_c, k_sel)
        s_sel = jnp.where(valid[..., None], s_sel, -jnp.inf).reshape(B, H, Q_CHUNK, K * MOBA_BLOCK)
        k_own = lax.dynamic_index_in_dim(kb, own, axis=2, keepdims=False)
        v_own = lax.dynamic_index_in_dim(vb, own, axis=2, keepdims=False)
        s_own = jnp.einsum('bhqd,bhsd->bhqs', q_c, k_own)
        causal = (own * MOBA_BLOCK + key_off)[None, :] <= (q0 + q_off)[:, None]
        s_own = jnp.where(causal, s_own, -jnp.inf)
        p = jax.nn.softmax(jnp.concatenate([s_sel, s_own], axis=-1), axis=-1)
        p_sel = p[..., :K * MOBA_BLOCK].reshape(B, H, Q_CHUNK, K, MOBA_BLOCK)
        p_own = p[..., K * MOBA_BLOCK:]
        return (jnp.einsum('bhqks,bhqksd->bhqd', p_sel, v_sel)
                + jnp.einsum('bhqs,bhsd->bhqd', p_own, v_own))

    out = lax.map(attend_chunk, jnp.arange(T // Q_CHUNK))
    out = jnp.transpose(out, (1, 0, 3, 2, 4)).reshape(B, T, C)
    return out.astype(x.dtype) @ w_o

def first_inputs(seed: int = 0) -> dict:
    key = jax.random.key(seed)
    ks = iter(jax.random.split(key, 32))
    C, H, N, F = D_MODEL, N_HEADS, HEAD_DIM, D_FF
    nrm = lambda shape, s: jax.random.normal(next(ks), shape, jnp.float32) * s
    return {
        'x': nrm((BATCH, SEQ, C), 1.0),
        'rwkv_mu': jax.random.uniform(next(ks), (N_RWKV, 6, C), jnp.float32),
        'rwkv_w_rkv': nrm((N_RWKV, 3, C, C), C ** -0.5),
        'rwkv_w0': jax.random.uniform(next(ks), (N_RWKV, C), jnp.float32, -5.0, 0.5),
        'rwkv_w1': nrm((N_RWKV, C, DECAY_LORA), C ** -0.5),
        'rwkv_w2': nrm((N_RWKV, DECAY_LORA, C), 0.5 * DECAY_LORA ** -0.5),
        'rwkv_a0': nrm((N_RWKV, C), 0.1),
        'rwkv_a1': nrm((N_RWKV, C, AAA_LORA), C ** -0.5),
        'rwkv_a2': nrm((N_RWKV, AAA_LORA, C), 0.5 * AAA_LORA ** -0.5),
        'rwkv_g1': nrm((N_RWKV, C, GATE_LORA), C ** -0.5),
        'rwkv_g2': nrm((N_RWKV, GATE_LORA, C), GATE_LORA ** -0.5),
        'rwkv_k_k': 0.85 + nrm((N_RWKV, C), 0.05),
        'rwkv_k_a': 1.0 + nrm((N_RWKV, C), 0.05),
        'rwkv_r_k': nrm((N_RWKV, H, N), 0.1),
        'rwkv_gn_g': 1.0 + nrm((N_RWKV, C), 0.05),
        'rwkv_gn_b': nrm((N_RWKV, C), 0.02),
        'rwkv_w_o': nrm((N_RWKV, C, C), BETA * C ** -0.5),
        'moba_w_qkv': nrm((N_MOBA, C, 3 * C), C ** -0.5),
        'moba_w_o': nrm((N_MOBA, C, C), BETA * C ** -0.5),
        'ffn_w_in': nrm((DEPTH, C, 2 * F), C ** -0.5),
        'ffn_w_down': nrm((DEPTH, F, C), BETA * F ** -0.5),
        'ln_mix_g': 1.0 + nrm((DEPTH, C), 0.05),
        'ln_mix_b': nrm((DEPTH, C), 0.02),
        'ln_ffn_g': 1.0 + nrm((DEPTH, C), 0.05),
        'ln_ffn_b': nrm((DEPTH, C), 0.02),
    }

def first_block(x, rwkv_mu, rwkv_w_rkv, rwkv_w0, rwkv_w1, rwkv_w2, rwkv_a0, rwkv_a1, rwkv_a2,
              rwkv_g1, rwkv_g2, rwkv_k_k, rwkv_k_a, rwkv_r_k, rwkv_gn_g, rwkv_gn_b, rwkv_w_o,
              moba_w_qkv, moba_w_o, ffn_w_in, ffn_w_down, ln_mix_g, ln_mix_b, ln_ffn_g, ln_ffn_b):
    for i in range(DEPTH):
        j = i // N_MIXERS
        if i % N_MIXERS == 0:
            h = rwkv7_time_mix(x, rwkv_mu[j], rwkv_w_rkv[j], rwkv_w0[j], rwkv_w1[j], rwkv_w2[j],
                               rwkv_a0[j], rwkv_a1[j], rwkv_a2[j], rwkv_g1[j], rwkv_g2[j],
                               rwkv_k_k[j], rwkv_k_a[j], rwkv_r_k[j], rwkv_gn_g[j], rwkv_gn_b[j],
                               rwkv_w_o[j])
        else:
            h = moba_attention(x, moba_w_qkv[j], moba_w_o[j])
        x = layer_norm(ALPHA * x + h, ln_mix_g[i], ln_mix_b[i])
        x = layer_norm(ALPHA * x + swiglu_ffn(x, ffn_w_in[i], ffn_w_down[i]), ln_ffn_g[i], ln_ffn_b[i])
    return x


DEPTH_2 = 1

N_MEM = 256
D_MIX = D_MODEL
ML_HEADS = 4
ML_DH = D_MIX // 2 // ML_HEADS
ML_W = ML_HEADS * ML_DH
ML_CHUNK = 64
CONV_W = 4
FX_HEADS = 8
FX_DH = (D_MIX - ML_W) // FX_HEADS
FX_W = FX_HEADS * FX_DH
Q_BLOCK = 128
X_HEADS = 4
X_DH = D_MODEL // X_HEADS
D_FF_2 = 4 * D_MODEL
EPS = 1e-6
IN_SIZES = (2 * ML_W, ML_W, ML_W, ML_HEADS, ML_HEADS, FX_W, FX_W, FX_W, FX_HEADS)
IN_COLS = 4 * ML_W + 2 * ML_HEADS + 3 * FX_W + FX_HEADS


def rmsnorm(x, g):
    xf = x.astype(jnp.float32)
    y = xf * lax.rsqrt(jnp.mean(xf * xf, axis=-1, keepdims=True) + EPS)
    return (y * g.astype(jnp.float32)).astype(x.dtype)

def causal_conv(u, w, b):
    S = u.shape[1]
    up = jnp.pad(u, ((0, 0), (CONV_W - 1, 0), (0, 0)))
    out = b
    for j in range(CONV_W):
        out = out + up[:, j:j + S] * w[j]
    return out

def mlstm_chunkwise(q, k, v, ig, lf):
    B, S, H, dh = q.shape
    nc = S // ML_CHUNK
    k = k * (dh ** -0.5)

    def to_chunks(t):
        t = t.reshape((B, nc, ML_CHUNK) + t.shape[2:])
        return jnp.moveaxis(t, (1, 3), (0, 2))

    causal = jnp.tril(jnp.ones((ML_CHUNK, ML_CHUNK), dtype=bool))

    def body(carry, xs):
        C, n, m = carry
        qc, kc, vc, ic, fc = xs
        b = jnp.cumsum(fc, axis=-1)
        g = b[..., -1]
        dmat = b[..., :, None] - b[..., None, :] + ic[..., None, :]
        dmat = jnp.where(causal, dmat, -jnp.inf)
        m_inter = b + m[..., None]
        m_t = jnp.maximum(m_inter, jnp.max(dmat, axis=-1))
        scores = jnp.einsum('bhtd,bhsd->bhts', qc, kc) * jnp.exp(dmat - m_t[..., None])
        inter = jnp.exp(m_inter - m_t)
        num = (jnp.einsum('bhts,bhsd->bhtd', scores, vc)
               + inter[..., None] * jnp.einsum('bhed,bhtd->bhte', C, qc))
        den = scores.sum(-1) + inter * jnp.einsum('bhd,bhtd->bht', n, qc)
        h = num / jnp.maximum(jnp.abs(den), jnp.exp(-m_t))[..., None]
        a = g[..., None] - b + ic
        m_new = jnp.maximum(g + m, jnp.max(a, axis=-1))
        decay = jnp.exp(g + m - m_new)
        wa = jnp.exp(a - m_new[..., None])
        C_new = decay[..., None, None] * C + jnp.einsum('bhs,bhse,bhsd->bhed', wa, vc, kc)
        n_new = decay[..., None] * n + jnp.einsum('bhs,bhsd->bhd', wa, kc)
        return (C_new, n_new, m_new), h

    init = (jnp.zeros((B, H, dh, dh), jnp.float32), jnp.zeros((B, H, dh), jnp.float32),
            jnp.zeros((B, H), jnp.float32))
    _, hs = lax.scan(body, init, (to_chunks(q), to_chunks(k), to_chunks(v), to_chunks(ig), to_chunks(lf)))
    hs = jnp.moveaxis(hs, (0, 2), (1, 3))
    return hs.reshape(B, S, H, dh)

def forgetting_attention(q, k, v, lf):
    B, S, H, dh = q.shape
    nb = S // Q_BLOCK
    cT = jnp.cumsum(lf, axis=1).transpose(0, 2, 1)
    qb = q.reshape(B, nb, Q_BLOCK, H, dh).transpose(1, 0, 2, 3, 4)
    cb = cT.reshape(B, H, nb, Q_BLOCK).transpose(2, 0, 1, 3)
    kpos = jnp.arange(S)
    scale = dh ** -0.5

    def block(args):
        qi, ci, blk = args
        qpos = blk * Q_BLOCK + jnp.arange(Q_BLOCK)
        s = jnp.einsum('bqhd,bkhd->bhqk', qi, k, preferred_element_type=jnp.float32) * scale
        s = s + (ci[..., :, None] - cT[..., None, :])
        s = jnp.where(qpos[:, None] >= kpos[None, :], s, -jnp.inf)
        p = jax.nn.softmax(s, axis=-1)
        return jnp.einsum('bhqk,bkhd->bqhd', p.astype(v.dtype), v)

    out = lax.map(block, (qb, cb, jnp.arange(nb)))
    return out.transpose(1, 0, 2, 3, 4).reshape(B, S, H, dh)

def cross_attention(h, memn, w_q, w_kv, w_o):
    B, S, D = h.shape
    M = memn.shape[1]
    q = (h @ w_q).reshape(B, S, X_HEADS, X_DH)
    k, v = jnp.split(memn @ w_kv, 2, axis=-1)
    k = k.reshape(B, M, X_HEADS, X_DH)
    v = v.reshape(B, M, X_HEADS, X_DH)
    s = jnp.einsum('bqhd,bmhd->bhqm', q, k, preferred_element_type=jnp.float32) * (X_DH ** -0.5)
    p = jax.nn.softmax(s, axis=-1)
    o = jnp.einsum('bhqm,bmhd->bqhd', p.astype(v.dtype), v).reshape(B, S, D)
    return o @ w_o

def second_inputs(seed: int = 0) -> dict:
    key = jax.random.key(seed)
    ks = jax.random.split(key, 24)
    f32 = jnp.float32

    def w(k, shape, fan_in):
        return jax.random.normal(k, shape, f32) * (fan_in ** -0.5)

    def gain(k, shape):
        return 1.0 + 0.1 * jax.random.normal(k, shape, f32)

    def small(k, shape):
        return 0.01 * jax.random.normal(k, shape, f32)

    return {
        "x": jax.random.normal(ks[0], (BATCH, SEQ, D_MODEL), f32),
        "mem": jax.random.normal(ks[1], (BATCH, N_MEM, D_MODEL), f32),
        "ln1": gain(ks[2], (DEPTH_2, D_MODEL)),
        "w_in": w(ks[3], (DEPTH_2, D_MODEL, IN_COLS), D_MODEL),
        "ml_conv_w": w(ks[4], (DEPTH_2, CONV_W, 2 * ML_W), CONV_W),
        "ml_conv_b": small(ks[5], (DEPTH_2, 2 * ML_W)),
        "ml_b_i": small(ks[6], (DEPTH_2, ML_HEADS)),
        "ml_b_f": 3.0 + 0.1 * jax.random.normal(ks[7], (DEPTH_2, ML_HEADS), f32),
        "ml_norm": gain(ks[8], (DEPTH_2, ML_W)),
        "fx_b_f": 3.0 + 0.1 * jax.random.normal(ks[9], (DEPTH_2, FX_HEADS), f32),
        "w_out": w(ks[10], (DEPTH_2, D_MIX, D_MODEL), D_MIX),
        "ln_x": gain(ks[11], (DEPTH_2, D_MODEL)),
        "ln_mem": gain(ks[12], (DEPTH_2, D_MODEL)),
        "w_xq": w(ks[13], (DEPTH_2, D_MODEL, D_MODEL), D_MODEL),
        "w_xkv": w(ks[14], (DEPTH_2, D_MODEL, 2 * D_MODEL), D_MODEL),
        "w_xo": w(ks[15], (DEPTH_2, D_MODEL, D_MODEL), D_MODEL),
        "ln2": gain(ks[16], (DEPTH_2, D_MODEL)),
        "w_ff1": w(ks[17], (DEPTH_2, D_MODEL, D_FF_2), D_MODEL),
        "w_ff2": w(ks[18], (DEPTH_2, D_FF_2, D_MODEL), D_FF_2),
        "ln_f": gain(ks[19], (D_MODEL,)),
    }

def second_block(x, mem, ln1, w_in, ml_conv_w, ml_conv_b, ml_b_i, ml_b_f, ml_norm, fx_b_f, w_out,
              ln_x, ln_mem, w_xq, w_xkv, w_xo, ln2, w_ff1, w_ff2, ln_f):
    B, S, _ = x.shape
    splits = [int(v) for v in np.cumsum(IN_SIZES)[:-1]]
    for l in range(DEPTH_2):
        h = rmsnorm(x, ln1[l])
        z = h @ w_in[l]
        ml_qk, ml_v, ml_o, ml_i, ml_f, fx_q, fx_k, fx_v, fx_f = jnp.split(z, splits, axis=-1)

        ml_qk = jax.nn.silu(causal_conv(ml_qk, ml_conv_w[l], ml_conv_b[l]))
        mq, mk = jnp.split(ml_qk.astype(jnp.float32), 2, axis=-1)
        mq = mq.reshape(B, S, ML_HEADS, ML_DH)
        mk = mk.reshape(B, S, ML_HEADS, ML_DH)
        mv = ml_v.astype(jnp.float32).reshape(B, S, ML_HEADS, ML_DH)
        ig = ml_i.astype(jnp.float32) + ml_b_i[l].astype(jnp.float32)
        lf = jax.nn.log_sigmoid(ml_f.astype(jnp.float32) + ml_b_f[l].astype(jnp.float32))
        mh = mlstm_chunkwise(mq, mk, mv, ig, lf)
        mh = mh * lax.rsqrt(jnp.mean(mh * mh, axis=-1, keepdims=True) + EPS)
        mh = mh * ml_norm[l].astype(jnp.float32).reshape(ML_HEADS, ML_DH)
        ml_out = (mh.reshape(B, S, ML_W) * jax.nn.sigmoid(ml_o.astype(jnp.float32))).astype(x.dtype)

        fq = fx_q.reshape(B, S, FX_HEADS, FX_DH)
        fk = fx_k.reshape(B, S, FX_HEADS, FX_DH)
        fv = fx_v.reshape(B, S, FX_HEADS, FX_DH)
        flf = jax.nn.log_sigmoid(fx_f.astype(jnp.float32) + fx_b_f[l].astype(jnp.float32))
        fx_out = forgetting_attention(fq, fk, fv, flf).reshape(B, S, FX_W)

        x = x + jnp.concatenate([ml_out, fx_out], axis=-1) @ w_out[l]

        x = x + cross_attention(rmsnorm(x, ln_x[l]), rmsnorm(mem, ln_mem[l]), w_xq[l], w_xkv[l], w_xo[l])

        u = jax.nn.relu(rmsnorm(x, ln2[l]) @ w_ff1[l])
        x = x + (u * u) @ w_ff2[l]
    return rmsnorm(x, ln_f)


def setup_inputs(seed=0):
    out = dict(first_inputs(seed))
    for name, value in second_inputs(seed + 1).items():
        if name != "x":
            out[name + "_2"] = value
    return out


def reference(
    x, rwkv_mu, rwkv_w_rkv, rwkv_w0, rwkv_w1, rwkv_w2, rwkv_a0, rwkv_a1, rwkv_a2, rwkv_g1,
    rwkv_g2, rwkv_k_k, rwkv_k_a, rwkv_r_k, rwkv_gn_g, rwkv_gn_b, rwkv_w_o, moba_w_qkv, moba_w_o,
    ffn_w_in, ffn_w_down, ln_mix_g, ln_mix_b, ln_ffn_g, ln_ffn_b, mem_2, ln1_2, w_in_2,
    ml_conv_w_2, ml_conv_b_2, ml_b_i_2, ml_b_f_2, ml_norm_2, fx_b_f_2, w_out_2, ln_x_2,
    ln_mem_2, w_xq_2, w_xkv_2, w_xo_2, ln2_2, w_ff1_2, w_ff2_2, ln_f_2,
):
    x = first_block(
        x, rwkv_mu, rwkv_w_rkv, rwkv_w0, rwkv_w1, rwkv_w2, rwkv_a0, rwkv_a1, rwkv_a2, rwkv_g1,
        rwkv_g2, rwkv_k_k, rwkv_k_a, rwkv_r_k, rwkv_gn_g, rwkv_gn_b, rwkv_w_o, moba_w_qkv,
        moba_w_o, ffn_w_in, ffn_w_down, ln_mix_g, ln_mix_b, ln_ffn_g, ln_ffn_b,
    )
    return second_block(
        x, mem_2, ln1_2, w_in_2, ml_conv_w_2, ml_conv_b_2, ml_b_i_2, ml_b_f_2, ml_norm_2,
        fx_b_f_2, w_out_2, ln_x_2, ln_mem_2, w_xq_2, w_xkv_2, w_xo_2, ln2_2, w_ff1_2, w_ff2_2,
        ln_f_2,
    )


_drawn_inputs = setup_inputs


def setup_inputs(seed=0):
    import zlib

    import numpy as np

    out = dict(_drawn_inputs(seed))
    spreads = {}
    factors = {'rwkv_w1': 7.351,
     'rwkv_w2': 7.217,
     'rwkv_a0': 5.047,
     'rwkv_k_k': 7.266,
     'rwkv_k_a': 4.284,
     'rwkv_gn_g': 4.895,
     'rwkv_gn_b': 7.794,
     'ml_conv_b_2': 8.0,
     'ml_b_i_2': 64.0,
     'ml_b_f_2': 31.176,
     'fx_b_f_2': 26.648,
     'ln_x_2': 5.053,
     'ln_mem_2': 3.577}
    for name, (base, spread) in spreads.items():
        noise = np.random.default_rng([zlib.crc32(name.encode()), seed]).standard_normal(out[name].shape)
        drawn = base * np.exp(spread * noise) if base else spread * noise
        out[name] = __import__('jax').numpy.asarray(drawn.astype(out[name].dtype))
    for name, factor in factors.items():
        out[name] = (out[name] * factor).astype(out[name].dtype)
    return out
```

```python
from contextlib import ExitStack

import numpy as np

import concourse.bass as bass
from concourse import mybir

F32 = mybir.dt.float32
F32R = mybir.dt.float32r
ALU = mybir.AluOpType
ACT = mybir.ActivationFunctionType
AX_X = mybir.AxisListType.X

P = 128
T = 256
TT = T // P
C = 1024
KT = C // P
HD = 64
NEG = -1.0e30
SLAB = 2048
RAW = 3
WS = 3
ALPHA = (2 * 2) ** 0.25
LN_EPS = 1e-5
GN_EPS = HD * 1e-5
RMS_EPS = 1e-6
DECAY = float(np.exp(-0.5))
LORA = 64
GLORA = 160
D_FF = 2816
D_FF2 = 4096
IN_COLS = 3600
NL = 7


def constants():
    i = np.arange(P)[:, None]
    j = np.arange(P)[None, :]
    c = {}
    c["ident"] = i == j
    c["headones"] = i // HD == j // HD
    c["strict"] = i < j
    c["incl"] = i <= j
    for n in range(NL):
        s = 1 << n
        c[f"level{n}"] = (i // (2 * s) == j // (2 * s)) & (i // s < j // s)
    c["level0T"] = (i // 2 == j // 2) & (i > j)
    c["reset"] = np.broadcast_to(np.arange(2 * T)[None, :] % P != 0, (P, 2 * T))
    c["headsel"] = i // HD == np.arange(2)[None, :]
    inv = np.float32(10000.0) ** (-np.arange(0, HD, 2, dtype=np.float32) / np.float32(HD))
    ang = np.arange(T, dtype=np.float32)[:, None] * inv[None, :]
    f = np.arange(P) % (HD // 2)
    c["cos"] = np.cos(ang).T[f]
    c["sin"] = np.sin(ang).T[f]
    rot = np.zeros((P, P), np.float32)
    for m in range(P):
        if m % HD < HD // 2:
            rot[m + HD // 2, m] = -1.0
        else:
            rot[m - HD // 2, m] = 1.0
    c["rot"] = rot
    low = np.where(j <= i, 0.0, NEG)
    c["causal"] = np.concatenate([low, np.zeros((P, P)), low], axis=1)
    c["nomask"] = np.zeros((P, 2 * T))
    c["onesrow"] = np.ones((P, P))
    c["gatesel"] = np.concatenate([np.broadcast_to(i == h, (P, P)) for h in range(12)], axis=1)
    return {k: np.ascontiguousarray(v, dtype=np.float32) for k, v in c.items()}




def weight_plan():
    plan, start = [], {}

    def section(name, slabs):
        start[name] = len(plan)
        plan.extend(slabs)

    def wide(src, layer, c0, n):
        return [("wide", src, layer, 0, c0 + 256 * i) for i in range(n)]

    def tall(src, layer, n):
        return [("tall", src, layer, 2 * i, 0) for i in range(n)]

    section("rkv", [s for n in range(3) for s in wide("rwkv_w_rkv", n, 0, 4)])
    section("rwkv_o", tall("rwkv_w_o", 0, 4))
    for layer in range(2):
        slabs = []
        for j in range(D_FF // 256 + 1):
            if j < D_FF // 256:
                slabs += wide("ffn_w_in", layer, 256 * j, 1) + wide("ffn_w_in", layer, D_FF + 256 * j, 1)
            if j:
                slabs.append(("tall", "ffn_w_down", layer, 2 * (j - 1), 0))
        if layer == 1:
            section("qkv", [wide("moba_w_qkv", 0, n * C + 256 * g, 1)[0] for g in range(4) for n in range(3)])
            section("moba_o", tall("moba_w_o", 0, 4))
        section(f"ffn{layer}", slabs)
    section("ml_qk", wide("w_in_2", 0, 0, 4))
    section("ml_v", wide("w_in_2", 0, 1024, 2))
    section("ml_o", wide("w_in_2", 0, 1536, 2))
    section("fx_qk", wide("w_in_2", 0, 2056, 4))
    section("fx_v", wide("w_in_2", 0, 3080, 2))
    section("x_k", wide("w_xkv_2", 0, 0, 4))
    section("x_v", wide("w_xkv_2", 0, C, 4))
    section("mix_o", tall("w_out_2", 0, 4))
    section("x_q", wide("w_xq_2", 0, 0, 4))
    section("x_o", tall("w_xo_2", 0, 4))
    slabs = []
    for j in range(D_FF2 // 256 + 1):
        if j < D_FF2 // 256:
            slabs += wide("w_ff1_2", 0, 256 * j, 1)
        if j:
            slabs.append(("tall", "w_ff2_2", 0, 2 * (j - 1), 0))
    section("ff2", slabs)
    return plan, start


PARAMS = [("rwkv_mu", 6 * KT), ("rwkv_w0", KT), ("rwkv_a0", KT), ("rwkv_k_k", KT), ("rwkv_k_a", KT),
          ("rwkv_r_k", KT), ("ln_mix_g", 2 * KT), ("ln_mix_b", 2 * KT), ("ln_ffn_g", 2 * KT), ("ln_ffn_b", 2 * KT),
          ("ln1_2", KT), ("ln_x_2", KT), ("ln_mem_2", KT), ("ln2_2", KT), ("ml_conv_w_2", 4 * KT),
          ("ml_conv_b_2", KT), ("ml_norm_2", 4)]
PCOL = {}
for _name, _n in PARAMS:
    PCOL[_name] = sum(n for _, n in PARAMS[:len(PCOL)])
N_PARAMS = sum(n for _, n in PARAMS)
CONST_SETS = {
    "base": ["ident", "causal"],
    "rwkv": ["headones", "strict", "incl"] + [f"level{n}" for n in range(NL)] + ["level0T", "reset", "headsel"],
    "rope": ["cos", "sin", "rot"],
    "gates": ["gatesel"],
}


def const_columns(which):
    at, out = 0, {}
    table = constants()
    for name in CONST_SETS[which]:
        out[name] = (at, table[name].shape[1])
        at += table[name].shape[1]
    return out, at


def over(ap, n):
    return ap.unsqueeze(1).broadcast_to([ap.shape[0], n, ap.shape[1]])


def along(ap, n):
    return ap.unsqueeze(2).broadcast_to([ap.shape[0], ap.shape[1], n])


def build(nc, d, out, upto=99):
    plan, first = weight_plan()
    n_slabs = len(plan)

    with ExitStack() as ctx:
        def sb(name, shape, dt=F32, where=None):
            return (where or ctx).enter_context(nc.sbuf_tensor(name, shape, dt))

        def sem(name):
            return ctx.enter_context(nc.semaphore(name))

        ps = ctx.enter_context(nc.psum_tensor("ps", [P, 8, 512], F32))

        w_raw = sb("w_raw", [P, RAW, SLAB])
        w_hi = sb("w_hi", [P, WS, SLAB], F32R)
        w_lo = sb("w_lo", [P, WS, SLAB], F32R)
        x_tm = sb("x_tm", [P, TT, C])
        mix_hi = sb("mix_hi", [P, KT, T], F32R)
        mix_lo = sb("mix_lo", [P, KT, T], F32R)
        cols_b, n_b = const_columns("base")
        base_c = sb("base_c", [P, n_b])
        par = sb("par", [P, N_PARAMS])
        stats = sb("stats", [P, TT, 2, 6])
        mv = sb("mv", [P, TT, 2])
        sd = sb("sd", [P, TT])
        rstd = sb("rstd", [P, TT])
        shift = sb("shift", [P, TT])
        eps_c = sb("eps_c", [P, 3])
        mx = sb("mx", [P, 8])
        sm = sb("sm", [P, 8])
        rs = sb("rs", [P, 8])
        ident = base_c[:, 0:P]
        causal = base_c[:, P:4 * P]

        with ExitStack() as a_rw:
            ar = sb("ar", [P, KT, TT, 2, P], where=a_rw)
            k_fm, r_fm = (ar[:, :, :, n, :].rearrange("p a t c -> p (a t) c") for n in range(2))
            rk_sel = sb("rk_sel", [P, KT, 2], where=a_rw)
            v_tm = sb("v_tm", [P, TT, C], where=a_rw)
            cols_r, n_r = const_columns("rwkv")
            rw_c = sb("rw_c", [P, n_r], where=a_rw)
            tanh_w = sb("tanh_w", [LORA, T], where=a_rw)
            lora_a = sb("lora_a", [LORA, T], where=a_rw)
            sig_g = sb("sig_g", [P, T], where=a_rw)
            sig_g2 = sb("sig_g2", [GLORA - P, T], where=a_rw)
            with ExitStack() as a:
                rx_hi = sb("rx_hi", [P, KT, T], F32R, a)
                rx_lo = sb("rx_lo", [P, KT, T], F32R, a)
                xt = sb("xt", [P, KT, T], where=a)
                xx = sb("xx", [P, KT, T], where=a)
                mixed = sb("mixed", [P, 2, KT, T], where=a)
                w1 = sb("w1", [P, KT, LORA], where=a)
                a1 = sb("a1", [P, KT, LORA], where=a)
                g1 = sb("g1", [P, KT, GLORA], where=a)
            with ExitStack() as a:
                w_m, nt_m, dt_m, d_a = (sb(n, [P, TT, 4, P], where=a) for n in ("w_m", "nt_m", "dt_m", "d_a"))
                w2 = sb("w2", [LORA, 256], where=a)
                a2 = sb("a2", [LORA, 256], where=a)
                g2 = sb("g2", [P, 256], where=a)
                g2b = sb("g2b", [GLORA - P, 256], where=a)
                gn_g = sb("gn_g", [P, 256], where=a)
                gn_b = sb("gn_b", [P, 256], where=a)
                sw, av, kk, cum, cprev, e_pos, e_neg, kmod, norm_k, b_t, k_t = (
                    sb(n, [P, 4, P], where=a) for n in
                    ("sw", "av", "kk", "cum", "cprev", "e_pos", "e_neg", "kmod", "norm_k", "b_t", "k_t"))
                bk_tm = sb("bk_tm", [P, 2, 2, 2, P], where=a)
                d_b, rb_a, rb_b, ak_a, rk_a = (sb(n, [P, TT, 4, P], where=a) for n in
                                               ("d_b", "rb_a", "rb_b", "ak_a", "rk_a"))
                u_m = sb("u_m", [P, 256], where=a)
                sa_m = sb("sa_m", [P, TT, 256], where=a)
                state = sb("state", [P, 2, HD], where=a)
                smid = sb("smid", [P, 4], where=a)
                sdec = sb("sdec", [P, 4, 2], where=a)
                bon = sb("bon", [P, 4, TT * 4], where=a)
                ymean, yvar, ysd, yrs = (sb(n, [P, TT * 4], where=a) for n in ("ymean", "yvar", "ysd", "yrs"))
            g_sb, y_sq, y_fm, y_sb = (w_raw[:, RAW - 1, 512 * n:512 * n + 512].rearrange("p (a b) -> p a b", a=m)
                                for n, m in ((0, TT), (1, TT * 4), (2, 2), (3, TT * 4)))
            four = lambda n: x_tm[:, n, :].rearrange("p (t h c) -> p t h c", t=TT, h=4)
            d_m, rb_m, ak_m, rk_m = (d_a, d_b), (rb_a, rb_b), (four(0), ak_a), (four(1), rk_a)

        def rc(name, lo=0, n=None):
            at, m = cols_r[name]
            return rw_c[:, at + lo:at + (n or m)]

        a_m = ctx.enter_context(ExitStack())
        x_hi = sb("x_hi", [P, KT, T], F32R, a_m)
        x_lo = sb("x_lo", [P, KT, T], F32R, a_m)
        xn = sb("xn", [P, TT, C], where=a_m)
        x_fm = sb("x_fm", [P, KT, T], where=a_m)
        gain = sb("gain", [P, 2, C], where=a_m)
        xk_fm = sb("xk_fm", [P, KT, T + 3], where=a_m)
        conv_in = xk_fm
        gsel = sb("gsel", [P, 12 * P], where=a_m)
        gate_w = sb("gate_w", [P, KT, 16], where=a_m)
        gate_bf = sb("gate_bf", [12, 1], where=a_m)
        gate_bi = sb("gate_bi", [4, 1], where=a_m)
        with ExitStack() as a:
            hid = sb("hid", [P, 2, 512], where=a)
            act_f = sb("act_f", [P, 2, 512], where=a)
            hid_hi = sb("hid_hi", [P, 3, 512], F32R, a)
            hid_lo = sb("hid_lo", [P, 3, 512], F32R, a)

        with ExitStack() as a:
            rope_c = sb("rope_c", [P, 2 * T + P], where=a)
            ma_q, ma_k, ma_q2, ma_k2, ma_v, rt = (sb(n, [P, 2, T], where=a) for n in
                                                  ("ma_q", "ma_k", "ma_q2", "ma_k2", "ma_v", "rt"))
            ma_vv = sb("ma_vv", [P, 2, TT, 256], where=a)
            ma_s = sb("ma_s", [P, 4, 3 * P], where=a)
            ma_p = sb("ma_p", [P, 4, 3 * P], where=a)
            ma_o = sb("ma_o", [P, 2, T], where=a)
        with ExitStack() as a:
            conv_out = sb("conv_out", [P, KT, T], where=a)
            ml_v = sb("ml_v", [P, TT, 512], where=a)
            ml_o = sb("ml_o", [P, TT, 512], where=a)
            fx_q = sb("fx_q", [P, 4, T], where=a)
            fx_k = sb("fx_k", [P, 4, T], where=a)
            fx_v = sb("fx_v", [P, TT, 512], where=a)
            se_s = sb("se_s", [P, 4, 3 * P], where=a)
            se_p = sb("se_p", [P, 4, 3 * P], where=a)
            bias = sb("bias", [P, 4, 3 * P], where=a)
            zf, za, ones_t, gi = (sb(n, [12, T], where=a) for n in ("zf", "za", "ones_t", "gi"))
            gst = sb("gst", [HD, T], where=a)
            tc = sb("tc", [P, TT, HD], where=a)
            em = sb("em", [P, 8], where=a)
            den = sb("den", [P, 8], where=a)
            ml_rs = sb("ml_rs", [P, 8], where=a)
            se_o = sb("se_o", [P, 2, T], where=a)
            ml_y = x_fm[:, 0:4, :].rearrange("p a (b c) -> p (a b) c", c=P)
            ml_sq = x_fm[:, 4:8, :].rearrange("p a (b c) -> p (a b) c", c=P)
        with ExitStack() as a:
            xq_fm = sb("xq_fm", [P, KT, T], where=a)
            cr_s = sb("cr_s", [P, 4, 512], where=a)
            cr_p = sb("cr_p", [P, 4, 512], where=a)
            cr_o = sb("cr_o", [P, 2, T], where=a)
            zero_m = sb("zero_m", [P, T], where=a)

        raw_loaded = [sem(f"raw_loaded{i}") for i in range(RAW)]
        hi_done, lo_dve, lo_pool, slab_done = sem("hi_done"), sem("lo_dve"), sem("lo_pool"), sem("slab_done")
        dve_step, act_step, pool_step = sem("dve_step"), sem("act_step"), sem("pool_step")
        consts_loaded, par_loaded, x_loaded, xt_loaded = (
            sem("consts_loaded"), sem("par_loaded"), sem("x_loaded"), sem("xt_loaded"))
        lora1_loaded, lora2_loaded, lora2_used = sem("lora1_loaded"), sem("lora2_loaded"), sem("lora2_used")
        out_stored = sem("out_stored")
        eps_set = sem("eps_set")

        def lo_engine(i):
            return ("dve", i // 2 + 1) if i % 2 == 0 else ("pool", i // 2 + 1)

        def wait_slab(pe, i):
            who, n = lo_engine(i)
            pe.wait_ge(lo_dve if who == "dve" else lo_pool, n)

        def wview(w, i, kind):
            v = w[:, i % WS, :]
            return v.rearrange("p (k n) -> p k n", k=8 if kind == "wide" else 2)

        pe_step = sem("pe_step")
        HEADS = [0, 2, 1, 3]
        mixed_ready = sem("mixed_ready")
        mix_hi_done, mix_lo_done = sem("mix_hi_done"), sem("mix_lo_done")
        lora1_mm, lora1_out = sem("lora1_mm"), sem("lora1_out")
        proj_taken = sem("proj_taken")
        aux_ready, aux_taken = sem("aux_ready"), sem("aux_taken")
        kk2_ready, rkr_ready, cum_ready, exp_done, prep_ready = (
            sem(n) for n in ("kk2_ready", "rkr_ready", "cum_ready", "exp_done", "prep_ready"))
        inv_ready = [sem(f"inv_ready{t}") for t in range(TT)]
        inv_taken = [sem(f"inv_taken{t}") for t in range(TT)]
        nt_taken = [sem(f"nt_taken{t}") for t in range(TT)]
        yvar_ready, ysd_ready, y_ready, rwkv_lo_done = (
            sem(n) for n in ("yvar_ready", "ysd_ready", "y_ready", "rwkv_lo_done"))
        bonus_ready = sem("bonus_ready")
        gate_lora_loaded, cprev_ready, kmod_ready, kk_ready, a_ready, ymean_ready, ysq_ready, yrs_ready = (
            sem(n) for n in ("gate_lora_loaded", "cprev_ready", "kmod_ready", "kk_ready", "a_ready", "ymean_ready",
                             "ysq_ready", "yrs_ready"))
        (A_W, A_A, A_KK, A_BON, A_BK, A_U0, A_SA0, A_ST, A_U1, A_SA1, A_Y, A_G, A_YT) = range(13)
        PREP = (A_W, A_A, A_KK, A_BON, A_BK)
        SLOTS = [(A_W,), (A_U0, A_A), (A_SA0, A_KK), (A_ST, A_YT), (A_U1,), (A_SA1,), (A_Y, A_BON), (), (A_BK, A_G), (), (),
                 ()]

        def slot_steps(g, slot):
            steps = [(g + 1 if k in PREP else g - 2 if k == A_YT else g - 1, k) for k in SLOTS[slot]]
            return [(n, k) for n, k in steps if 0 <= n < 4]

        def v_bank(i):
            return 2 + i % 2

        tail_steps = [(3, A_U0), (2, A_YT)] + [(3, k) for k in (A_SA0, A_ST, A_U1, A_SA1, A_Y, A_G, A_YT)]
        aux_order = [(0, k) for k in PREP] + [s for g in range(4) for i in range(12) for s in slot_steps(g, i)] + tail_steps
        aux_at = lambda g, k: aux_order.index((g, k))
        INV = 2 + 2 * (NL - 1)
        INVR = 3 + 2 * (NL - 1)
        MIXES = [("r", 0), ("k", 2), ("w", 1), ("a", 4), ("v", 3), ("g", 5)]
        stat_ready, sd_ready, xn_ready, tr_ready, xfm_ready, xhi_ready, xlo_ready, xtm_ready = (
            sem(n) for n in ("stat_ready", "sd_ready", "xn_ready", "tr_ready", "xfm_ready", "xhi_ready",
                             "xlo_ready", "xtm_ready"))
        gain_loaded = sem("gain_loaded")
        ffn_act, ffn_taken, hid_hi_done, hid_ready = (
            sem(n) for n in ("ffn_act", "ffn_taken", "hid_hi_done", "hid_ready"))
        p_taken = sem("p_taken")
        late_loaded = sem("late_loaded")
        rot_ready, rope_done, scores_ready, masked_ready, exp_ready, p_ready, pt_ready, pt_taken = (
            sem(n) for n in ("rot_ready", "rope_done", "scores_ready", "masked_ready", "exp_ready", "p_ready",
                             "pt_ready", "pt_taken"))
        o_ready, o_taken, o_lo_done = sem("o_ready"), sem("o_taken"), sem("o_lo_done")
        conv_ready, silu_ready, gate_mm, gate_abs, gate_ln, gate_rows, gate_tr, gate_cols, em_ready = (
            sem(n) for n in ("conv_ready", "silu_ready", "gate_mm", "gate_abs", "gate_ln", "gate_rows", "gate_tr",
                             "gate_cols", "em_ready"))
        row_ready, row_taken, w_ready, ml_var, ml_sd, ml_ready, ml_tr, ml_fm = (
            sem(n) for n in ("row_ready", "row_taken", "w_ready", "ml_var", "ml_sd", "ml_ready", "ml_tr", "ml_fm"))
        half_done = sem("half_done")
        rstd_ready, xn_act, xn_dve = sem("rstd_ready"), sem("xn_act"), sem("xn_dve")
        mem_loaded, final_ready = sem("mem_loaded"), sem("final_ready")

        NORMS = [
            ("mix0", ("ln_mix_g", 0), ("ln_mix_b", 0), 0, True), ("ffn0", ("ln_ffn_g", 0), ("ln_ffn_b", 0), 0, True),
            ("mix1", ("ln_mix_g", KT), ("ln_mix_b", KT), 0, True), ("ffn1", ("ln_ffn_g", KT), ("ln_ffn_b", KT), 0, True),
            ("ln1", ("ln1_2", 0), None, 2, False), ("mem", ("ln_mem_2", 0), None, 2, False),
            ("lnx", ("ln_x_2", 0), None, 2, False), ("ln2", ("ln2_2", 0), None, 2, False),
            ("final", None, None, 2, False)]
        FM_NORMS = [0, 1, 2, 4, 5, 6, 7]
        FFN = {"ffn0": (first["ffn0"], 11, 0), "ffn1": (first["ffn1"], 11, 11), "ff2": (first["ff2"], 16, 22)}

        def ffn_slabs(name, j):
            s0, n, _ = FFN[name]
            w = 1 if name == "ff2" else 2
            at = s0 + (w + 1) * j - (1 if j else 0)
            return (list(range(at, at + w)) if j < n else []), (at + (w if j < n else 0) if j else None)
        P_FIRST = {"qkv": 0, "ml_qk": 12, "ml_v": 16, "ml_o": 18, "fx_qk": 20, "fx_v": 24, "x_k": 26, "x_v": 30, "x_q": 34}
        def memory_slab(n):
            return first["x_k"] + n

        U_MOBA, U_ML, U_FX, U_X = 0, 16, 20, 28
        O_MOBA, O_FX, O_X = 0, 4, 8
        O_ML = 4
        CAUSAL = [(0, 0, P), (1, P, 3 * P)]
        FULL = [(0, 0, T), (1, T, 2 * T)]
        BLOCKS = {"causal": [(0, 0, 0), (P, 1, 0), (2 * P, 1, 1)],
                  "full": [(0, 0, 0), (T, 1, 0), (P, 0, 1), (T + P, 1, 1)]}

        def pcol(name, n=0):
            return par[:, PCOL[name] + n:PCOL[name] + n + 1]

        def chain(eng, s):
            count = [0]

            def link(ins):
                count[0] += 1
                ins.then_inc(s, 1)
                eng.wait_ge(s, count[0])
            return link


        block = ctx.enter_context(nc.Block())

        @block.sync
        def _(sp):
            def load_wa(g):
                for dst, src in ((w2, d["w2"]), (a2, d["a2"])):
                    sp.dma_start(dst[:, :], src[:, 256 * g:256 * g + 256]).then_inc(lora2_loaded, 16)

            def load_g(g):
                at = slice(256 * g, 256 * g + 256)
                for dst, src in ((g2, d["g2"][0:P]), (g2b, d["g2"][P:GLORA])):
                    sp.dma_start(dst[:, :], src[:, at]).then_inc(gate_lora_loaded, 16)
                for dst, src in ((gn_g, d["gn_g"]), (gn_b, d["gn_b"])):
                    sp.dma_start(dst[:, :], src[:, at].partition_broadcast(P)).then_inc(gate_lora_loaded, 16)

            sp.dma_start(xt[:, :, :], d["xT"]).then_inc(xt_loaded, 16)
            sp.dma_start(par[:, :], d["params"]).then_inc(par_loaded, 16)
            for i in range(n_slabs):
                if i >= RAW:
                    who, n = lo_engine(i - RAW)
                    if i == 17:
                        sp.wait_ge(rwkv_lo_done, 4)
                    sp.wait_ge(lo_dve if who == "dve" else lo_pool, n)
                sp.dma_start(w_raw[:, i % RAW, :], d["weights"][i]).then_inc(raw_loaded[i % RAW], 16)
                if i == 11:
                    sp.wait_ge(lora1_mm, 3)
                    sp.wait_ge(mix_lo_done, 3)
                    load_wa(0)
                    load_g(0)
                if i == 16:
                    for g in range(1, 4):
                        sp.wait_ge(aux_ready, aux_at(g - 1, A_A) + 1)
                        load_wa(g)
                    for g in range(1, 4):
                        sp.wait_ge(aux_ready, aux_at(g - 1, A_G) + 1)
                        sp.wait_ge(y_ready, g)
                        load_g(g)
                        if g == 3:
                            sp.wait_ge(aux_ready, aux_at(2, A_Y) + 1)
                            sp.dma_start(x_tm[:, :, :], d["x"]).then_inc(x_loaded, 16)
        @block.scalar
        def _(act):
            link = chain(act, act_step)

            def hi(i):
                if i >= n_slabs:
                    return
                act.wait_ge(raw_loaded[i % RAW], 16 * (i // RAW + 1))
                if i >= WS:
                    act.wait_ge(slab_done, i - WS + 1)
                nc.scalar.copy(w_hi[:, i % WS, :], w_raw[:, i % RAW, :]).then_inc(hi_done, 1)

            def take_proj(i):
                act.wait_ge(slab_done, i + 1)
                n, g = i // 4, i % 4
                if n == 2:
                    nc.scalar.copy(v_tm[:, :, 256 * g:256 * g + 256],
                                   ps[:, v_bank(i), :].rearrange("p (a b) -> p a b", a=2)).then_inc(proj_taken, 1)
                else:
                    dst = (r_fm, k_fm)[n]
                    nc.scalar.copy(dst[:, 4 * g:4 * g + 4, :],
                                   ps[:, i % 4, :].rearrange("p (a b) -> p a b", a=4)).then_inc(proj_taken, 1)
                hi(i + WS)

            def mix_high(q, dst, n):
                act.wait_ge(mixed_ready, q + 1)
                nc.scalar.copy(dst[:, :, :], mixed[:, q % 2, :, :]).then_inc(mix_hi_done, 1)

            hi(0)
            mix_high(0, rx_hi, 0)
            nc.scalar.dma_start(w1[:, :, :], d["w1"]).then_inc(lora1_loaded, 16)
            nc.scalar.dma_start(a1[:, :, :], d["a1"]).then_inc(lora1_loaded, 16)
            nc.scalar.dma_start(g1[:, :, :], d["g1"]).then_inc(lora1_loaded, 16)
            nc.scalar.dma_start(base_c[:, :], d["const_base"]).then_inc(consts_loaded, 16)
            nc.scalar.dma_start(rw_c[:, :], d["const_rwkv"]).then_inc(consts_loaded, 16)
            hi(1)
            hi(2)
            mix_high(1, mix_hi, 1)
            for i in range(4):
                take_proj(i)
            act.wait_ge(lora1_mm, 1)
            nc.scalar.activation(tanh_w[:, :], ps[0:LORA, 4, 0:T], ACT.Tanh).then_inc(lora1_out, 1)
            act.wait_ge(lora1_mm, 2)
            nc.scalar.copy(lora_a[:, :], ps[0:LORA, 5, 0:T]).then_inc(lora1_out, 1)
            take_proj(4)
            act.wait_ge(slab_done, 4)
            mix_high(4, rx_hi, 2)
            for i in range(5, 8):
                take_proj(i)
            act.wait_ge(lora1_mm, 3)
            nc.scalar.activation(sig_g[:, :], ps[:, 6, 0:T], ACT.Sigmoid).then_inc(lora1_out, 1)
            nc.scalar.activation(sig_g2[:, :], ps[0:GLORA - P, 7, 0:T], ACT.Sigmoid).then_inc(lora1_out, 1)

            def aux(g, k):
                n = aux_at(g, k)
                act.wait_ge(aux_ready, n + 1)
                return ps[:, n % 2, :]

            def squares(g):
                if g:
                    act.wait_ge(prep_ready, g)
                    act.wait_ge(a_ready, g)
                else:
                    act.wait_ge(mix_lo_done, 3)
                for m in range(2):
                    k2 = k_fm[:, 4 * g + 2 * m:4 * g + 2 * m + 2, :]
                    nc.scalar.activation(kk[:, 2 * m:2 * m + 2, :], k2, ACT.Copy, scale=pcol("rwkv_k_k", 2 * g + m))
                    ins = nc.scalar.activation(kmod[:, 2 * m:2 * m + 2, :], k2, ACT.Square,
                                               scale=pcol("rwkv_k_k", 2 * g + m))
                ins.then_inc(kk2_ready, 1)

            def exponentials(g):
                act.wait_ge(cum_ready, g + 1)
                nc.scalar.activation(e_pos[:, :, :], cum[:, :, :], ACT.Exp, scale=-DECAY)
                nc.scalar.activation(e_neg[:, :, :], cum[:, :, :], ACT.Exp, scale=DECAY)
                act.wait_ge(cprev_ready, g + 1)
                nc.scalar.activation(cprev[:, :, :], cprev[:, :, :], ACT.Exp, scale=-DECAY)
                nc.scalar.activation(sdec[:, g, :], sdec[:, g, :], ACT.Exp, scale=-DECAY).then_inc(exp_done, 1)

            def step(g, k):
                z = aux(g, k)
                if k in (A_W, A_A):
                    name, dst = (("rwkv_w0", sw), ("rwkv_a0", av))[k == A_A]
                    for m in range(2):
                        ins = nc.scalar.activation(dst[:, 2 * m:2 * m + 2, :], z[:, T * m:T * m + T].rearrange(
                            "p (t c) -> p t c", t=2), ACT.Sigmoid, bias=pcol(name, 2 * g + m))
                elif k == A_KK:
                    ins = nc.scalar.activation(norm_k[:, :, :], z.rearrange("p (a b) -> p a b", a=4), ACT.Sqrt)
                elif k == A_BON:
                    ins = nc.scalar.copy(bon[:, g, :], z[:, 0:8])
                elif k == A_BK:
                    ins = nc.scalar.copy(bk_tm[:, g % 2, :, :, :].rearrange("p a b c -> p (a b c)"), z)
                elif k == A_G:
                    ins = nc.scalar.copy(g_sb[:, :, :], z.rearrange("p (a b) -> p a b", a=2))
                elif k in (A_U0, A_U1):
                    ins = nc.scalar.copy(u_m[:, :], z[:, 0:256])
                elif k in (A_SA0, A_SA1):
                    ins = nc.scalar.copy(sa_m[:, k == A_SA1, :], z[:, 0:256])
                elif k == A_ST:
                    for m in range(2):
                        ins = nc.scalar.activation(state[:, m, :], z[:, HD * m:HD * m + HD], ACT.Copy,
                                                   scale=sdec[:, g, m:m + 1])
                elif k == A_Y:
                    ins = nc.scalar.copy(y_sb[:, :, :], z.rearrange("p (h c) -> p h c", h=8))
                else:
                    z = z.rearrange("p (a b) -> p a b", a=2)
                    if g:
                        act.wait_ge(rwkv_lo_done, g)
                    nc.scalar.copy(y_fm[:, :, :], z)
                    ins = nc.scalar.copy(mix_hi[:, 2 * g:2 * g + 2, :], z)
                ins.then_inc(aux_taken, 1)

            def deviation(g):
                act.wait_ge(yvar_ready, g + 1)
                nc.scalar.activation(ysd[:, :], yvar[:, :], ACT.Sqrt, bias=eps_c[:, 1:2], scale=1.0 / HD).then_inc(ysd_ready, 1)

            squares(0)
            take_proj(8)
            step(0, A_W)
            step(0, A_A)
            step(0, A_KK)
            take_proj(9)
            exponentials(0)
            take_proj(10)
            step(0, A_BON)
            take_proj(11)
            step(0, A_BK)
            for g in range(4):
                for t in range(TT):
                    act.wait_ge(inv_ready[t], INVR * g + 2)
                    nc.scalar.copy(nt_m[:, t].rearrange("p a b -> p (a b)"), ps[:, 4 + 3 * t, :]).then_inc(nt_taken[t], 1)
                if g < 3:
                    squares(g + 1)
                for slot in range(12):
                    for n, k in slot_steps(g, slot):
                        step(n, k)
                    if slot == 3 and g < 3:
                        exponentials(g + 1)
                    if slot == 8 and g:
                        deviation(g - 1)
            for n, k in tail_steps:
                if (n, k) == (3, A_YT):
                    deviation(3)
                    for i in range(2):
                        hi(first["rwkv_o"] + i + WS)
                step(n, k)
            def after(i):
                hi(i + WS)

            def norm_tokens(q, src):
                name, g_at, b_at, e, mean = NORMS[q]
                for t in range(TT):
                    act.wait_ge(stat_ready, 2 * q + t + 1)
                    nc.scalar.activation(sd[:, t:t + 1], mv[:, t, 1:2], ACT.Sqrt, bias=eps_c[:, e:e + 1]).then_inc(sd_ready, 1)
                    if q == 3:
                        continue
                    act.wait_ge(rstd_ready, 2 * q + t + 1)
                    at = slice(0, 512) if t else slice(0, C)
                    if mean:
                        ins = nc.scalar.activation(xn[:, t, at], src[:, t, at], ACT.Identity, scale=rstd[:, t:t + 1],
                                                   bias=shift[:, t:t + 1])
                    else:
                        ins = nc.scalar.activation(xn[:, t, at], src[:, t, at], ACT.Copy, scale=rstd[:, t:t + 1])
                    ins.then_inc(xn_act, 1)

            def feature_major(q, i):
                name, g_at, b_at, e, mean = NORMS[q]
                act.wait_ge(tr_ready, 4 * FM_NORMS.index(q) + i + 1)
                for m in range(2):
                    k = 2 * i + m
                    z = ps[:, 4 + i, T * m:T * m + T]
                    if b_at:
                        ins = nc.scalar.activation(x_fm[:, k, :], z, ACT.Identity, scale=pcol(g_at[0], g_at[1] + k),
                                                   bias=pcol(b_at[0], b_at[1] + k))
                    else:
                        ins = nc.scalar.activation(x_fm[:, k, :], z, ACT.Copy, scale=pcol(g_at[0], g_at[1] + k))
                link(ins)

            def high_part(q, i):
                if i in (1, 2):
                    act.wait_ge(xfm_ready, 2 * FM_NORMS.index(q) + i)
                nc.scalar.copy(x_hi[:, 2 * i:2 * i + 2, :], x_fm[:, 2 * i:2 * i + 2, :]).then_inc(xhi_ready, 1)

            def norm(q, src):
                norm_tokens(q, src)
                feature_major(q, 0)
                for i in range(3):
                    high_part(q, i)
                feature_major(q, 3)
                high_part(q, 3)

            def load_gain(which, layer, q):
                if q:
                    act.wait_ge(xtm_ready, q)
                else:
                    act.wait_ge(slab_done, first["rkv"] + 12)
                    act.wait_ge(y_ready, 4)
                for n, s in enumerate(("g", "b")):
                    nc.scalar.dma_start(gain[:, n, :], d[f"{which}_{s}"][layer:layer + 1, :].partition_broadcast(P))\
                        .then_inc(gain_loaded, 16)

            def ffn(name):
                s0, n, h0 = FFN[name]
                for j in range(n + 1):
                    up, down = ffn_slabs(name, j)
                    if j < n:
                        act.wait_ge(slab_done, up[0] + 1)
                        if h0 + j >= 2:
                            act.wait_ge(ffn_taken, h0 + j - 1)
                        nc.scalar.activation(act_f[:, j % 2, :], ps[:, 4 + 2 * (j % 2), :],
                                             ACT.Relu if name == "ff2" else ACT.Silu).then_inc(ffn_act, 1)
                        for i in up:
                            after(i)
                        act.wait_ge(ffn_taken, h0 + j + 1)
                        if j >= 3:
                            act.wait_ge(slab_done, ffn_slabs(name, j - 2)[1] + 1)
                        nc.scalar.copy(hid_hi[:, j % 3, :], hid[:, j % 2, :]).then_inc(hid_hi_done, 1)
                    if 0 < j < n:
                        after(down)

            def take(n, i, dst, scale=1.0):
                act.wait_ge(slab_done, i + 1)
                nc.scalar.activation(dst, ps[:, n % 3, :].rearrange("p (a b) -> p a b", a=2), ACT.Copy,
                                     scale=scale).then_inc(p_taken, 1)
                after(i)

            def exps(u, s, tiles):
                act.wait_ge(masked_ready, u + 1 - (4 if u >= U_ML else 0))
                for t, c0, c1 in tiles:
                    ins = nc.scalar.activation(s[:, u % 4, c0:c1], s[:, u % 4, c0:c1], ACT.Exp,
                                               bias=mx[:, 2 * (u % 4) + t:2 * (u % 4) + t + 1],
                                               accum_out=sm[:, 2 * (u % 4) + t:2 * (u % 4) + t + 1])
                ins.then_inc(exp_ready, 1)

            def take_pt(u, dst, n):
                act.wait_ge(pt_ready, u + 1)
                nc.scalar.copy(dst[:, u % 4, 0:n], ps[:, 4 + u % 4, 0:n]).then_inc(pt_taken, 1)

            def take_o(o, bank, o_sb, f2, ready=None):
                act.wait_ge(o_ready, ready or o + 1)
                if o:
                    act.wait_ge(o_lo_done, o)
                z = ps[:, bank, :].rearrange("p (a b) -> p a b", a=2)
                nc.scalar.copy(o_sb[:, :, :], z)
                nc.scalar.copy(mix_hi[:, f2, :], z).then_inc(o_taken, 1)

            load_gain("mix", 0, 0)
            after(first["rwkv_o"] + 2)
            norm(0, x_tm)
            after(first["rwkv_o"] + 3)
            load_gain("ffn", 0, 1)
            ffn("ffn0")
            norm(1, x_tm)
            after(first["ffn0"] + 32)
            nc.scalar.dma_start(rope_c[:, :], d["const_rope"]).then_inc(late_loaded, 16)
            nc.scalar.dma_start(gsel[:, :], d["const_gates"]).then_inc(late_loaded, 16)
            nc.scalar.dma_start(gate_w[:, :, :], d["gate_w"]).then_inc(late_loaded, 16)
            nc.scalar.dma_start(gate_bf[:, :], d["gate_b"][0:12]).then_inc(late_loaded, 16)
            nc.scalar.dma_start(gate_bi[:, :], d["gate_b"][12:16]).then_inc(late_loaded, 16)
            load_gain("mix", 1, 2)
            for g in range(-1, 4):
                if g >= 0:
                    for u in range(4 * g, 4 * g + 4):
                        exps(U_MOBA + u, ma_s, CAUSAL)
                if g < 3:
                    for n, dst in enumerate((ma_q, ma_k, ma_vv[:, (g + 1) % 2])):
                        take(3 * g + 3 + n, first["qkv"] + 3 * g + 3 + n, dst if n == 2 else dst[:, :, :])
                if g >= 0:
                    for u in range(4 * g, 4 * g + 4):
                        take_pt(U_MOBA + u, ma_p, 3 * P)
                    take_o(O_MOBA + g, 3, ma_o, slice(2 * g, 2 * g + 2))
            for i in range(3):
                after(first["moba_o"] + i)
            norm(2, x_tm)
            after(first["moba_o"] + 3)
            load_gain("ffn", 1, 3)
            ffn("ffn1")
            norm_tokens(3, x_tm)
            norm(4, x_tm)
            after(first["ffn1"] + 32)
            nc.scalar.dma_start(gain[:, :, :], d["mem"]).then_inc(mem_loaded, 16)
            act.wait_ge(gate_abs, 1)
            link(nc.scalar.activation(za[:, :], za[:, :], ACT.Exp, scale=-1.0))
            nc.scalar.activation(za[:, :], za[:, :], ACT.Ln, bias=1.0).then_inc(gate_ln, 1)

            def takes(section, n, dst, scale=lambda j: 1.0):
                for j in range(n):
                    take(P_FIRST[section] + j, first[section] + j, dst(j), scale(j))
            takes("ml_qk", 4, lambda j: conv_in[:, 2 * j:2 * j + 2, 3:T + 3])
            norm_tokens(5, gain)
            takes("ml_v", 2, lambda j: ml_v[:, :, 256 * j:256 * j + 256])
            for i in (0, 3):
                feature_major(5, i)
            for j in range(2):
                act.wait_ge(slab_done, first["ml_o"] + j + 1)
                n = P_FIRST["ml_o"] + j
                nc.scalar.activation(ml_o[:, :, 256 * j:256 * j + 256], ps[:, n % 3, :].rearrange("p (a b) -> p a b", a=2),
                                     ACT.Sigmoid).then_inc(p_taken, 1)
                after(first["ml_o"] + j)
            act.wait_ge(conv_ready, 1)
            nc.scalar.activation(conv_out[:, :, :], conv_out[:, :, :], ACT.Silu).then_inc(silu_ready, 1)
            takes("fx_qk", 4, lambda j: (fx_q, fx_k)[j // 2][:, 2 * (j % 2):2 * (j % 2) + 2, :],
                  lambda j: (HD ** -0.5, 1.0)[j // 2])
            takes("fx_v", 2, lambda j: fx_v[:, :, 256 * j:256 * j + 256])
            for i in range(4):
                high_part(5, i)

            def take_memory(n):
                j = n % 4
                act.wait_ge(slab_done, memory_slab(n) + 1)
                z = ps[:, 2, :].rearrange("p (a b) -> p a b", a=2)
                dst = gain[:, :, 256 * j:256 * j + 256] if n >= 4 else xk_fm[:, 2 * j:2 * j + 2, 0:T]
                nc.scalar.copy(dst, z).then_inc(p_taken, 1)
                after(memory_slab(n))

            act.wait_ge(gate_tr, 1)
            nc.scalar.copy(tc[:, :, :], ps[:, 3, 0:P].rearrange("p (a b) -> p a b", a=2)).then_inc(gate_cols, 1)
            act.wait_ge(em_ready, 1)
            nc.scalar.activation(em[:, :], em[:, :], ACT.Exp, scale=-1.0).then_inc(em_ready, 1)
            for u in range(4):
                act.wait_ge(row_taken, u + 1)
                nc.scalar.activation(bias[:, u, :], bias[:, u, :], ACT.Exp).then_inc(w_ready, 1)
            take_memory(0)
            take_memory(1)
            for u in range(4):
                take_pt(U_ML + u, se_p, 3 * P)
            take_memory(2)
            for g in range(2):
                take_memory(3 + 2 * g)
                for u in range(4):
                    exps(U_FX + 4 * g + u, se_s, CAUSAL)
                if g == 0:
                    act.wait_ge(ml_var, 1)
                    nc.scalar.activation(ml_rs[:, :], ml_rs[:, :], ACT.Sqrt, scale=1.0 / P, bias=eps_c[:, 2:3]).then_inc(ml_sd, 1)
                else:
                    for b in range(2):
                        act.wait_ge(ml_fm, b + 1)
                        nc.scalar.copy(mix_hi[:, 2 * b:2 * b + 2, :], se_o[:, :, :]).then_inc(o_taken, 1)
                take_memory(4 + 2 * g)
                for u in range(4):
                    take_pt(U_FX + 4 * g + u, se_p, 3 * P)
                take_o(O_FX + 3 * g, 3, se_o, slice(4 + 2 * g, 6 + 2 * g), O_ML + 3 + g)
            take_memory(7)
            for i in range(3):
                after(first["mix_o"] + i)
            norm(6, x_tm)
            after(first["mix_o"] + 3)
            takes("x_q", 4, lambda j: xq_fm[:, 2 * j:2 * j + 2, :], lambda j: (C // 4) ** -0.5)
            for u in range(4):
                exps(U_X + u, cr_s, FULL)
            for u in range(4):
                take_pt(U_X + u, cr_p, 512)
            for u in range(4):
                take_o(O_X + u, u, cr_o, slice(2 * u, 2 * u + 2))
            nc.scalar.dma_start(gain[:, 0, :], d["final_g"].partition_broadcast(P)).then_inc(gain_loaded, 16)
            for i in range(3):
                after(first["x_o"] + i)
            norm(7, x_tm)
            after(first["x_o"] + 3)
            ffn("ff2")
            norm_tokens(8, x_tm)
            for t in range(TT):
                act.wait_ge(final_ready, t + 1)
                nc.scalar.dma_start(out[:, t, :], xn[:, t, :]).then_inc(out_stored, 16)
            act.wait_ge(out_stored, 32)

        @block.gpsimd
        def _(pool):
            plink = chain(pool, pool_step)

            def lo(i):
                if i >= n_slabs or lo_engine(i)[0] != "pool":
                    return
                pool.wait_ge(hi_done, i + 1)
                nc.gpsimd.tensor_tensor(w_lo[:, i % WS, :], w_raw[:, i % RAW, :], w_hi[:, i % WS, :].bitcast(F32),
                                        ALU.subtract).then_inc(lo_pool, 1)
            for i in range(first["rwkv_o"]):
                lo(i)

            def operands(g):
                k4 = slice(4 * g, 4 * g + 4)
                tt = nc.gpsimd.tensor_tensor
                pool.wait_ge(cum_ready, g + 1)
                tt(cprev[:, :, :], cum[:, :, :], sw[:, :, :], ALU.subtract).then_inc(cprev_ready, 1)
                pool.wait_ge(kmod_ready, g + 1)
                pool.wait_ge(cprev_ready, g + 1)
                tt(sw[:, :, :], r_fm[:, k4, :], kmod[:, :, :], ALU.mult).then_inc(rkr_ready, 1)
                pool.wait_ge(kk_ready, 2 * g + 2)
                if g:
                    for t in range(TT):
                        pool.wait_ge(inv_ready[t], INVR * (g - 1) + 3)
                plink(tt(b_t[:, :, :], kk[:, :, :], av[:, :, :], ALU.mult))
                pool.wait_ge(exp_done, g + 1)
                tt(b_t[:, :, :], b_t[:, :, :], e_neg[:, :, :], ALU.mult)
                tt(k_t[:, :, :], kmod[:, :, :], e_neg[:, :, :], ALU.mult)
                pool.wait_ge(rkr_ready, g + 1)
                tt(r_fm[:, k4, :], r_fm[:, k4, :], e_pos[:, :, :], ALU.mult).then_inc(prep_ready, 1)

            def outputs(g):
                at = slice(256 * g, 256 * g + 256)
                tt = nc.gpsimd.tensor_tensor
                pool.wait_ge(ymean_ready, g + 1)
                plink(tt(y_sb[:, :, :], y_sb[:, :, :], along(ymean[:, :], HD), ALU.subtract))
                tt(y_sq[:, :, :], y_sb[:, :, :], y_sb[:, :, :], ALU.mult).then_inc(ysq_ready, 1)
                pool.wait_ge(yvar_ready, g + 1)
                v8 = v_tm[:, :, at].rearrange("p t (h c) -> p t h c", c=HD)
                for t in range(TT):
                    tt(y_sq[:, 4 * t:4 * t + 4, :], v8[:, t], along(bon[:, g, 4 * t:4 * t + 4], HD), ALU.mult)
                pool.wait_ge(yrs_ready, g + 1)
                plink(tt(y_sb[:, :, :], y_sb[:, :, :], along(yrs[:, :], HD), ALU.mult))
                flat = lambda y: y[:, :, :].rearrange("p (t h) c -> p t (h c)", t=TT)
                pool.wait_ge(gate_lora_loaded, 64 * (g + 1))
                plink(tt(flat(y_sb), flat(y_sb), over(gn_g[:, :], TT), ALU.mult))
                plink(tt(flat(y_sb), flat(y_sb), over(gn_b[:, :], TT), ALU.add))
                plink(tt(flat(y_sb), flat(y_sb), flat(y_sq), ALU.add))
                pool.wait_ge(aux_taken, aux_at(g, A_G) + 1)
                tt(flat(y_sb), flat(y_sb), g_sb[:, :, :], ALU.mult).then_inc(y_ready, 1)

            operands(0)
            for i in range(WS):
                lo(first["rwkv_o"] + i)
            for g in range(4):
                if g < 3:
                    operands(g + 1)
                if g:
                    outputs(g - 1)
            pool.wait_ge(prep_ready, 4)
            pool.wait_ge(aux_taken, aux_at(3, A_BON) + 1)
            e4 = e_pos[:, :, :].rearrange("p (t a) (h c) -> p t (a h) c", t=TT, c=HD)
            for t in range(TT):
                ins = nc.gpsimd.tensor_tensor(e4[:, t], v_tm[:, t, 768:1024].rearrange("p (h c) -> p h c", c=HD),
                                              along(bon[:, 3, 4 * t:4 * t + 4], HD), ALU.mult)
            ins.then_inc(bonus_ready, 1)
            def gain_offset(q):
                pool.wait_ge(xn_act, 2 * q + 2)
                pool.wait_ge(xn_dve, q + 1)
                pool.wait_ge(gain_loaded, 32 * (q + 1))
                for t in range(TT):
                    ins = nc.gpsimd.tensor_tensor(x_tm[:, t, :], xn[:, t, :], gain[:, 0, :], ALU.mult)
                plink(ins)
                for t in range(TT):
                    ins = nc.gpsimd.tensor_tensor(x_tm[:, t, :], x_tm[:, t, :], gain[:, 1, :], ALU.add)
                ins.then_inc(xtm_ready, 1)

            at = first["rwkv_o"] + WS
            for q, last in enumerate((first["rwkv_o"] + 3, first["ffn0"] + 32, first["moba_o"] + 3)):
                for i in range(at, last + 1 + WS):
                    lo(i)
                gain_offset(q)
                at = last + 1 + WS
            for i in range(at, n_slabs):
                lo(i)

        @block.vector
        def _(dve):
            link = chain(dve, dve_step)
            V = nc.vector
            for n, e in enumerate((LN_EPS, GN_EPS, RMS_EPS)):
                ins = V.memset(eps_c[:, n:n + 1], e)
            link(ins)

            def lo(i):
                if i >= n_slabs or lo_engine(i)[0] != "dve":
                    return
                dve.wait_ge(hi_done, i + 1)
                V.tensor_tensor(w_lo[:, i % WS, :], w_raw[:, i % RAW, :], w_hi[:, i % WS, :].bitcast(F32),
                                ALU.subtract).then_inc(lo_dve, 1)

            def mix(q):
                if q in (2, 3):
                    dve.wait_ge(mix_hi_done, q - 1)
                    dve.wait_ge(mix_lo_done, q - 1)
                elif q in (4, 5):
                    dve.wait_ge(lora1_mm, q - 3)
                for k in range(KT):
                    ins = V.scalar_tensor_tensor(mixed[:, q % 2, k, :], xx[:, k, :], pcol("rwkv_mu", KT * MIXES[q][1] + k),
                                                 xt[:, k, :], ALU.mult, ALU.add)
                ins.then_inc(mixed_ready, 1)

            def mix_low(n, q, dst, high):
                dve.wait_ge(mix_hi_done, n + 1)
                V.tensor_tensor(dst[:, :, :], mixed[:, q % 2, :, :], high[:, :, :].bitcast(F32),
                                ALU.subtract).then_inc(mix_lo_done, 1)

            dve.wait_ge(xt_loaded, 16)
            dve.wait_ge(par_loaded, 16)
            V.tensor_tensor(xx[:, :, 1:T], xt[:, :, 0:T - 1], xt[:, :, 1:T], ALU.subtract)
            link(V.tensor_scalar(xx[:, :, 0:1], xt[:, :, 0:1], -1.0, None, ALU.mult))
            mix(0)
            mix_low(0, 0, rx_lo, rx_hi)
            lo(0)
            mix(1)
            lo(2)
            mix_low(1, 1, mix_lo, mix_hi)
            mix(2)
            lo(4)
            mix(3)
            lo(6)
            mix(4)
            dve.wait_ge(slab_done, 4)
            mix_low(2, 4, rx_lo, rx_hi)
            mix(5)
            for i in range(8, 12, 2):
                lo(i)

            dve.wait_ge(consts_loaded, 32)
            dve.wait_ge(par_loaded, 16)
            for k in range(KT):
                ins = V.tensor_scalar(rk_sel[:, k, :], rc("headsel"), pcol("rwkv_r_k", k), None, ALU.mult)
            link(ins)
            flat = lambda t: t.rearrange("p a b -> p (a b)")

            def decays(g):
                dve.wait_ge(aux_taken, aux_at(g, A_W) + 1)
                link(V.tensor_tensor_scan(flat(cum), rc("reset"), flat(sw), 0.0, ALU.mult, ALU.add))
                link(V.tensor_copy(smid[:, :], cum[:, :, P // 2 - 1]))
                last = cum[:, :, :].rearrange("p (a t) c -> p a t c", t=TT)[:, :, 1, P - 1]
                mid = smid[:, :].rearrange("p (a t) -> p a t", t=TT)
                link(V.tensor_tensor(sdec[:, g, :], cum[:, :, :].rearrange("p (a t) c -> p a t c", t=TT)[:, :, 0, P - 1],
                                     mid[:, :, 0], ALU.subtract))
                link(V.tensor_tensor(sdec[:, g, :], sdec[:, g, :], mid[:, :, 1], ALU.add))
                V.tensor_tensor(cum[:, :, :], cum[:, :, :], along(smid[:, :], P), ALU.subtract).then_inc(cum_ready, 1)

            def modified_k(g):
                dve.wait_ge(aux_taken, aux_at(g, A_A) + 1)
                dve.wait_ge(aux_ready, aux_at(g, A_KK) + 1)
                for m in range(2):
                    at = slice(2 * m, 2 * m + 2)
                    ins = V.tensor_scalar(kmod[:, at, :], av[:, at, :], 1.0, pcol("rwkv_k_a", 2 * g + m),
                                          ALU.subtract, ALU.mult)
                link(ins)
                V.scalar_tensor_tensor(kmod[:, :, :], kmod[:, :, :], 1.0, k_fm[:, 4 * g:4 * g + 4, :],
                                       ALU.add, ALU.mult).then_inc(kmod_ready, 1)

            def normalized_k(g, m):
                at = slice(2 * m, 2 * m + 2)
                dve.wait_ge(aux_taken, aux_at(g, A_KK) + 1)
                link(V.tensor_scalar(norm_k[:, at, :], norm_k[:, at, :], 1e-12, None, ALU.max))
                link(V.reciprocal(norm_k[:, at, :], norm_k[:, at, :]))
                V.tensor_tensor(kk[:, at, :], kk[:, at, :], norm_k[:, at, :], ALU.mult).then_inc(kk_ready, 1)

            def a_tilde(g):
                dve.wait_ge(exp_done, g + 1)
                dve.wait_ge(kk_ready, 2 * g + 2)
                dve.wait_ge(kmod_ready, g + 1)
                V.scalar_tensor_tensor(k_fm[:, 4 * g:4 * g + 4, :], kk[:, :, :], -1.0, cprev[:, :, :],
                                       ALU.mult, ALU.mult).then_inc(a_ready, 1)

            def y_mean(g):
                dve.wait_ge(aux_taken, aux_at(g, A_Y) + 1)
                link(V.tensor_reduce(ymean[:, :], y_sb[:, :, :], AX_X, ALU.add))
                V.tensor_scalar(ymean[:, :], ymean[:, :], 1.0 / HD, None, ALU.mult).then_inc(ymean_ready, 1)

            def y_variance(g):
                dve.wait_ge(ysq_ready, g + 1)
                V.tensor_reduce(yvar[:, :], y_sq[:, :, :], AX_X, ALU.add).then_inc(yvar_ready, 1)

            def y_scale(g):
                dve.wait_ge(ysd_ready, g + 1)
                V.reciprocal(yrs[:, :], ysd[:, :]).then_inc(yrs_ready, 1)

            def mix_out_low(g):
                dve.wait_ge(aux_taken, aux_at(g, A_YT) + 1)
                V.tensor_tensor(mix_lo[:, 2 * g:2 * g + 2, :], y_fm[:, :, :], mix_hi[:, 2 * g:2 * g + 2, :].bitcast(F32),
                                ALU.subtract).then_inc(rwkv_lo_done, 1)

            def last_outputs():
                y_mean(3)
                dve.wait_ge(ymean_ready, 4)
                link(V.tensor_tensor(y_sb[:, :, :], y_sb[:, :, :], along(ymean[:, :], HD), ALU.subtract))
                V.tensor_tensor(y_sq[:, :, :], y_sb[:, :, :], y_sb[:, :, :], ALU.mult).then_inc(ysq_ready, 1)
                y_variance(3)
                y2 = y_sb[:, :, :].rearrange("p (t h) c -> p t (h c)", t=TT)
                dve.wait_ge(gate_lora_loaded, 256)
                y_scale(3)
                dve.wait_ge(yrs_ready, 4)
                link(V.tensor_tensor(y_sb[:, :, :], y_sb[:, :, :], along(yrs[:, :], HD), ALU.mult))
                link(V.tensor_tensor(y2, y2, over(gn_g[:, :], TT), ALU.mult))
                link(V.tensor_tensor(y2, y2, over(gn_b[:, :], TT), ALU.add))
                dve.wait_ge(bonus_ready, 1)
                link(V.tensor_tensor(y2, y2, e_pos[:, :, :].rearrange("p (t a) c -> p t (a c)", t=TT), ALU.add))
                dve.wait_ge(aux_taken, aux_at(3, A_G) + 1)
                V.tensor_tensor(y2, y2, g_sb[:, :, :], ALU.mult).then_inc(y_ready, 1)

            def take_scores(g):
                d_g, rb_g, ak_g, rk_g = d_m[g % 2], rb_m[g % 2], ak_m[g % 2], rk_m[g % 2]
                for t in range(TT):
                    dve.wait_ge(inv_ready[t], INVR * g + 1)
                    ba = ps[:, 2 + 3 * t:4 + 3 * t, :].rearrange("p b (h s c) -> p (b h) s c", h=2, s=2)
                    for b in range(2):
                        V.tensor_tensor(w_m[:, t, 2 * b:2 * b + 2], ba[:, 2 * b:2 * b + 2, 0], over(rc("level0"), 2), ALU.mult)
                        ins = V.tensor_tensor(rb_g[:, t, 2 * b:2 * b + 2], ba[:, 2 * b:2 * b + 2, 1], over(rc("incl"), 2), ALU.mult)
                    link(ins)
                    V.tensor_tensor(d_g[:, t], w_m[:, t], over(ident, 4), ALU.add).then_inc(inv_taken[t], 1)
                for t in range(TT):
                    dve.wait_ge(nt_taken[t], g + 1)
                    link(V.tensor_tensor(dt_m[:, t], nt_m[:, t], over(rc("level0T"), 4), ALU.mult))
                    link(V.tensor_tensor(dt_m[:, t], dt_m[:, t], over(ident, 4), ALU.add))
                    dve.wait_ge(inv_ready[t], INVR * g + 3)
                    ka = ps[:, 2 + 3 * t:4 + 3 * t, :].rearrange("p b (h s c) -> p (b h) s c", h=2, s=2)
                    for b in range(2):
                        V.tensor_tensor(ak_g[:, t, 2 * b:2 * b + 2], ka[:, 2 * b:2 * b + 2, 0], over(rc("strict"), 2), ALU.mult)
                        ins = V.tensor_tensor(rk_g[:, t, 2 * b:2 * b + 2], ka[:, 2 * b:2 * b + 2, 1], over(rc("incl"), 2), ALU.mult)
                    ins.then_inc(inv_taken[t], 1)

            def take_half_level(g, slot):
                n, d_g = slot // 2 + 1, d_m[g % 2]
                b4 = lambda b: ps[:, b, :].rearrange("p (h c) -> p h c", h=4)
                for t in range(TT):
                    dve.wait_ge(inv_ready[t], INVR * g + 3 + slot + 1)
                    if slot % 2 == 0:
                        V.tensor_tensor(w_m[:, t], b4(2 + 3 * t), over(rc(f"level{n}"), 4), ALU.mult).then_inc(inv_taken[t], 1)
                    else:
                        if n < NL - 1:
                            V.tensor_tensor(dt_m[:, t], b4(4 + 3 * t), dt_m[:, t], ALU.add)
                        V.tensor_tensor(d_g[:, t], b4(3 + 3 * t), d_g[:, t], ALU.add).then_inc(inv_taken[t], 1)

            dve.wait_ge(aux_taken, 1)
            decays(0)
            modified_k(0)
            normalized_k(0, 0)
            normalized_k(0, 1)
            a_tilde(0)
            for i in range(12, 15, 2):
                lo(i)
            for g in range(4):
                take_scores(g)
                for slot in range(12):
                    take_half_level(g, slot)
                    if slot == 4 and g > 1:
                        mix_out_low(g - 2)
                    if g < 3:
                        if slot == 1:
                            decays(g + 1)
                        elif slot == 3:
                            modified_k(g + 1)
                        elif slot in (4, 5):
                            normalized_k(g + 1, slot - 4)
                        elif slot == 6:
                            a_tilde(g + 1)
                    if g:
                        if slot == 7:
                            y_mean(g - 1)
                        elif slot == 8:
                            y_variance(g - 1)
                        elif slot == 9:
                            y_scale(g - 1)
            mix_out_low(2)
            last_outputs()
            for i in range(2):
                lo(first["rwkv_o"] + i + WS)
            mix_out_low(3)
            def after(i):
                lo(i + WS)

            def add_product(src, scale, t, last_slab, half, base=0):
                if t:
                    dve.wait_ge(slab_done, last_slab + 1)
                else:
                    dve.wait_ge(half_done, half)
                for n in range(2):
                    at = src[:, t, 512 * n:512 * n + 512]
                    ins = V.scalar_tensor_tensor(at, at, scale, ps[:, base + 2 * t + n, :], ALU.mult, ALU.add)
                link(ins)

            def norm_tokens(q, src, scale=None, last_slab=None, half=None):
                name, g_at, b_at, e, mean = NORMS[q]

                def add(t):
                    if scale is not None:
                        add_product(src, scale, t, last_slab, half, 0 if q else 4)

                def statistics(t):
                    for n in range(2):
                        ins = V.bn_stats(stats[:, t, n, :], src[:, t, 512 * n:512 * n + 512])
                    link(ins)
                    ins = V.bn_aggr(mv[:, t, :], stats[:, t, :, :].rearrange("p a b -> p (a b)"))
                    if not mean:
                        link(ins)
                        link(V.tensor_tensor(sd[:, t:t + 1], mv[:, t, 0:1], mv[:, t, 0:1], ALU.mult))
                        ins = V.tensor_tensor(mv[:, t, 1:2], mv[:, t, 1:2], sd[:, t:t + 1], ALU.add)
                    ins.then_inc(stat_ready, 1)

                def scales(t):
                    dve.wait_ge(sd_ready, 2 * q + t + 1)
                    link(V.reciprocal(rstd[:, t:t + 1], sd[:, t:t + 1]))
                    V.scalar_tensor_tensor(shift[:, t:t + 1], mv[:, t, 0:1], -1.0, rstd[:, t:t + 1],
                                           ALU.mult, ALU.mult).then_inc(rstd_ready, 1)

                add(0)
                statistics(0)
                add(1)
                scales(0)
                statistics(1)
                scales(1)
                if q == 3:
                    return
                dve.wait_ge(rstd_ready, 2 * q + 2)
                if mean:
                    ins = V.tensor_scalar(xn[:, 1, 512:C], src[:, 1, 512:C], mv[:, 1, 0:1], rstd[:, 1:2],
                                          ALU.subtract, ALU.mult)
                else:
                    ins = V.tensor_scalar(xn[:, 1, 512:C], src[:, 1, 512:C], rstd[:, 1:2], None, ALU.mult)
                ins.then_inc(xn_dve, 1)

            def features(q):
                name, g_at, b_at, e, mean = NORMS[q]
                for i in (1, 2):
                    dve.wait_ge(tr_ready, 4 * FM_NORMS.index(q) + i + 1)
                    for m in range(2):
                        k = 2 * i + m
                        z = ps[:, 4 + i, T * m:T * m + T]
                        if b_at:
                            ins = V.tensor_scalar(x_fm[:, k, :], z, pcol(g_at[0], g_at[1] + k), pcol(b_at[0], b_at[1] + k),
                                                  ALU.mult, ALU.add)
                        else:
                            ins = V.tensor_scalar(x_fm[:, k, :], z, pcol(g_at[0], g_at[1] + k), None, ALU.mult)
                    ins.then_inc(xfm_ready, 1)

            def low_parts(q):
                for i in range(4):
                    dve.wait_ge(xhi_ready, 4 * FM_NORMS.index(q) + i + 1)
                    k = slice(2 * i, 2 * i + 2)
                    V.tensor_tensor(x_lo[:, k, :], x_fm[:, k, :], x_hi[:, k, :].bitcast(F32), ALU.subtract)\
                     .then_inc(xlo_ready, 1)

            def norm(q, *how):
                norm_tokens(q, *how)
                features(q)
                low_parts(q)

            def scale_stream():
                dve.wait_ge(rstd_ready, 8)
                dve.wait_ge(gain_loaded, 128)
                for t in range(TT):
                    link(V.scalar_tensor_tensor(x_tm[:, t, :], x_tm[:, t, :], mv[:, t, 0:1], gain[:, 0, :],
                                                ALU.subtract, ALU.mult))
                    link(V.scalar_tensor_tensor(x_tm[:, t, :], x_tm[:, t, :], rstd[:, t:t + 1], gain[:, 1, :],
                                                ALU.mult, ALU.add))

            def ffn(name):
                s0, n, h0 = FFN[name]
                for j in range(n + 1):
                    up, down = ffn_slabs(name, j)
                    if j < n:
                        dve.wait_ge(slab_done, up[-1] + 1)
                        dve.wait_ge(ffn_act, h0 + j + 1)
                        if h0 + j >= 2:
                            dve.wait_ge(hid_hi_done, h0 + j - 1)
                        if name == "ff2":
                            V.scalar_tensor_tensor(hid[:, j % 2, :], ps[:, 4 + 2 * (j % 2), :], 0.0, act_f[:, j % 2, :],
                                                   ALU.max, ALU.mult).then_inc(ffn_taken, 1)
                        else:
                            V.tensor_tensor(hid[:, j % 2, :], act_f[:, j % 2, :], ps[:, 5 + 2 * (j % 2), :],
                                            ALU.mult).then_inc(ffn_taken, 1)
                        for i in up:
                            after(i)
                        dve.wait_ge(hid_hi_done, h0 + j + 1)
                        V.tensor_tensor(hid_lo[:, j % 3, :], hid[:, j % 2, :], hid_hi[:, j % 3, :].bitcast(F32),
                                        ALU.subtract).then_inc(hid_ready, 1)
                    if 0 < j < n:
                        after(down)

            def masked(u, s, tiles, mask):
                dve.wait_ge(scores_ready, u + 1)
                for t, c0, c1 in tiles:
                    n = 2 * (u % 4) + t
                    ins = V.tensor_tensor_reduce(out=s[:, u % 4, c0:c1], in0=ps[:, 4 + u % 4, c0:c1], in1=mask(u, t, c0, c1),
                                                 scale=1.0, scalar=-3.0e38, op0=ALU.add, op1=ALU.max,
                                                 accum_out=rs[:, n:n + 1])
                link(ins)
                n = 2 * (u % 4)
                V.tensor_scalar(mx[:, n:n + 2], rs[:, n:n + 2], -1.0, None, ALU.mult).then_inc(masked_ready, 1)

            def probs(u, s, tiles):
                dve.wait_ge(exp_ready, u + 1 - (4 if u >= U_ML else 0))
                n = 2 * (u % 4)
                link(V.reciprocal(rs[:, n:n + 2], sm[:, n:n + 2]))
                for t, c0, c1 in tiles:
                    ins = V.tensor_scalar(s[:, u % 4, c0:c1], s[:, u % 4, c0:c1], rs[:, n + t:n + t + 1], None, ALU.mult)
                ins.then_inc(p_ready, 1)

            def out_low(o, o_sb, f2):
                dve.wait_ge(o_taken, o + 1)
                V.tensor_tensor(mix_lo[:, f2, :], o_sb[:, :, :], mix_hi[:, f2, :].bitcast(F32),
                                ALU.subtract).then_inc(o_lo_done, 1)

            def causal_mask(u, t, c0, c1):
                return causal[:, c0:c1]

            after(first["rwkv_o"] + 2)
            dve.wait_ge(x_loaded, 16)
            norm(0, x_tm, ALPHA, first["rwkv_o"] + 3, 1)
            after(first["rwkv_o"] + 3)
            ffn("ffn0")
            dve.wait_ge(xtm_ready, 1)
            norm(1, x_tm, ALPHA, first["ffn0"] + 32, 2)
            after(first["ffn0"] + 32)
            dve.wait_ge(late_loaded, 80)
            cos, sin = rope_c[:, 0:T], rope_c[:, T:2 * T]
            def rope(g):
                for n, src, dst, c in ((0, ma_q, ma_q2, HD ** -0.5), (1, ma_k, ma_k2, 1.0)):
                    dve.wait_ge(rot_ready, 2 * g + n + 1)
                    for m in range(2):
                        V.scalar_tensor_tensor(rt[:, m, :], ps[:, 3, T * m:T * m + T], c, sin, ALU.mult, ALU.mult)
                        ins = V.scalar_tensor_tensor(dst[:, m, :], src[:, m, :], c, cos, ALU.mult, ALU.mult)
                    link(ins)
                    V.tensor_tensor(dst[:, :, :], dst[:, :, :], rt[:, :, :], ALU.add).then_inc(rope_done, 1)

            for g in range(-1, 4):
                if g >= 0:
                    for u in range(4 * g, 4 * g + 4):
                        masked(U_MOBA + u, ma_s, CAUSAL, causal_mask)
                if g < 3:
                    n = first["qkv"] + 3 * (g + 1)
                    after(n)
                    after(n + 1)
                    rope(g + 1)
                if g >= 0:
                    for u in range(4 * g, 4 * g + 4):
                        probs(U_MOBA + u, ma_s, CAUSAL)
                if g < 3:
                    after(n + 2)
                if g >= 0:
                    out_low(O_MOBA + g, ma_o, slice(2 * g, 2 * g + 2))
            for i in range(3):
                after(first["moba_o"] + i)
            dve.wait_ge(xtm_ready, 2)
            norm(2, x_tm, ALPHA, first["moba_o"] + 3, 3)
            after(first["moba_o"] + 3)
            ffn("ffn1")
            dve.wait_ge(xtm_ready, 3)
            norm_tokens(3, x_tm, ALPHA, first["ffn1"] + 32, 4)
            scale_stream()
            norm(4, x_tm)
            after(first["ffn1"] + 32)
            V.memset(conv_in[:, :, 0:3], 0.0)
            V.memset(ones_t[:, :], 1.0)
            link(V.memset(gst[:, :], 0.0))
            dve.wait_ge(late_loaded, 80)
            dve.wait_ge(gate_mm, 1)
            link(V.tensor_scalar(zf[:, :], ps[0:12, 3, 0:T], gate_bf[:, :], None, ALU.add))
            link(V.tensor_scalar(gi[0:4, :], ps[0:4, 3, T:2 * T], gate_bi[:, :], None, ALU.add))
            V.scalar_tensor_tensor(za[:, :], zf[:, :], -1.0, zf[:, :], ALU.mult, ALU.max).then_inc(gate_abs, 1)
            dve.wait_ge(gate_ln, 1)
            link(V.tensor_scalar(zf[:, :], zf[:, :], 0.0, None, ALU.min))
            link(V.tensor_tensor(zf[:, :], zf[:, :], za[:, :], ALU.subtract))
            link(V.tensor_tensor_scan(gst[0:12, :], ones_t[:, :], zf[:, :], 0.0, ALU.mult, ALU.add))
            link(V.tensor_tensor(gi[0:4, :], gi[0:4, :], gst[0:4, :], ALU.subtract))
            V.tensor_tensor_scan(gst[32:36, :], ones_t[0:4, :], gi[0:4, :], 0.0, ALU.mult, ALU.max).then_inc(gate_rows, 1)
            for j in range(4):
                after(first["ml_qk"] + j)
            dve.wait_ge(mem_loaded, 16)
            norm_tokens(5, gain)
            dve.wait_ge(p_taken, P_FIRST["ml_qk"] + 4)
            for k in range(KT):
                ins = V.tensor_scalar(conv_out[:, k, :], conv_in[:, k, 0:T], pcol("ml_conv_w_2", k), pcol("ml_conv_b_2", k),
                                      ALU.mult, ALU.add)
            link(ins)
            for n in range(1, 4):
                if n == 2:
                    for j in range(2):
                        after(first["ml_v"] + j)
                for k in range(KT):
                    ins = V.scalar_tensor_tensor(conv_out[:, k, :], conv_in[:, k, n:n + T], pcol("ml_conv_w_2", KT * n + k),
                                                 conv_out[:, k, :], ALU.mult, ALU.add)
                if n < 3:
                    link(ins)
                else:
                    ins.then_inc(conv_ready, 1)
            features(5)
            for name, n in (("ml_o", 2), ("fx_qk", 4), ("fx_v", 2)):
                for j in range(n):
                    after(first[name] + j)
            dve.wait_ge(silu_ready, 1)
            V.tensor_scalar(conv_out[:, 4:8, :], conv_out[:, 4:8, :], P ** -0.5, None, ALU.mult).then_inc(silu_ready, 1)
            low_parts(5)
            dve.wait_ge(gate_cols, 1)
            for t in range(TT):
                ins = V.tensor_tensor(em[:, 4 * t:4 * t + 4], tc[:, t, 0:4], tc[:, t, 32:36], ALU.add)
            ins.then_inc(em_ready, 1)

            def rows(u, n):
                dve.wait_ge(row_ready, n + 1)
                for t, c0, c1 in CAUSAL:
                    z = ps[:, 3, 0:c1 - c0]
                    dst = bias[:, u, c0:c1]
                    if n < 4:
                        ins = V.scalar_tensor_tensor(dst, z, tc[:, t, 32 + n:33 + n], causal[:, c0:c1], ALU.subtract, ALU.add)
                    else:
                        link(V.tensor_scalar(dst, z, -1.0, tc[:, t, n:n + 1], ALU.mult, ALU.add))
                        ins = V.tensor_tensor(dst, dst, causal[:, c0:c1], ALU.add)
                ins.then_inc(row_taken, 1)

            def fx_bias(g):
                for u in range(4):
                    rows(u, 4 + 4 * g + u)

            def fx_masked(g):
                dve.wait_ge(row_taken, 8 + 4 * g)
                for u in range(4):
                    masked(U_FX + 4 * g + u, se_s, CAUSAL, lambda w, t, c0, c1: bias[:, w % 4, c0:c1])

            def fx_probs(g):
                for u in range(4):
                    probs(U_FX + 4 * g + u, se_s, CAUSAL)

            for u in range(4):
                rows(u, u)
            after(memory_slab(0))
            for u in range(4):
                dve.wait_ge(scores_ready, U_ML + u + 1)
                dve.wait_ge(w_ready, u + 1)
                for t, c0, c1 in CAUSAL:
                    ins = V.tensor_tensor_reduce(out=se_s[:, u, c0:c1], in0=ps[:, 4 + u, c0:c1], in1=bias[:, u, c0:c1],
                                                 scale=1.0, scalar=0.0, op0=ALU.mult, op1=ALU.add,
                                                 accum_out=den[:, 4 * t + u:4 * t + u + 1])
                ins.then_inc(p_ready, 1)
            after(memory_slab(1))
            dve.wait_ge(em_ready, 2)
            dve.wait_ge(p_ready, U_ML + 4)
            link(V.scalar_tensor_tensor(den[:, :], den[:, :], -1.0, den[:, :], ALU.mult, ALU.max))
            link(V.tensor_tensor(den[:, :], den[:, :], em[:, :], ALU.max))
            link(V.reciprocal(den[:, :], den[:, :]))
            fx_bias(0)
            after(memory_slab(2))
            fx_masked(0)
            dve.wait_ge(o_ready, O_ML + 2)
            for t in range(TT):
                ins = V.tensor_tensor(ml_y[:, 4 * t:4 * t + 4], ps[:, t, :].rearrange("p (h c) -> p h c", h=4),
                                      along(den[:, 4 * t:4 * t + 4], P), ALU.mult)
            link(ins)
            link(V.tensor_tensor(ml_sq, ml_y, ml_y, ALU.mult))
            V.tensor_reduce(ml_rs[:, :], ml_sq, AX_X, ALU.add).then_inc(ml_var, 1)
            fx_probs(0)
            after(memory_slab(3))
            dve.wait_ge(ml_sd, 1)
            link(V.reciprocal(ml_rs[:, :], ml_rs[:, :]))
            link(V.tensor_tensor(ml_y, ml_y, along(ml_rs[:, :], P), ALU.mult))
            V.tensor_tensor(ml_y, ml_y, ml_o[:, :, :].rearrange("p t (h c) -> p (t h) c", c=P),
                            ALU.mult).then_inc(ml_ready, 1)
            out_low(O_FX, se_o, slice(4, 6))
            fx_bias(1)
            after(memory_slab(4))
            after(memory_slab(5))
            fx_masked(1)
            dve.wait_ge(o_lo_done, O_FX + 1)
            for b in range(2):
                dve.wait_ge(ml_tr, b + 1)
                if b:
                    dve.wait_ge(o_lo_done, O_FX + 2)
                for m in range(2):
                    ins = V.tensor_scalar(se_o[:, m, :], ps[:, b, T * m:T * m + T], pcol("ml_norm_2", 2 * b + m), None, ALU.mult)
                ins.then_inc(ml_fm, 1)
                out_low(O_FX + 1 + b, se_o, slice(2 * b, 2 * b + 2))
            fx_probs(1)
            after(memory_slab(6))
            out_low(O_FX + 3, se_o, slice(6, 8))
            after(memory_slab(7))
            for i in range(3):
                after(first["mix_o"] + i)
            norm(6, x_tm, 1.0, first["mix_o"] + 3, 5)
            after(first["mix_o"] + 3)
            for j in range(4):
                after(first["x_q"] + j)
            link(V.memset(zero_m[:, :], 0.0))
            for u in range(4):
                masked(U_X + u, cr_s, FULL, lambda w, t, c0, c1: zero_m[:, :])
            for u in range(4):
                probs(U_X + u, cr_s, FULL)
            for u in range(4):
                out_low(O_X + u, cr_o, slice(2 * u, 2 * u + 2))
            for i in range(3):
                after(first["x_o"] + i)
            norm(7, x_tm, 1.0, first["x_o"] + 3, 6)
            after(first["x_o"] + 3)
            ffn("ff2")
            norm_tokens(8, x_tm, 1.0, first["ff2"] + 31, 7)
            dve.wait_ge(xn_act, 16)
            dve.wait_ge(xn_dve, 8)
            dve.wait_ge(gain_loaded, 16 * 9)
            for t in range(TT):
                V.tensor_tensor(xn[:, t, :], xn[:, t, :], gain[:, 0, :], ALU.mult).then_inc(final_ready, 1)

        @block.tensor
        def _(pe):
            def three(out, hi_l, lo_l, hi_r, lo_r, start, stop):
                nc.tensor.matmul(out, hi_l, hi_r, start=start, stop=False)
                nc.tensor.matmul(out, hi_l, lo_r, start=False, stop=False)
                return nc.tensor.matmul(out, lo_l, hi_r, start=False, stop=stop)

            def wide_fm(i, hi_x, lo_x, bank, x_first=None):
                wait_slab(pe, i)
                wh, wl = wview(w_hi, i, "wide"), wview(w_lo, i, "wide")
                for m in range(2):
                    for k in range(KT):
                        f = slice(P * m, P * m + P)
                        if x_first is not None and m == 0 and k % 2 == 0:
                            pe.wait_ge(xlo_ready, x_first + k // 2 + 1)
                        last = three(ps[:, bank, T * m:T * m + T], wh[:, k, f], wl[:, k, f], hi_x[:, k, :], lo_x[:, k, :],
                                     k == 0, k == KT - 1)
                last.then_inc(slab_done, 1)

            def wide_tm(i, hi_x, lo_x, bank):
                wait_slab(pe, i)
                wh, wl = wview(w_hi, i, "wide"), wview(w_lo, i, "wide")
                for t in range(TT):
                    for k in range(KT):
                        f = slice(P * t, P * t + P)
                        last = three(ps[:, bank, T * t:T * t + T], hi_x[:, k, f], lo_x[:, k, f], wh[:, k, :], wl[:, k, :],
                                     k == 0, k == KT - 1)
                last.then_inc(slab_done, 1)

            def tall_half(i, hi_x, lo_x, start, stop, t, base=0):
                if t == 0:
                    wait_slab(pe, i)
                wh, wl = wview(w_hi, i, "tall"), wview(w_lo, i, "tall")
                for k in range(2):
                    for n in range(2):
                        f, c = slice(P * t, P * t + P), slice(512 * n, 512 * n + 512)
                        last = three(ps[:, base + 2 * t + n, :], hi_x[:, k, f], lo_x[:, k, f], wh[:, k, c], wl[:, k, c],
                                     start and k == 0, stop and k == 1)
                if t:
                    last.then_inc(slab_done, 1)
                return last

            def tall(i, hi_x, lo_x, start, stop, base=0, signal_half=False):
                for t in range(TT):
                    last = tall_half(i, hi_x, lo_x, start, stop, t, base)
                    if signal_half and t == 0:
                        last.then_inc(half_done, 1)

            mm = nc.tensor.matmul
            fence = chain(pe, pe_step)

            def lora1(w, n, parts, q):
                pe.wait_ge(mixed_ready, q + 1)
                if n == 0:
                    pe.wait_ge(lora1_loaded, 48)
                for bank, lo_c, hi_c in parts:
                    for k in range(KT):
                        last = mm(ps[0:hi_c - lo_c, bank, 0:T], w[:, k, lo_c:hi_c], mixed[:, q % 2, k, :],
                                  start=k == 0, stop=k == KT - 1)
                last.then_inc(lora1_mm, 1)

            pe.wait_ge(mix_lo_done, 1)
            for i in range(4):
                wide_fm(i, rx_hi, rx_lo, i % 4)
            lora1(w1, 0, [(4, 0, LORA)], 2)
            lora1(a1, 1, [(5, 0, LORA)], 3)
            pe.wait_ge(mix_lo_done, 2)
            for i in range(4, 8):
                pe.wait_ge(proj_taken, i - 3)
                wide_fm(i, mix_hi, mix_lo, i % 4)
            lora1(g1, 2, [(6, 0, P), (7, P, GLORA)], 5)
            pe.wait_ge(mix_lo_done, 3)

            def aux_bank(g, k):
                n = aux_at(g, k)
                if n >= 2:
                    pe.wait_ge(aux_taken, n - 1)
                return ps[:, n % 2, :]

            def tok(t):
                return slice(P * t, P * t + P)

            def head(h):
                return slice(HD * (h % 2), HD * (h % 2) + HD), h // 2

            def step(g, k):
                z = aux_bank(g, k)
                d_g, rb_g, ak_g, rk_g = d_m[g % 2], rb_m[g % 2], ak_m[g % 2], rk_m[g % 2]
                v = lambda t, h: v_tm[:, t, 256 * g + HD * h:256 * g + HD * h + HD]
                t = int(k in (A_U1, A_SA1))
                if k in (A_W, A_A):
                    pe.wait_ge(lora2_loaded, 32 * (g + 1))
                    w, src = ((w2, tanh_w), (a2, lora_a))[k == A_A]
                    for m in range(2):
                        last = mm(z[:, T * m:T * m + T], w[:, P * m:P * m + P], src[:, :], start=True, stop=True)
                elif k == A_KK:
                    pe.wait_ge(kk2_ready, g + 1)
                    last = mm(z, rc("headones"), kmod[:, :, :].rearrange("p a b -> p (a b)"), start=True, stop=True)
                elif k == A_BON:
                    pe.wait_ge(rkr_ready, g + 1)
                    for t in range(TT):
                        for m in range(2):
                            last = mm(z[:, 4 * t + 2 * m:4 * t + 2 * m + 2], sw[:, 2 * m + t, :], rk_sel[:, 2 * g + m, :],
                                      start=True, stop=True)
                elif k == A_BK:
                    pe.wait_ge(prep_ready, g + 1)
                    for s, src in ((0, b_t), (1, k_t)):
                        for m in range(2):
                            last = nc.tensor.transpose(z[:, P * (2 * s + m):P * (2 * s + m) + P], src[:, 2 * m, :], ident)
                elif k == A_G:
                    pe.wait_ge(gate_lora_loaded, 64 * (g + 1))
                    for t in range(TT):
                        mm(z[:, T * t:T * t + T], sig_g[:, tok(t)], g2[:, :], start=True, stop=False)
                        last = mm(z[:, T * t:T * t + T], sig_g2[:, tok(t)], g2b[:, :], start=False, stop=True)
                elif k in (A_U0, A_U1):
                    for s, h in enumerate(HEADS):
                        q, m = head(h)
                        o = z[:, HD * h:HD * h + HD]
                        if t:
                            if s == 0:
                                pe.wait_ge(aux_taken, aux_at(g, A_ST) + 1)
                            if s == 2:
                                fence(last)
                            mm(o, ar[q, 2 * g + m, t, 0, :], state[q, m, :], start=True, stop=False)
                        last = mm(o, ak_g[:, t, s], v(t, h), start=not t, stop=True)
                elif k in (A_SA0, A_SA1):
                    pe.wait_ge(aux_taken, aux_at(g, A_U1 if t else A_U0) + 1)
                    pe.wait_ge(inv_taken[t], INV * (g + 1))
                    for s, h in enumerate(HEADS):
                        last = mm(z[:, HD * h:HD * h + HD], d_g[:, t, s], u_m[:, HD * h:HD * h + HD], start=True, stop=True)
                elif k == A_ST:
                    pe.wait_ge(aux_taken, aux_at(g, A_SA0) + 1)
                    for h in range(4):
                        q, m = head(h)
                        o = z[q, HD * m:HD * m + HD]
                        mm(o, bk_tm[:, g % 2, 0, m, q], sa_m[:, 0, HD * h:HD * h + HD], start=True, stop=False)
                        last = mm(o, bk_tm[:, g % 2, 1, m, q], v(0, h), start=False, stop=True)
                elif k == A_Y:
                    pe.wait_ge(aux_taken, aux_at(g, A_SA1) + 1)
                    for t in range(TT):
                        for s, h in enumerate(HEADS):
                            q, m = head(h)
                            if t and s in (0, 2):
                                fence(last)
                            o = z[:, 256 * t + HD * h:256 * t + HD * h + HD]
                            if t:
                                mm(o, ar[q, 2 * g + m, t, 1, :], state[q, m, :], start=True, stop=False)
                            mm(o, rb_g[:, t, s], sa_m[:, t, HD * h:HD * h + HD], start=not t, stop=False)
                            last = mm(o, rk_g[:, t, s], v(t, h), start=False, stop=True)
                else:
                    pe.wait_ge(y_ready, g + 1)
                    y2 = y_sb[:, :, :].rearrange("p (t h) c -> p t (h c)", t=TT)
                    for m in range(2):
                        for t in range(TT):
                            last = nc.tensor.transpose(z[:, T * m + P * t:T * m + P * t + P], y2[:, t, P * m:P * m + P], ident)
                last.then_inc(aux_ready, 1)

            for i in range(8, 12):
                pe.wait_ge(proj_taken, i - 1)
                wide_tm(i, rx_hi, rx_lo, v_bank(i))
                if i == 8:
                    pe.wait_ge(proj_taken, 6)
                    pe.wait_ge(lora1_out, 4)
                    pe.wait_ge(consts_loaded, 32)
                    for k in (A_W, A_A, A_KK):
                        step(0, k)
                elif i == 10:
                    step(0, A_BON)
            pe.wait_ge(lora1_out, 4)
            step(0, A_BK)
            for g in range(4):
                pe.wait_ge(a_ready, g + 1)
                pe.wait_ge(prep_ready, g + 1)
                if g == 0:
                    pe.wait_ge(proj_taken, 12)
                for t in range(TT):
                    if g:
                        pe.wait_ge(inv_taken[t], INV * g)
                    for s, h in enumerate(HEADS):
                        q, m = head(h)
                        last = mm(ps[:, 2 + 3 * t + s // 2, 256 * (s % 2):256 * (s % 2) + 256], b_t[q, 2 * m + t, :],
                                  ar[q, 2 * g + m, t, :, :].rearrange("p s c -> p (s c)"), start=True, stop=True)
                    last.then_inc(inv_ready[t], 1)
                for half in range(2):
                    for t in range(TT):
                        for s in (2 * half, 2 * half + 1):
                            q, m = head(HEADS[s])
                            last = mm(ps[:, 4 + 3 * t, P * s:P * s + P], ar[q, 2 * g + m, t, 0, :], b_t[q, 2 * m + t, :],
                                      start=True, stop=True)
                        if half:
                            last.then_inc(inv_ready[t], 1)
                    if not half:
                        fence(last)
                for t in range(TT):
                    pe.wait_ge(inv_taken[t], INV * g + 1)
                    for s, h in enumerate(HEADS):
                        q, m = head(h)
                        last = mm(ps[:, 2 + 3 * t + s // 2, 256 * (s % 2):256 * (s % 2) + 256], k_t[q, 2 * m + t, :],
                                  ar[q, 2 * g + m, t, :, :].rearrange("p s c -> p (s c)"), start=True, stop=True)
                    last.then_inc(inv_ready[t], 1)
                for slot in range(12):
                    n = slot // 2 + 1
                    for t in range(TT):
                        pe.wait_ge(inv_taken[t], INV * g + 2 + slot)
                        if slot == 0:
                            pe.wait_ge(nt_taken[t], g + 1)
                        for h in range(4):
                            if slot % 2 == 0:
                                last = mm(ps[:, 2 + 3 * t, P * h:P * h + P], nt_m[:, t, h], d_m[g % 2][:, t, h],
                                          start=True, stop=True)
                            else:
                                if n < NL - 1:
                                    mm(ps[:, 4 + 3 * t, P * h:P * h + P], w_m[:, t, h], dt_m[:, t, h], start=True, stop=True)
                                last = mm(ps[:, 3 + 3 * t, P * h:P * h + P], dt_m[:, t, h], w_m[:, t, h],
                                          start=True, stop=True)
                        last.then_inc(inv_ready[t], 1)
                    for n, k in slot_steps(g, slot):
                        step(n, k)
            def out_part(i, t):
                tall_half(first["rwkv_o"] + i, mix_hi[:, 2 * i:2 * i + 2, :], mix_lo[:, 2 * i:2 * i + 2, :], i == 0, False, t, 4)

            halves = [(i, t) for i in range(3) for t in range(TT)]
            for n, k in tail_steps:
                step(n, k)
                if n == 3 and k in (A_ST, A_U1, A_SA1, A_Y):
                    if k == A_ST:
                        pe.wait_ge(rwkv_lo_done, 3)
                        pe.wait_ge(inv_taken[1], INV * 4)
                    for i, t in (halves if k == A_Y else halves[:1]):
                        out_part(i, t)
                    halves = halves[1:]
            pe.wait_ge(rwkv_lo_done, 4)
            tall(first["rwkv_o"] + 3, mix_hi[:, 6:8, :], mix_lo[:, 6:8, :], False, True, 4, signal_half=True)
            def transposes(q):
                n = FM_NORMS.index(q)
                for t in range(TT):
                    pe.wait_ge(xn_act, 2 * n + t + 1)
                    if t:
                        pe.wait_ge(xn_dve, n + 1)
                    for i in range(4):
                        for m in range(2):
                            k = 2 * i + m
                            last = nc.tensor.transpose(ps[:, 4 + i, T * m + P * t:T * m + P * t + P],
                                                       xn[:, t, P * k:P * k + P], ident)
                        if t:
                            last.then_inc(tr_ready, 1)

            def product(section, ready, count):
                pe.wait_ge(ready, count)
                for i in range(4):
                    tall(first[section] + i, mix_hi[:, 2 * i:2 * i + 2, :], mix_lo[:, 2 * i:2 * i + 2, :], i == 0, i == 3,
                         signal_half=i == 3)

            def ffn(name, q):
                s0, n, h0 = FFN[name]
                first_use = 4 * FM_NORMS.index(q)
                for j in range(n + 1):
                    up, down = ffn_slabs(name, j)
                    if j < n:
                        if h0 + j >= 2:
                            pe.wait_ge(ffn_taken, h0 + j - 1)
                        for m, i in enumerate(up):
                            wide_fm(i, x_hi, x_lo, 4 + 2 * (j % 2) + m, first_use if j == 0 and m == 0 else None)
                    if j:
                        pe.wait_ge(hid_ready, h0 + j)
                        view = lambda w: w[:, (j - 1) % 3, :].rearrange("p (k n) -> p k n", k=2)
                        tall(down, view(hid_hi), view(hid_lo), j == 1, j == n, signal_half=j == n)

            def project(n, i, wide):
                if n >= 3:
                    pe.wait_ge(p_taken, max(n - 2, P_FIRST["x_q"]) if n >= P_FIRST["x_q"] else n - 2)
                wide(i, x_hi, x_lo, n % 3)

            def p_transposes(u, s, kind):
                pe.wait_ge(p_ready, u + 1)
                for n, (c0, tq, tk) in enumerate(BLOCKS[kind]):
                    at = (0 if tk == 0 else (P if kind == "causal" else T)) + P * tq if kind == "full" else P * n
                    last = nc.tensor.transpose(ps[:, 4 + u % 4, at:at + P], s[:, u % 4, c0:c0 + P], ident)
                last.then_inc(pt_ready, 1)

            pe.wait_ge(rwkv_lo_done, 1)
            transposes(0)
            ffn("ffn0", 0)
            transposes(1)
            pe.wait_ge(xlo_ready, 8)
            pe.wait_ge(late_loaded, 80)
            def rotate(g):
                if g > 1:
                    pe.wait_ge(o_taken, g - 1)
                for n, src in enumerate((ma_q, ma_k)):
                    if n or g:
                        pe.wait_ge(rope_done, 2 * g + n)
                    pe.wait_ge(p_taken, 3 * g + n + 1)
                    mm(ps[:, 3, :], rope_c[:, 2 * T:2 * T + P], src[:, :, :].rearrange("p a b -> p (a b)"),
                       start=True, stop=True).then_inc(rot_ready, 1)

            for g in range(-1, 4):
                if g >= 0:
                    pe.wait_ge(rope_done, 2 * g + 2)
                    if g:
                        pe.wait_ge(pt_taken, 4 * g)
                    for s, h in enumerate(HEADS):
                        q, m = head(h)
                        for t, c0, c1 in CAUSAL:
                            last = mm(ps[:, 4 + s, c0:c1], ma_q2[q, m, tok(t)], ma_k2[q, m, 0:c1 - c0], start=True, stop=True)
                        last.then_inc(scores_ready, 1)
                if g < 3:
                    n = 3 * (g + 1)
                    for j in range(2):
                        project(n + j, first["qkv"] + n + j, wide_fm)
                    rotate(g + 1)
                    project(n + 2, first["qkv"] + n + 2, wide_tm)
                if g >= 0:
                    for s in range(4):
                        p_transposes(U_MOBA + 4 * g + s, ma_s, "causal")
                    if g < 3:
                        pe.wait_ge(rope_done, 2 * g + 4)
                    for s, h in enumerate(HEADS):
                        q, m = head(h)
                        pe.wait_ge(pt_taken, 4 * g + s + 1)
                        v = lambda t: ma_vv[:, g % 2, t, HD * h:HD * h + HD]
                        mm(ps[q, 3, T * m:T * m + T], v(0), ma_p[:, s, 0:T], start=True, stop=False)
                        last = mm(ps[q, 3, T * m + P:T * m + T], v(1), ma_p[:, s, T:T + P], start=False, stop=True)
                    last.then_inc(o_ready, 1)
            product("moba_o", o_lo_done, 4)
            transposes(2)
            ffn("ffn1", 2)
            transposes(4)
            pe.wait_ge(xlo_ready, 16)
            pe.wait_ge(late_loaded, 80)
            for k in range(KT):
                mm(ps[0:12, 3, 0:T], gate_w[:, k, 0:12], x_fm[:, k, :], start=k == 0, stop=k == KT - 1)
            for k in range(KT):
                last = mm(ps[0:4, 3, T:2 * T], gate_w[:, k, 12:16], x_fm[:, k, :], start=k == 0, stop=k == KT - 1)
            last.then_inc(gate_mm, 1)
            for name, n, kind in (("ml_qk", 4, wide_fm), ("ml_v", 2, wide_tm), ("ml_o", 2, wide_tm),
                                  ("fx_qk", 4, wide_fm), ("fx_v", 2, wide_tm)):
                for j in range(n):
                    project(P_FIRST[name] + j, first[name] + j, kind)
                if name == "ml_v":
                    transposes(5)
            pe.wait_ge(gate_rows, 1)
            for t in range(TT):
                last = nc.tensor.transpose(ps[:, 3, HD * t:HD * t + HD], gst[:, tok(t)], ident[0:HD, 0:HD])
            last.then_inc(gate_tr, 1)

            def memory_product(n):
                pe.wait_ge(p_taken, P_FIRST["x_k"] + n)
                (wide_tm if n >= 4 else wide_fm)(memory_slab(n), x_hi, x_lo, 2)

            def row(n):
                if n:
                    pe.wait_ge(row_taken, n)
                else:
                    pe.wait_ge(gate_cols, 1)
                r, src = (4, gi) if n < 4 else (12, gst)
                mm(ps[:, 3, 0:T], gsel[0:r, P * n:P * n + P], src[0:r, :], start=True, stop=True).then_inc(row_ready, 1)

            def fx_rows(g):
                if g:
                    pe.wait_ge(o_taken, O_FX + 1)
                for u in range(4):
                    row(4 + 4 * g + u)
                    if u == 1:
                        memory_product(3 + 2 * g)

            def fx_scores(g):
                pe.wait_ge(pt_taken, U_FX + 4 * g)
                for s, h in enumerate(HEADS):
                    q, m = head(h)
                    for t, c0, c1 in CAUSAL:
                        last = mm(ps[:, 4 + s, c0:c1], fx_q[q, 2 * g + m, tok(t)], fx_k[q, 2 * g + m, 0:c1 - c0],
                                  start=True, stop=True)
                    last.then_inc(scores_ready, 1)

            def fx_outputs(g):
                for s in range(4):
                    p_transposes(U_FX + 4 * g + s, se_s, "causal")
                pe.wait_ge(row_taken, 8 + 4 * g)
                for s, h in enumerate(HEADS):
                    q, m = head(h)
                    pe.wait_ge(pt_taken, U_FX + 4 * g + s + 1)
                    v = lambda t: fx_v[:, t, 256 * g + HD * h:256 * g + HD * h + HD]
                    mm(ps[q, 3, T * m:T * m + T], v(0), se_p[:, s, 0:T], start=True, stop=False)
                    last = mm(ps[q, 3, T * m + P:T * m + T], v(1), se_p[:, s, T:T + P], start=False, stop=True)
                last.then_inc(o_ready, 1)

            for u in range(4):
                row(u)
                if u == 0:
                    pe.wait_ge(xlo_ready, 20)
                    memory_product(0)
            pe.wait_ge(silu_ready, 1)
            pe.wait_ge(p_taken, P_FIRST["fx_v"] + 2)
            for u in range(4):
                for t, c0, c1 in CAUSAL:
                    last = mm(ps[:, 4 + u, c0:c1], conv_out[:, u, tok(t)], conv_out[:, 4 + u, 0:c1 - c0], start=True, stop=True)
                last.then_inc(scores_ready, 1)
            memory_product(1)
            for u in range(4):
                p_transposes(U_ML + u, se_s, "causal")
            memory_product(2)
            for t in range(TT):
                for u in range(4):
                    pe.wait_ge(pt_taken, U_ML + u + 1)
                    v = lambda tk: ml_v[:, tk, P * u:P * u + P]
                    o = ps[:, t, P * u:P * u + P]
                    last = mm(o, se_p[:, u, P * t:P * t + P], v(0), start=True, stop=not t)
                    if t:
                        last = mm(o, se_p[:, u, T:T + P], v(1), start=False, stop=True)
                last.then_inc(o_ready, 1)
            fx_rows(0)
            fx_scores(0)
            memory_product(4)
            fx_outputs(0)
            fx_rows(1)
            fx_scores(1)
            pe.wait_ge(ml_ready, 1)
            for b in range(2):
                for m in range(2):
                    for t in range(TT):
                        last = nc.tensor.transpose(ps[:, b, T * m + P * t:T * m + P * t + P],
                                                   ml_y[:, 4 * t + 2 * b + m, :], ident)
                last.then_inc(ml_tr, 1)
            memory_product(6)
            fx_outputs(1)
            memory_product(7)
            pe.wait_ge(p_taken, P_FIRST["x_q"])
            product("mix_o", o_lo_done, 8)
            transposes(6)
            pe.wait_ge(xlo_ready, 24)
            for j in range(4):
                project(P_FIRST["x_q"] + j, first["x_q"] + j, wide_fm)
            pe.wait_ge(p_taken, P_FIRST["x_q"] + 4)
            for u in range(4):
                for t in range(TT):
                    for k in range(2):
                        last = mm(ps[:, 4 + u, T * t:T * t + T], xq_fm[:, 2 * u + k, tok(t)], xk_fm[:, 2 * u + k, 0:T],
                                  start=k == 0, stop=k == 1)
                last.then_inc(scores_ready, 1)
            for u in range(4):
                p_transposes(U_X + u, cr_s, "full")
            for u in range(4):
                pe.wait_ge(pt_taken, U_X + u + 1)
                for m in range(2):
                    for tk in range(TT):
                        last = mm(ps[:, u, T * m:T * m + T], gain[:, tk, T * u + P * m:T * u + P * m + P],
                                  cr_p[:, u, T * tk:T * tk + T], start=tk == 0, stop=tk == 1)
                last.then_inc(o_ready, 1)
            product("x_o", o_lo_done, 12)
            transposes(7)
            ffn("ff2", 7)


def lay_out(inputs):
    a = {k: np.ascontiguousarray(v) for k, v in inputs.items()}
    plan, _ = weight_plan()
    slabs = np.empty((len(plan), P, SLAB), np.float32)
    for i, (kind, src, layer, r0, c0) in enumerate(plan):
        w = a[src]
        w = w.reshape((-1,) + w.shape[-2:])[layer]
        if kind == "wide":
            slabs[i] = w[:, c0:c0 + 256].reshape(KT, P, 256).transpose(1, 0, 2).reshape(P, SLAB)
        else:
            slabs[i] = w[P * r0:P * (r0 + 2)].reshape(2, P, C).transpose(1, 0, 2).reshape(P, SLAB)
    tokens = lambda x: np.ascontiguousarray(x.reshape(TT, P, C).transpose(1, 0, 2))
    features = lambda w: np.ascontiguousarray(w.reshape(-1, P, w.shape[-1]).transpose(1, 0, 2))
    cols = {}
    for name, n in PARAMS:
        cols[name] = a[name].reshape(n, P).T
    table = constants()
    out = {
        "weights": slabs,
        "x": tokens(a["x"]),
        "xT": features(np.ascontiguousarray(a["x"][0].T)),
        "mem": tokens(a["mem_2"]),
        "params": np.ascontiguousarray(np.concatenate([cols[n] for n, _ in PARAMS], axis=1)),
        "w1": features(a["rwkv_w1"][0]), "a1": features(a["rwkv_a1"][0]), "g1": features(a["rwkv_g1"][0]),
        "w2": a["rwkv_w2"][0], "a2": a["rwkv_a2"][0], "g2": a["rwkv_g2"][0],
        "gn_g": a["rwkv_gn_g"], "gn_b": a["rwkv_gn_b"],
        "mix_g": a["ln_mix_g"], "mix_b": a["ln_mix_b"], "ffn_g": a["ln_ffn_g"], "ffn_b": a["ln_ffn_b"],
        "final_g": a["ln_f_2"].reshape(1, C),
        "gate_w": features(np.concatenate([a["w_in_2"][0][:, 2052:2056], a["w_in_2"][0][:, 3592:3600],
                                           a["w_in_2"][0][:, 2048:2052]], axis=1)),
        "gate_b": np.concatenate([a["ml_b_f_2"][0], a["fx_b_f_2"][0], a["ml_b_i_2"][0]]).reshape(16, 1),
    }
    for which, names in CONST_SETS.items():
        out["const_" + which] = np.ascontiguousarray(np.concatenate([table[n] for n in names], axis=1))
    return out


def kernel(**inputs):
    import concourse.bacc as bacc
    from concourse.bass_utils import run_bass_kernel_spmd

    nc = bacc.Bacc("TRN2", target_bir_lowering=False, num_devices=1)
    arrays = lay_out(inputs)
    d = {k: nc.dram_tensor("in_" + k, v.shape, F32, kind="ExternalInput").ap() for k, v in arrays.items()}
    out = nc.dram_tensor("out", (P, TT, C), F32, kind="ExternalOutput").ap()
    build(nc, d, out)
    r = run_bass_kernel_spmd(nc, [{"in_" + k: v for k, v in arrays.items()}], core_ids=[0])
    got = r.results[0]["out"]
    return np.ascontiguousarray(got.transpose(1, 0, 2)).reshape(1, T, C)
```

```python
from contextlib import ExitStack

import numpy as np

import concourse.bass as bass
from concourse import mybir

F32 = mybir.dt.float32
F32R = mybir.dt.float32r
ALU = mybir.AluOpType
ACT = mybir.ActivationFunctionType
AX_X = mybir.AxisListType.X

P = 128
T = 256
TT = T // P
C = 1024
KT = C // P
HD = 64
NEG = -1.0e30
SLAB = 2048
RAW = 3
WS = 3
ALPHA = (2 * 2) ** 0.25
LN_EPS = 1e-5
GN_EPS = HD * 1e-5
RMS_EPS = 1e-6
DECAY = float(np.exp(-0.5))
LORA = 64
GLORA = 160
D_FF = 2816
D_FF2 = 4096
NL = 7


def constants():
    i = np.arange(P)[:, None]
    j = np.arange(P)[None, :]
    c = {}
    c["ident"] = i == j
    c["headones"] = i // HD == j // HD
    c["strict"] = i < j
    c["incl"] = i <= j
    for n in range(NL):
        s = 1 << n
        c[f"level{n}"] = (i // (2 * s) == j // (2 * s)) & (i // s < j // s)
    c["level0T"] = (i // 2 == j // 2) & (i > j)
    c["reset"] = np.broadcast_to(np.arange(2 * T)[None, :] % P != 0, (P, 2 * T))
    c["headsel"] = i // HD == np.arange(2)[None, :]
    inv = np.float32(10000.0) ** (-np.arange(0, HD, 2, dtype=np.float32) / np.float32(HD))
    ang = np.arange(T, dtype=np.float32)[:, None] * inv[None, :]
    f = np.arange(P) % (HD // 2)
    c["cos"] = np.cos(ang).T[f]
    c["sin"] = np.sin(ang).T[f]
    rot = np.zeros((P, P), np.float32)
    for m in range(P):
        if m % HD < HD // 2:
            rot[m + HD // 2, m] = -1.0
        else:
            rot[m - HD // 2, m] = 1.0
    c["rot"] = rot
    low = np.where(j <= i, 0.0, NEG)
    c["causal"] = np.concatenate([low, np.zeros((P, P)), low], axis=1)
    c["gatesel"] = np.concatenate([np.broadcast_to(i == h, (P, P)) for h in range(12)], axis=1)
    return {k: np.ascontiguousarray(v, dtype=np.float32) for k, v in c.items()}




def weight_plan():
    plan, start = [], {}

    def section(name, slabs):
        start[name] = len(plan)
        plan.extend(slabs)

    def wide(src, layer, c0, n):
        return [("wide", src, layer, 0, c0 + 256 * i) for i in range(n)]

    def tall(src, layer, n):
        return [("tall", src, layer, 2 * i, 0) for i in range(n)]

    section("rkv", [s for n in range(3) for s in wide("rwkv_w_rkv", n, 0, 4)])
    section("rwkv_o", tall("rwkv_w_o", 0, 4))
    for layer in range(2):
        slabs = []
        for j in range(D_FF // 256 + 1):
            if j < D_FF // 256:
                slabs += wide("ffn_w_in", layer, 256 * j, 1) + wide("ffn_w_in", layer, D_FF + 256 * j, 1)
            if j:
                slabs.append(("tall", "ffn_w_down", layer, 2 * (j - 1), 0))
        if layer == 1:
            section("qkv", [wide("moba_w_qkv", 0, n * C + 256 * g, 1)[0] for g in range(4) for n in range(3)])
            section("moba_o", tall("moba_w_o", 0, 4))
        section(f"ffn{layer}", slabs)
    section("ml_qk", wide("w_in_2", 0, 0, 4))
    section("ml_v", wide("w_in_2", 0, 1024, 2))
    section("ml_o", wide("w_in_2", 0, 1536, 2))
    section("fx_qk", wide("w_in_2", 0, 2056, 4))
    section("fx_v", wide("w_in_2", 0, 3080, 2))
    section("x_k", wide("w_xkv_2", 0, 0, 4))
    section("x_v", wide("w_xkv_2", 0, C, 4))
    section("mix_o", tall("w_out_2", 0, 4))
    section("x_q", wide("w_xq_2", 0, 0, 4))
    section("x_o", tall("w_xo_2", 0, 4))
    slabs = []
    for j in range(D_FF2 // 256 + 1):
        if j < D_FF2 // 256:
            slabs += wide("w_ff1_2", 0, 256 * j, 1)
        if j:
            slabs.append(("tall", "w_ff2_2", 0, 2 * (j - 1), 0))
    section("ff2", slabs)
    return plan, start


PARAMS = [("rwkv_mu", 6 * KT), ("rwkv_w0", KT), ("rwkv_a0", KT), ("rwkv_k_k", KT), ("rwkv_k_a", KT),
          ("rwkv_r_k", KT), ("ln_mix_g", 2 * KT), ("ln_mix_b", 2 * KT), ("ln_ffn_g", 2 * KT), ("ln_ffn_b", 2 * KT),
          ("ln1_2", KT), ("ln_x_2", KT), ("ln_mem_2", KT), ("ln2_2", KT), ("ml_conv_w_2", 4 * KT),
          ("ml_conv_b_2", KT), ("ml_norm_2", 4)]
PCOL = {}
for _name, _n in PARAMS:
    PCOL[_name] = sum(n for _, n in PARAMS[:len(PCOL)])
N_PARAMS = sum(n for _, n in PARAMS)
CONST_SETS = {
    "base": ["ident", "causal"],
    "rwkv": ["headones", "strict", "incl"] + [f"level{n}" for n in range(NL)] + ["level0T", "reset", "headsel"],
    "rope": ["cos", "sin", "rot"],
    "gates": ["gatesel"],
}


def const_columns(which):
    at, out = 0, {}
    table = constants()
    for name in CONST_SETS[which]:
        out[name] = (at, table[name].shape[1])
        at += table[name].shape[1]
    return out, at


def over(ap, n):
    return ap.unsqueeze(1).broadcast_to([ap.shape[0], n, ap.shape[1]])


def along(ap, n):
    return ap.unsqueeze(2).broadcast_to([ap.shape[0], ap.shape[1], n])


def build(nc, d, out):
    plan, first = weight_plan()
    n_slabs = len(plan)

    with ExitStack() as ctx:
        def sb(name, shape, dt=F32, where=None):
            return (where or ctx).enter_context(nc.sbuf_tensor(name, shape, dt))

        def sem(name):
            return ctx.enter_context(nc.semaphore(name))

        ps = ctx.enter_context(nc.psum_tensor("ps", [P, 8, 512], F32))

        w_raw = sb("w_raw", [P, RAW, SLAB])
        w_hi = sb("w_hi", [P, WS, SLAB], F32R)
        w_lo = sb("w_lo", [P, WS, SLAB], F32R)
        x_tm = sb("x_tm", [P, TT, C])
        mix_hi = sb("mix_hi", [P, KT, T], F32R)
        mix_lo = sb("mix_lo", [P, KT, T], F32R)
        cols_b, n_b = const_columns("base")
        base_c = sb("base_c", [P, n_b])
        par = sb("par", [P, N_PARAMS])
        stats = sb("stats", [P, TT, 2, 6])
        mv = sb("mv", [P, TT, 2])
        sd = sb("sd", [P, TT])
        rstd = sb("rstd", [P, TT])
        shift = sb("shift", [P, TT])
        square = sb("square", [P, TT])
        eps_c = sb("eps_c", [P, 3])
        mx = sb("mx", [P, 8])
        sm = sb("sm", [P, 8])
        rs = sb("rs", [P, 8])
        ident = base_c[:, 0:P]
        causal = base_c[:, P:4 * P]

        with ExitStack() as a_rw:
            ar = sb("ar", [P, KT, TT, 2, P], where=a_rw)
            k_fm, r_fm = (ar[:, :, :, n, :].rearrange("p a t c -> p (a t) c") for n in range(2))
            rk_sel = sb("rk_sel", [P, KT, 2], where=a_rw)
            v_tm = sb("v_tm", [P, TT, C], where=a_rw)
            cols_r, n_r = const_columns("rwkv")
            rw_c = sb("rw_c", [P, n_r], where=a_rw)
            tanh_w = sb("tanh_w", [LORA, T], where=a_rw)
            lora_a = sb("lora_a", [LORA, T], where=a_rw)
            sig_g = sb("sig_g", [P, T], where=a_rw)
            sig_g2 = sb("sig_g2", [GLORA - P, T], where=a_rw)
            with ExitStack() as a:
                rx_hi = sb("rx_hi", [P, KT, T], F32R, a)
                rx_lo = sb("rx_lo", [P, KT, T], F32R, a)
                xt = sb("xt", [P, KT, T], where=a)
                xx = sb("xx", [P, KT, T], where=a)
                mixed = sb("mixed", [P, 2, KT, T], where=a)
                w1 = sb("w1", [P, KT, LORA], where=a)
                a1 = sb("a1", [P, KT, LORA], where=a)
                g1 = sb("g1", [P, KT, GLORA], where=a)
            with ExitStack() as a:
                w_m, nt_m, dt_m, d_a = (sb(n, [P, TT, 4, P], where=a) for n in ("w_m", "nt_m", "dt_m", "d_a"))
                w2 = sb("w2", [LORA, 256], where=a)
                a2 = sb("a2", [LORA, 256], where=a)
                g2 = sb("g2", [P, 256], where=a)
                g2b = sb("g2b", [GLORA - P, 256], where=a)
                gn_g = sb("gn_g", [P, 256], where=a)
                gn_b = sb("gn_b", [P, 256], where=a)
                sw, av, kk, cum, cprev, e_pos, e_neg, kmod, norm_k, b_t, k_t = (
                    sb(n, [P, 4, P], where=a) for n in
                    ("sw", "av", "kk", "cum", "cprev", "e_pos", "e_neg", "kmod", "norm_k", "b_t", "k_t"))
                bk_tm = sb("bk_tm", [P, 2, 2, 2, P], where=a)
                d_b, rb_a, rb_b, ak_a, rk_a = (sb(n, [P, TT, 4, P], where=a) for n in
                                               ("d_b", "rb_a", "rb_b", "ak_a", "rk_a"))
                u_m = sb("u_m", [P, 256], where=a)
                sa_m = sb("sa_m", [P, TT, 256], where=a)
                state = sb("state", [P, 2, HD], where=a)
                smid = sb("smid", [P, 4], where=a)
                sdec = sb("sdec", [P, 4, 2], where=a)
                bon = sb("bon", [P, 4, TT * 4], where=a)
                ymean, yvar, ysd, yrs = (sb(n, [P, TT * 4], where=a) for n in ("ymean", "yvar", "ysd", "yrs"))
            g_sb, y_sq, y_fm, y_sb = (w_raw[:, RAW - 1, 512 * n:512 * n + 512].rearrange("p (a b) -> p a b", a=m)
                                for n, m in ((0, TT), (1, TT * 4), (2, 2), (3, TT * 4)))
            four = lambda n: x_tm[:, n, :].rearrange("p (t h c) -> p t h c", t=TT, h=4)
            d_m, rb_m, ak_m, rk_m = (d_a, d_b), (rb_a, rb_b), (four(0), ak_a), (four(1), rk_a)

        def rc(name, lo=0, n=None):
            at, m = cols_r[name]
            return rw_c[:, at + lo:at + (n or m)]

        a_m = ctx.enter_context(ExitStack())
        x_hi = sb("x_hi", [P, KT, T], F32R, a_m)
        x_lo = sb("x_lo", [P, KT, T], F32R, a_m)
        xn = sb("xn", [P, TT, C], where=a_m)
        x_fm = sb("x_fm", [P, KT, T], where=a_m)
        gain = sb("gain", [P, 2, C], where=a_m)
        xk_fm = sb("xk_fm", [P, KT, T + 3], where=a_m)
        conv_in = xk_fm
        gsel = sb("gsel", [P, 12 * P], where=a_m)
        gate_w = sb("gate_w", [P, KT, 16], where=a_m)
        gate_bf = sb("gate_bf", [12, 1], where=a_m)
        gate_bi = sb("gate_bi", [4, 1], where=a_m)
        with ExitStack() as a:
            hid = sb("hid", [P, 2, 512], where=a)
            act_f = sb("act_f", [P, 2, 512], where=a)
            hid_hi = sb("hid_hi", [P, 2, 512], F32R, a)
            hid_lo = sb("hid_lo", [P, 2, 512], F32R, a)

        with ExitStack() as a:
            ma_q, ma_k, ma_q2, ma_k2, rt = (sb(n, [P, 2, T], where=a) for n in
                                                  ("ma_q", "ma_k", "ma_q2", "ma_k2", "rt"))
            ma_vv = sb("ma_vv", [P, 2, TT, 256], where=a)
            ma_s = sb("ma_s", [P, 4, 3 * P], where=a)
            ma_p = sb("ma_p", [P, 4, 3 * P], where=a)
            ma_o = sb("ma_o", [P, 2, T], where=a)
            rope_c = sb("rope_c", [P, 2 * T + P], where=a)
        with ExitStack() as a:
            conv_out = sb("conv_out", [P, KT, T], where=a)
            ml_v = sb("ml_v", [P, TT, 512], where=a)
            ml_o = sb("ml_o", [P, TT, 512], where=a)
            fx_q = sb("fx_q", [P, 4, T], where=a)
            fx_k = sb("fx_k", [P, 4, T], where=a)
            fx_v = sb("fx_v", [P, TT, 512], where=a)
            se_s = sb("se_s", [P, 4, 3 * P], where=a)
            se_p = sb("se_p", [P, 4, 3 * P], where=a)
            bias = sb("bias", [P, 4, 3 * P], where=a)
            zf, za, ones_t, gi = (sb(n, [12, T], where=a) for n in ("zf", "za", "ones_t", "gi"))
            gst = sb("gst", [HD, T], where=a)
            tc = sb("tc", [P, TT, HD], where=a)
            em = sb("em", [P, 8], where=a)
            den = sb("den", [P, 8], where=a)
            ml_rs = sb("ml_rs", [P, 8], where=a)
            se_o = sb("se_o", [P, 2, T], where=a)
            ml_y = x_fm[:, 0:4, :].rearrange("p a (b c) -> p (a b) c", c=P)
            ml_sq = x_fm[:, 4:8, :].rearrange("p a (b c) -> p (a b) c", c=P)
        with ExitStack() as a:
            xq_fm = sb("xq_fm", [P, KT, T], where=a)
            cr_s = sb("cr_s", [P, 4, 512], where=a)
            cr_p = sb("cr_p", [P, 4, 512], where=a)
            cr_o = sb("cr_o", [P, 2, T], where=a)
            zero_m = sb("zero_m", [P, T], where=a)

        raw_loaded = [sem(f"raw_loaded{i}") for i in range(RAW)]
        hi_done, lo_dve, lo_pool, slab_done = sem("hi_done"), sem("lo_dve"), sem("lo_pool"), sem("slab_done")
        dve_step, act_step, pool_step = sem("dve_step"), sem("act_step"), sem("pool_step")
        consts_loaded, par_loaded, x_loaded, xt_loaded = (
            sem("consts_loaded"), sem("par_loaded"), sem("x_loaded"), [sem("xt_loaded0"), sem("xt_loaded1")])
        lora1_loaded, lora2_loaded = sem("lora1_loaded"), sem("lora2_loaded")
        out_stored = sem("out_stored")

        def lo_engine(i):
            return ("dve", i // 2 + 1) if i % 2 == 0 else ("pool", i // 2 + 1)

        def wait_slab(eng, i, r=0, per=0):
            who, n = lo_engine(i)
            eng.wait_ge(lo_dve if who == "dve" else lo_pool, n + r * (per // 2))

        def wview(w, i, kind):
            v = w[:, i % WS, :]
            return v.rearrange("p (k n) -> p k n", k=8 if kind == "wide" else 2)

        pe_step = sem("pe_step")
        HEADS = [0, 2, 1, 3]
        mixed_ready = sem("mixed_ready")
        mix_hi_done, mix_lo_done = sem("mix_hi_done"), sem("mix_lo_done")
        lora1_mm, lora1_out = sem("lora1_mm"), sem("lora1_out")
        proj_taken = sem("proj_taken")
        aux_ready, aux_taken = sem("aux_ready"), sem("aux_taken")
        kk2_ready, rkr_ready, cum_ready, exp_done, prep_ready = (
            sem(n) for n in ("kk2_ready", "rkr_ready", "cum_ready", "exp_done", "prep_ready"))
        inv_ready = [sem(f"inv_ready{t}") for t in range(TT)]
        inv_taken = [sem(f"inv_taken{t}") for t in range(TT)]
        nt_taken = [sem(f"nt_taken{t}") for t in range(TT)]
        yvar_ready, ysd_ready, y_ready, rwkv_lo_done = (
            sem(n) for n in ("yvar_ready", "ysd_ready", "y_ready", "rwkv_lo_done"))
        bonus_ready = sem("bonus_ready")
        gate_lora_loaded, cprev_ready, kmod_ready, kk_ready, a_ready, ymean_ready, ysq_ready, yrs_ready = (
            sem(n) for n in ("gate_lora_loaded", "cprev_ready", "kmod_ready", "kk_ready", "a_ready", "ymean_ready",
                             "ysq_ready", "yrs_ready"))
        (A_W, A_A, A_KK, A_BON, A_BK, A_U0, A_SA0, A_ST, A_U1, A_SA1, A_Y, A_G, A_YT) = range(13)
        PREP = (A_W, A_A, A_KK, A_BON, A_BK)
        SLOTS = [(A_W,), (A_U0, A_A,), (A_SA0, A_KK,), (A_ST, A_YT,), (A_U1,), (A_SA1,), (A_Y, A_BON,), (), (A_BK, A_G,), (), (), ()]

        def slot_steps(g, slot):
            steps = [(g + 1 if k in PREP else g - 2 if k == A_YT else g - 1, k) for k in SLOTS[slot]]
            return [(n, k) for n, k in steps if 0 <= n < 4]

        def v_bank(i):
            return 2 + i % 2

        tail_steps = [(3, A_U0), (2, A_YT)] + [(3, k) for k in (A_SA0, A_ST, A_U1, A_SA1, A_Y, A_G, A_YT)]
        aux_order = [(0, k) for k in PREP] + [s for g in range(4) for i in range(12) for s in slot_steps(g, i)] + tail_steps
        aux_at = lambda g, k: aux_order.index((g, k))
        INV = 2 + 2 * (NL - 1)
        INVR = 3 + 2 * (NL - 1)
        MIXES = [("r", 0), ("k", 2), ("w", 1), ("a", 4), ("v", 3), ("g", 5)]
        stat_ready, sd_ready, tr_ready, xfm_ready, xhi_ready, xlo_ready, xtm_ready = (
            sem(n) for n in ("stat_ready", "sd_ready", "tr_ready", "xfm_ready", "xhi_ready",
                             "xlo_ready", "xtm_ready"))
        gain_loaded = sem("gain_loaded")
        ffn_act, ffn_taken, hid_hi_done, hid_ready = (
            sem(n) for n in ("ffn_act", "ffn_taken", "hid_hi_done", "hid_ready"))
        p_taken = sem("p_taken")
        late_loaded = sem("late_loaded")
        rot_ready, rope_done, scores_ready, masked_ready, exp_ready, p_ready, pt_ready, pt_taken = (
            sem(n) for n in ("rot_ready", "rope_done", "scores_ready", "masked_ready", "exp_ready", "p_ready",
                             "pt_ready", "pt_taken"))
        o_ready, o_taken, o_lo_done = sem("o_ready"), sem("o_taken"), sem("o_lo_done")
        conv_ready, silu_ready, gate_mm, gate_abs, gate_ln, gate_rows, gate_tr, gate_cols, em_ready = (
            sem(n) for n in ("conv_ready", "silu_ready", "gate_mm", "gate_abs", "gate_ln", "gate_rows", "gate_tr",
                             "gate_cols", "em_ready"))
        row_ready, row_taken, w_ready, ml_var, ml_sd, ml_ready, ml_tr, ml_fm = (
            sem(n) for n in ("row_ready", "row_taken", "w_ready", "ml_var", "ml_sd", "ml_ready", "ml_tr", "ml_fm"))
        bank_done = sem("bank_done")
        rstd_ready, xn0_ready, xn_act, xn_dve = sem("rstd_ready"), sem("xn0_ready"), sem("xn_act"), sem("xn_dve")
        mem_loaded, final_ready = sem("mem_loaded"), sem("final_ready")

        NORMS = [
            ("mix0", ("ln_mix_g", 0), ("ln_mix_b", 0), 0, True), ("ffn0", ("ln_ffn_g", 0), ("ln_ffn_b", 0), 0, True),
            ("mix1", ("ln_mix_g", KT), ("ln_mix_b", KT), 0, True), ("ffn1", ("ln_ffn_g", KT), ("ln_ffn_b", KT), 0, True),
            ("ln1", ("ln1_2", 0), None, 2, False), ("mem", ("ln_mem_2", 0), None, 2, False),
            ("lnx", ("ln_x_2", 0), None, 2, False), ("ln2", ("ln2_2", 0), None, 2, False),
            ("final", None, None, 2, False)]
        FM_NORMS = [0, 1, 2, 4, 5, 6, 7]
        FFN = {"ffn0": (first["ffn0"], 11, 0, 2, 4), "ffn1": (first["ffn1"], 11, 11, 2, 4), "ff2": (first["ff2"], 16, 22, 6, 2)}
        FFN_PEEL = 3

        def ffn_slabs(name, j):
            s0, n = FFN[name][:2]
            w = 1 if name == "ff2" else 2
            at = s0 + (w + 1) * j - (1 if j else 0)
            return (list(range(at, at + w)) if j < n else []), (at + (w if j < n else 0) if j else None)
        P_FIRST = {"qkv": 0, "ml_qk": 12, "ml_v": 16, "ml_o": 18, "fx_qk": 20, "fx_v": 24, "x_k": 26, "x_v": 30, "x_q": 34}
        def memory_slab(n):
            return first["x_k"] + n

        U_MOBA, U_ML, U_FX, U_X = 0, 16, 20, 28
        O_MOBA, O_ML, O_FX, O_X = 0, 4, 4, 8
        CAUSAL = [(0, 0, P), (1, P, 3 * P)]
        FULL = [(0, 0, T), (1, T, 2 * T)]
        BLOCKS = {"causal": [(0, 0, 0), (P, 1, 0), (2 * P, 1, 1)],
                  "full": [(0, 0, 0), (T, 1, 0), (P, 0, 1), (T + P, 1, 1)]}

        def pcol(name, n=0):
            return par[:, PCOL[name] + n:PCOL[name] + n + 1]

        def chain(eng, s):
            count = [0]

            def link(ins):
                count[0] += 1
                ins.then_inc(s, 1)
                eng.wait_ge(s, count[0])
            return link

        block = ctx.enter_context(nc.Block())

        @block.sync
        def _(sp):
            def load_wa(g):
                for dst, src in ((w2, d["w2"]), (a2, d["a2"])):
                    sp.dma_start(dst[:, :], src[:, 256 * g:256 * g + 256]).then_inc(lora2_loaded, 16)

            def load_g(g):
                at = slice(256 * g, 256 * g + 256)
                for dst, src in ((g2, d["g2"][0:P]), (g2b, d["g2"][P:GLORA])):
                    sp.dma_start(dst[:, :], src[:, at]).then_inc(gate_lora_loaded, 16)
                for dst, src in ((gn_g, d["gn_g"]), (gn_b, d["gn_b"])):
                    sp.dma_start(dst[:, :], src[:, at].partition_broadcast(P)).then_inc(gate_lora_loaded, 16)

            sp.dma_start(par[:, :], d["params"]).then_inc(par_loaded, 16)
            for n, k in enumerate((slice(0, KT // 2), slice(KT // 2, KT))):
                sp.dma_start(xt[:, k, :], d["xT"][:, k]).then_inc(xt_loaded[n], 16)
            def load(i, r=0, per=0):
                if i >= RAW:
                    wait_slab(sp, i - RAW, r, per)
                src = d["weights"][i + r * per] if per else d["weights"][i]
                sp.dma_start(w_raw[:, i % RAW, :], src).then_inc(raw_loaded[i % RAW], 16)

            for i in range(18):
                if i == 17:
                    sp.wait_ge(rwkv_lo_done, 4)
                load(i)
                if i == 11:
                    sp.wait_ge(lora1_mm, 3)
                    sp.wait_ge(mix_lo_done, 4)
                    load_wa(0)
                    load_g(0)
                if i == 16:
                    for g in range(1, 4):
                        sp.wait_ge(aux_ready, aux_at(g - 1, A_A) + 1)
                        load_wa(g)
                    for g in range(1, 4):
                        sp.wait_ge(aux_ready, aux_at(g - 1, A_G) + 1)
                        sp.wait_ge(y_ready, g)
                        load_g(g)
                        if g == 3:
                            sp.wait_ge(aux_ready, aux_at(2, A_Y) + 1)
                            sp.dma_start(x_tm[:, :, :], d["x"]).then_inc(x_loaded, 16)
            rounds = (n_slabs - 18) // 6
            with sp.Fori(0, rounds) as r:
                for i in range(18, 24):
                    load(i, r, 6)
            for i in range(18 + 6 * rounds, n_slabs):
                load(i)

        @block.scalar
        def _(act):
            link = chain(act, act_step)

            def hi(i, r=0, per=0):
                if i >= n_slabs:
                    return
                act.wait_ge(raw_loaded[i % RAW], 16 * (i // RAW + 1) + r * (16 * per // RAW))
                if i >= WS:
                    act.wait_ge(slab_done, i - WS + 1 + r * per)
                nc.scalar.copy(w_hi[:, i % WS, :], w_raw[:, i % RAW, :]).then_inc(hi_done, 1)

            def take_proj(i):
                act.wait_ge(slab_done, i + 1)
                n, g = i // 4, i % 4
                if n == 2:
                    nc.scalar.copy(v_tm[:, :, 256 * g:256 * g + 256],
                                   ps[:, v_bank(i), :].rearrange("p (a b) -> p a b", a=2)).then_inc(proj_taken, 1)
                else:
                    dst = (r_fm, k_fm)[n]
                    nc.scalar.copy(dst[:, 4 * g:4 * g + 4, :],
                                   ps[:, i % 4, :].rearrange("p (a b) -> p a b", a=4)).then_inc(proj_taken, 1)
                hi(i + WS)

            def mix_high(q, dst, k=slice(0, KT)):
                act.wait_ge(mixed_ready, q + 1 + (k.stop == KT))
                nc.scalar.copy(dst[:, k, :], mixed[:, q % 2, k, :]).then_inc(mix_hi_done, 1)

            mix_high(0, rx_hi, slice(0, KT // 2))
            hi(0)
            mix_high(0, rx_hi, slice(KT // 2, KT))
            nc.scalar.dma_start(w1[:, :, :], d["w1"]).then_inc(lora1_loaded, 16)
            nc.scalar.dma_start(a1[:, :, :], d["a1"]).then_inc(lora1_loaded, 16)
            nc.scalar.dma_start(g1[:, :, :], d["g1"]).then_inc(lora1_loaded, 16)
            nc.scalar.dma_start(base_c[:, :], d["const_base"]).then_inc(consts_loaded, 16)
            nc.scalar.dma_start(rw_c[:, :], d["const_rwkv"]).then_inc(consts_loaded, 16)
            hi(1)
            hi(2)
            mix_high(1, mix_hi)
            for i in range(4):
                take_proj(i)
            act.wait_ge(lora1_mm, 1)
            nc.scalar.activation(tanh_w[:, :], ps[0:LORA, 4, 0:T], ACT.Tanh).then_inc(lora1_out, 1)
            act.wait_ge(lora1_mm, 2)
            nc.scalar.copy(lora_a[:, :], ps[0:LORA, 5, 0:T]).then_inc(lora1_out, 1)
            take_proj(4)
            act.wait_ge(slab_done, 4)
            mix_high(4, rx_hi)
            for i in range(5, 8):
                take_proj(i)
            act.wait_ge(lora1_mm, 3)
            nc.scalar.activation(sig_g[:, :], ps[:, 6, 0:T], ACT.Sigmoid).then_inc(lora1_out, 1)
            nc.scalar.activation(sig_g2[:, :], ps[0:GLORA - P, 7, 0:T], ACT.Sigmoid).then_inc(lora1_out, 1)

            def aux(g, k):
                n = aux_at(g, k)
                act.wait_ge(aux_ready, n + 1)
                return ps[:, n % 2, :]

            def squares(g):
                if g:
                    act.wait_ge(prep_ready, g)
                    act.wait_ge(a_ready, g)
                else:
                    act.wait_ge(mix_lo_done, 4)
                for m in range(2):
                    k2 = k_fm[:, 4 * g + 2 * m:4 * g + 2 * m + 2, :]
                    nc.scalar.activation(kk[:, 2 * m:2 * m + 2, :], k2, ACT.Copy, scale=pcol("rwkv_k_k", 2 * g + m))
                    ins = nc.scalar.activation(kmod[:, 2 * m:2 * m + 2, :], k2, ACT.Square,
                                               scale=pcol("rwkv_k_k", 2 * g + m))
                ins.then_inc(kk2_ready, 1)

            def exponentials(g):
                act.wait_ge(cum_ready, g + 1)
                nc.scalar.activation(e_pos[:, :, :], cum[:, :, :], ACT.Exp, scale=-DECAY)
                nc.scalar.activation(e_neg[:, :, :], cum[:, :, :], ACT.Exp, scale=DECAY)
                act.wait_ge(cprev_ready, g + 1)
                nc.scalar.activation(cprev[:, :, :], cprev[:, :, :], ACT.Exp, scale=-DECAY)
                nc.scalar.activation(sdec[:, g, :], sdec[:, g, :], ACT.Exp, scale=-DECAY).then_inc(exp_done, 1)

            def step(g, k):
                z = aux(g, k)
                if k in (A_W, A_A):
                    name, dst = (("rwkv_w0", sw), ("rwkv_a0", av))[k == A_A]
                    for m in range(2):
                        ins = nc.scalar.activation(dst[:, 2 * m:2 * m + 2, :], z[:, T * m:T * m + T].rearrange(
                            "p (t c) -> p t c", t=2), ACT.Sigmoid, bias=pcol(name, 2 * g + m))
                elif k == A_KK:
                    ins = nc.scalar.activation(norm_k[:, :, :], z.rearrange("p (a b) -> p a b", a=4), ACT.Sqrt)
                elif k == A_BON:
                    ins = nc.scalar.copy(bon[:, g, :], z[:, 0:8])
                elif k == A_BK:
                    ins = nc.scalar.copy(bk_tm[:, g % 2, :, :, :].rearrange("p a b c -> p (a b c)"), z)
                elif k == A_G:
                    ins = nc.scalar.copy(g_sb[:, :, :], z.rearrange("p (a b) -> p a b", a=2))
                elif k in (A_U0, A_U1):
                    ins = nc.scalar.copy(u_m[:, :], z[:, 0:256])
                elif k in (A_SA0, A_SA1):
                    ins = nc.scalar.copy(sa_m[:, k == A_SA1, :], z[:, 0:256])
                elif k == A_ST:
                    for m in range(2):
                        ins = nc.scalar.activation(state[:, m, :], z[:, HD * m:HD * m + HD], ACT.Copy,
                                                   scale=sdec[:, g, m:m + 1])
                elif k == A_Y:
                    ins = nc.scalar.copy(y_sb[:, :, :], z.rearrange("p (h c) -> p h c", h=8))
                else:
                    z = z.rearrange("p (a b) -> p a b", a=2)
                    if g:
                        act.wait_ge(rwkv_lo_done, g)
                    nc.scalar.copy(y_fm[:, :, :], z)
                    ins = nc.scalar.copy(mix_hi[:, 2 * g:2 * g + 2, :], z)
                ins.then_inc(aux_taken, 1)

            def deviation(g):
                act.wait_ge(yvar_ready, g + 1)
                nc.scalar.activation(ysd[:, :], yvar[:, :], ACT.Sqrt, bias=eps_c[:, 1:2], scale=1.0 / HD).then_inc(ysd_ready, 1)

            squares(0)
            take_proj(8)
            step(0, A_W)
            step(0, A_A)
            step(0, A_KK)
            take_proj(9)
            exponentials(0)
            take_proj(10)
            step(0, A_BON)
            take_proj(11)
            step(0, A_BK)
            for g in range(4):
                for t in range(TT):
                    act.wait_ge(inv_ready[t], INVR * g + 2)
                    nc.scalar.copy(nt_m[:, t].rearrange("p a b -> p (a b)"), ps[:, 4 + 3 * t, :]).then_inc(nt_taken[t], 1)
                if g < 3:
                    squares(g + 1)
                for slot in range(12):
                    for n, k in slot_steps(g, slot):
                        step(n, k)
                    if slot == 2 and g < 3:
                        exponentials(g + 1)
                    if slot == 8 and g:
                        deviation(g - 1)
            for n, k in tail_steps:
                if (n, k) == (3, A_YT):
                    deviation(3)
                    for i in range(2):
                        hi(first["rwkv_o"] + i + WS)
                step(n, k)

            def after(i, r=0, per=0):
                hi(i + WS, r, per)

            def norm_tokens(q, src):
                name, g_at, b_at, e, mean = NORMS[q]
                for t in range(TT):
                    if q == 5:
                        act.wait_ge(mem_loaded, 16)
                    else:
                        act.wait_ge(stat_ready, 2 * (q - (q > 5)) + t + 1)
                    if mean:
                        nc.scalar.activation(sd[:, t:t + 1], mv[:, t, 1:2], ACT.Sqrt, bias=eps_c[:, e:e + 1]).then_inc(sd_ready, 1)
                    else:
                        link(nc.scalar.activation(xn[:, t, :], src[:, t, :], ACT.Square, accum_out=square[:, t:t + 1]))
                        nc.scalar.activation(sd[:, t:t + 1], square[:, t:t + 1], ACT.Sqrt, scale=1.0 / C,
                                             bias=eps_c[:, e:e + 1]).then_inc(sd_ready, 1)
                    if q in (3, 8) or (t == 0 and not mean):
                        continue
                    act.wait_ge(rstd_ready, 2 * q + t + 1)
                    at = slice(0, 512) if t else slice(0, C)
                    if mean:
                        ins = nc.scalar.activation(xn[:, t, at], src[:, t, at], ACT.Identity, scale=rstd[:, t:t + 1],
                                                   bias=shift[:, t:t + 1])
                    else:
                        ins = nc.scalar.activation(xn[:, t, at], src[:, t, at], ACT.Copy, scale=rstd[:, t:t + 1])
                    ins.then_inc(xn_act if t else xn0_ready, 1)

            def feature_major(q, i):
                name, g_at, b_at, e, mean = NORMS[q]
                act.wait_ge(tr_ready, 4 * FM_NORMS.index(q) + i + 1)
                for m in range(2):
                    k = 2 * i + m
                    z = ps[:, 4 + i, T * m:T * m + T]
                    if b_at:
                        ins = nc.scalar.activation(x_fm[:, k, :], z, ACT.Identity, scale=pcol(g_at[0], g_at[1] + k),
                                                   bias=pcol(b_at[0], b_at[1] + k))
                    else:
                        ins = nc.scalar.activation(x_fm[:, k, :], z, ACT.Copy, scale=pcol(g_at[0], g_at[1] + k))
                link(ins)

            def high_part(q, i):
                if i in (1, 2):
                    act.wait_ge(xfm_ready, 2 * FM_NORMS.index(q) + i)
                nc.scalar.copy(x_hi[:, 2 * i:2 * i + 2, :], x_fm[:, 2 * i:2 * i + 2, :]).then_inc(xhi_ready, 1)

            def norm(q, src):
                norm_tokens(q, src)
                feature_major(q, 0)
                for i in range(3):
                    high_part(q, i)
                feature_major(q, 3)
                high_part(q, 3)

            def load_gain(which, layer, q):
                if q:
                    act.wait_ge(xtm_ready, 2 * q)
                else:
                    act.wait_ge(slab_done, first["rkv"] + 12)
                    act.wait_ge(y_ready, 4)
                for n, s in enumerate(("g", "b")):
                    nc.scalar.dma_start(gain[:, n, :], d[f"{which}_{s}"][layer:layer + 1, :].partition_broadcast(P))\
                        .then_inc(gain_loaded, 16)

            def ffn(name):
                s0, n, h0, per, rounds = FFN[name]
                slabs = per * (2 if name == "ff2" else 3)

                def step(j, r=0):
                    up, down = ffn_slabs(name, j)
                    if j < n:
                        act.wait_ge(slab_done, up[0] + 1 + r * slabs)
                        if h0 + j >= 2:
                            act.wait_ge(ffn_taken, h0 + j - 1 + r * per)
                        nc.scalar.activation(act_f[:, j % 2, :], ps[:, 4 + 2 * (j % 2), :],
                                             ACT.Relu if name == "ff2" else ACT.Silu).then_inc(ffn_act, 1)
                        for i in up:
                            after(i, r, slabs)
                        act.wait_ge(ffn_taken, h0 + j + 1 + r * per)
                        if j >= 2:
                            act.wait_ge(slab_done, ffn_slabs(name, j - 1)[1] + 1 + r * slabs)
                        nc.scalar.copy(hid_hi[:, j % 2, :], hid[:, j % 2, :]).then_inc(hid_hi_done, 1)
                    if 0 < j < n:
                        after(down, r, slabs)

                for j in range(FFN_PEEL):
                    step(j)
                if name != "ff2":
                    load_gain("ffn", int(name[-1]), 1 + 2 * int(name[-1]))
                with act.Fori(0, rounds) as r:
                    for j in range(FFN_PEEL, FFN_PEEL + per):
                        step(j, r)
                for j in range(FFN_PEEL + per * rounds, n + 1):
                    step(j)

            def take(n, i, dst, scale=1.0):
                act.wait_ge(slab_done, i + 1)
                nc.scalar.activation(dst, ps[:, n % 3, :].rearrange("p (a b) -> p a b", a=2), ACT.Copy,
                                     scale=scale).then_inc(p_taken, 1)
                after(i)

            def exps(u, s, tiles):
                act.wait_ge(masked_ready, u + 1 - (4 if u >= U_ML else 0))
                for t, c0, c1 in tiles:
                    ins = nc.scalar.activation(s[:, u % 4, c0:c1], s[:, u % 4, c0:c1], ACT.Exp,
                                               bias=mx[:, 2 * (u % 4) + t:2 * (u % 4) + t + 1],
                                               accum_out=sm[:, 2 * (u % 4) + t:2 * (u % 4) + t + 1])
                ins.then_inc(exp_ready, 1)

            def take_pt(u, dst, n):
                act.wait_ge(pt_ready, u + 1)
                nc.scalar.copy(dst[:, u % 4, 0:n], ps[:, 4 + u % 4, 0:n]).then_inc(pt_taken, 1)

            def take_o(o, bank, o_sb, f2, ready=None):
                act.wait_ge(o_ready, ready or o + 1)
                if o:
                    act.wait_ge(o_lo_done, o)
                z = ps[:, bank, :].rearrange("p (a b) -> p a b", a=2)
                nc.scalar.copy(o_sb[:, :, :], z)
                nc.scalar.copy(mix_hi[:, f2, :], z).then_inc(o_taken, 1)

            load_gain("mix", 0, 0)
            after(first["rwkv_o"] + 2)
            norm(0, x_tm)
            after(first["rwkv_o"] + 3)
            nc.scalar.dma_start(rope_c[:, :], d["const_rope"]).then_inc(late_loaded, 16)
            nc.scalar.dma_start(gsel[:, :], d["const_gates"]).then_inc(late_loaded, 16)
            nc.scalar.dma_start(gate_w[:, :, :], d["gate_w"]).then_inc(late_loaded, 16)
            nc.scalar.dma_start(gate_bf[:, :], d["gate_b"][0:12]).then_inc(late_loaded, 16)
            nc.scalar.dma_start(gate_bi[:, :], d["gate_b"][12:16]).then_inc(late_loaded, 16)
            ffn("ffn0")
            norm(1, x_tm)
            after(first["ffn0"] + 32)
            for g in range(-1, 4):
                if g >= 0:
                    for u in range(4 * g, 4 * g + 4):
                        exps(U_MOBA + u, ma_s, CAUSAL)
                if g < 3:
                    for n, dst in enumerate((ma_q, ma_k, ma_vv[:, (g + 1) % 2])):
                        take(3 * g + 3 + n, first["qkv"] + 3 * g + 3 + n, dst if n == 2 else dst[:, :, :])
                if g == 0:
                    load_gain("mix", 1, 2)
                if g >= 0:
                    for u in range(4 * g, 4 * g + 4):
                        take_pt(U_MOBA + u, ma_p, 3 * P)
                    take_o(O_MOBA + g, 3, ma_o, slice(2 * g, 2 * g + 2))
            for i in range(3):
                after(first["moba_o"] + i)
            norm(2, x_tm)
            after(first["moba_o"] + 3)
            ffn("ffn1")
            norm_tokens(3, x_tm)
            norm(4, x_tm)
            after(first["ffn1"] + 32)
            nc.scalar.dma_start(gain[:, :, :], d["mem"]).then_inc(mem_loaded, 16)
            act.wait_ge(gate_abs, 1)
            link(nc.scalar.activation(za[:, :], za[:, :], ACT.Exp, scale=-1.0))
            nc.scalar.activation(za[:, :], za[:, :], ACT.Ln, bias=1.0).then_inc(gate_ln, 1)

            def takes(section, n, dst, scale=lambda j: 1.0):
                for j in range(n):
                    take(P_FIRST[section] + j, first[section] + j, dst(j), scale(j))
            takes("ml_qk", 4, lambda j: conv_in[:, 2 * j:2 * j + 2, 3:T + 3])
            norm_tokens(5, gain)
            takes("ml_v", 2, lambda j: ml_v[:, :, 256 * j:256 * j + 256])
            for i in (0, 3):
                feature_major(5, i)
            act.wait_ge(gate_tr, 1)
            nc.scalar.copy(tc[:, :, :], ps[:, 3, 0:P].rearrange("p (a b) -> p a b", a=2)).then_inc(gate_cols, 1)
            for j in range(2):
                act.wait_ge(slab_done, first["ml_o"] + j + 1)
                n = P_FIRST["ml_o"] + j
                nc.scalar.activation(ml_o[:, :, 256 * j:256 * j + 256], ps[:, n % 3, :].rearrange("p (a b) -> p a b", a=2),
                                     ACT.Sigmoid).then_inc(p_taken, 1)
                after(first["ml_o"] + j)
            act.wait_ge(conv_ready, 1)
            nc.scalar.activation(conv_out[:, :, :], conv_out[:, :, :], ACT.Silu).then_inc(silu_ready, 1)
            takes("fx_qk", 4, lambda j: (fx_q, fx_k)[j // 2][:, 2 * (j % 2):2 * (j % 2) + 2, :],
                  lambda j: (HD ** -0.5, 1.0)[j // 2])
            dst = lambda j: fx_v[:, :, 256 * j:256 * j + 256]
            take(P_FIRST["fx_v"], first["fx_v"], dst(0))
            act.wait_ge(slab_done, first["fx_v"] + 2)
            for i in range(4):
                high_part(5, i)
            take(P_FIRST["fx_v"] + 1, first["fx_v"] + 1, dst(1))

            def take_memory(n):
                j = n % 4
                act.wait_ge(slab_done, memory_slab(n) + 1)
                z = ps[:, 2, :].rearrange("p (a b) -> p a b", a=2)
                dst = gain[:, :, 256 * j:256 * j + 256] if n >= 4 else xk_fm[:, 2 * j:2 * j + 2, 0:T]
                nc.scalar.copy(dst, z).then_inc(p_taken, 1)
                after(memory_slab(n))

            act.wait_ge(em_ready, 1)
            nc.scalar.activation(em[:, :], em[:, :], ACT.Exp, scale=-1.0).then_inc(em_ready, 1)
            for u in range(4):
                act.wait_ge(row_taken, u + 1)
                nc.scalar.activation(bias[:, u, :], bias[:, u, :], ACT.Exp).then_inc(w_ready, 1)
            take_memory(0)
            take_memory(1)
            for u in range(4):
                take_pt(U_ML + u, se_p, 3 * P)
            take_memory(2)
            for u in range(4):
                exps(U_FX + u, se_s, CAUSAL)
            act.wait_ge(ml_var, 1)
            nc.scalar.activation(ml_rs[:, :], ml_rs[:, :], ACT.Sqrt, scale=1.0 / P, bias=eps_c[:, 2:3]).then_inc(ml_sd, 1)
            take_memory(3)
            for u in range(4):
                take_pt(U_FX + u, se_p, 3 * P)
            take_o(O_FX, 3, se_o, slice(4, 6), O_ML + 3)
            take_memory(4)
            take_memory(5)
            for b in range(2):
                act.wait_ge(ml_fm, b + 1)
                nc.scalar.copy(mix_hi[:, 2 * b:2 * b + 2, :], se_o[:, :, :]).then_inc(o_taken, 1)
            take_memory(6)
            for u in range(4):
                exps(U_FX + 4 + u, se_s, CAUSAL)
            take_memory(7)
            for u in range(4):
                take_pt(U_FX + 4 + u, se_p, 3 * P)
            take_o(O_FX + 3, 3, se_o, slice(6, 8), O_ML + 4)
            for i in range(3):
                after(first["mix_o"] + i)
            norm(6, x_tm)
            after(first["mix_o"] + 3)
            takes("x_q", 4, lambda j: xq_fm[:, 2 * j:2 * j + 2, :], lambda j: (C // 4) ** -0.5)
            for u in range(4):
                exps(U_X + u, cr_s, FULL)
            for u in range(4):
                take_pt(U_X + u, cr_p, 512)
            for u in range(4):
                take_o(O_X + u, u, cr_o, slice(2 * u, 2 * u + 2))
            nc.scalar.dma_start(gain[:, 0, :], d["final_g"].partition_broadcast(P)).then_inc(gain_loaded, 16)
            for i in range(3):
                after(first["x_o"] + i)
            norm(7, x_tm)
            after(first["x_o"] + 3)
            ffn("ff2")
            norm_tokens(8, x_tm)
            for t in range(TT):
                act.wait_ge(final_ready, t + 1)
                nc.scalar.dma_start(out[:, t, :], xn[:, t, :]).then_inc(out_stored, 16)
            act.wait_ge(out_stored, 32)

        @block.gpsimd
        def _(pool):
            plink = chain(pool, pool_step)

            def lo(i, r=0, per=0):
                if i >= n_slabs or lo_engine(i)[0] != "pool":
                    return
                pool.wait_ge(hi_done, i + 1 + r * per)
                nc.gpsimd.tensor_tensor(w_lo[:, i % WS, :], w_raw[:, i % RAW, :], w_hi[:, i % WS, :].bitcast(F32),
                                        ALU.subtract).then_inc(lo_pool, 1)
            for i in range(first["rwkv_o"]):
                lo(i)

            def operands(g):
                k4 = slice(4 * g, 4 * g + 4)
                tt = nc.gpsimd.tensor_tensor
                pool.wait_ge(cum_ready, g + 1)
                tt(cprev[:, :, :], cum[:, :, :], sw[:, :, :], ALU.subtract).then_inc(cprev_ready, 1)
                pool.wait_ge(kmod_ready, g + 1)
                pool.wait_ge(cprev_ready, g + 1)
                tt(sw[:, :, :], r_fm[:, k4, :], kmod[:, :, :], ALU.mult).then_inc(rkr_ready, 1)
                pool.wait_ge(kk_ready, 2 * g + 2)
                if g:
                    for t in range(TT):
                        pool.wait_ge(inv_ready[t], INVR * (g - 1) + 3)
                plink(tt(b_t[:, :, :], kk[:, :, :], av[:, :, :], ALU.mult))
                pool.wait_ge(exp_done, g + 1)
                tt(b_t[:, :, :], b_t[:, :, :], e_neg[:, :, :], ALU.mult)
                tt(k_t[:, :, :], kmod[:, :, :], e_neg[:, :, :], ALU.mult)
                pool.wait_ge(rkr_ready, g + 1)
                tt(r_fm[:, k4, :], r_fm[:, k4, :], e_pos[:, :, :], ALU.mult).then_inc(prep_ready, 1)

            def outputs(g):
                at = slice(256 * g, 256 * g + 256)
                tt = nc.gpsimd.tensor_tensor
                pool.wait_ge(ymean_ready, g + 1)
                plink(tt(y_sb[:, :, :], y_sb[:, :, :], along(ymean[:, :], HD), ALU.subtract))
                tt(y_sq[:, :, :], y_sb[:, :, :], y_sb[:, :, :], ALU.mult).then_inc(ysq_ready, 1)
                pool.wait_ge(yvar_ready, g + 1)
                v8 = v_tm[:, :, at].rearrange("p t (h c) -> p t h c", c=HD)
                for t in range(TT):
                    tt(y_sq[:, 4 * t:4 * t + 4, :], v8[:, t], along(bon[:, g, 4 * t:4 * t + 4], HD), ALU.mult)
                pool.wait_ge(yrs_ready, g + 1)
                plink(tt(y_sb[:, :, :], y_sb[:, :, :], along(yrs[:, :], HD), ALU.mult))
                flat = lambda y: y[:, :, :].rearrange("p (t h) c -> p t (h c)", t=TT)
                pool.wait_ge(gate_lora_loaded, 64 * (g + 1))
                plink(tt(flat(y_sb), flat(y_sb), over(gn_g[:, :], TT), ALU.mult))
                plink(tt(flat(y_sb), flat(y_sb), over(gn_b[:, :], TT), ALU.add))
                plink(tt(flat(y_sb), flat(y_sb), flat(y_sq), ALU.add))
                pool.wait_ge(aux_taken, aux_at(g, A_G) + 1)
                tt(flat(y_sb), flat(y_sb), g_sb[:, :, :], ALU.mult).then_inc(y_ready, 1)

            operands(0)
            for i in range(WS):
                lo(first["rwkv_o"] + i)
            for g in range(4):
                if g < 3:
                    operands(g + 1)
                if g:
                    outputs(g - 1)
            pool.wait_ge(prep_ready, 4)
            pool.wait_ge(aux_taken, aux_at(3, A_BON) + 1)
            e4 = e_pos[:, :, :].rearrange("p (t a) (h c) -> p t (a h) c", t=TT, c=HD)
            for t in range(TT):
                ins = nc.gpsimd.tensor_tensor(e4[:, t], v_tm[:, t, 768:1024].rearrange("p (h c) -> p h c", c=HD),
                                              along(bon[:, 3, 4 * t:4 * t + 4], HD), ALU.mult)
            ins.then_inc(bonus_ready, 1)

            def gain_offset(q, t):
                if t:
                    pool.wait_ge(xn_act, q + 1)
                    pool.wait_ge(xn_dve, q + 1)
                else:
                    pool.wait_ge(xn0_ready, q + 1)
                pool.wait_ge(gain_loaded, 32 * (q + 1))
                plink(nc.gpsimd.tensor_tensor(x_tm[:, t, :], xn[:, t, :], gain[:, 0, :], ALU.mult))
                nc.gpsimd.tensor_tensor(x_tm[:, t, :], x_tm[:, t, :], gain[:, 1, :], ALU.add).then_inc(xtm_ready, 1)

            def low_parts(a, b):
                rounds = (b - a) // 6
                if rounds > 1:
                    with pool.Fori(0, rounds) as r:
                        for i in range(a, a + 6):
                            lo(i, r, 6)
                    a += 6 * rounds
                for i in range(a, b):
                    lo(i)

            at = first["rwkv_o"] + WS
            for q, last in enumerate((first["rwkv_o"] + 3, first["ffn0"] + 32, first["moba_o"] + 3)):
                low_parts(at, last + WS)
                gain_offset(q, 0)
                low_parts(last + WS, last + WS + 2)
                gain_offset(q, 1)
                at = last + WS + 2
            low_parts(at, n_slabs)

        @block.vector
        def _(dve):
            link = chain(dve, dve_step)
            V = nc.vector
            for n, e in enumerate((LN_EPS, GN_EPS, RMS_EPS)):
                ins = V.memset(eps_c[:, n:n + 1], e)
            link(ins)

            def lo(i, r=0, per=0):
                if i >= n_slabs or lo_engine(i)[0] != "dve":
                    return
                dve.wait_ge(hi_done, i + 1 + r * per)
                V.tensor_tensor(w_lo[:, i % WS, :], w_raw[:, i % RAW, :], w_hi[:, i % WS, :].bitcast(F32),
                                ALU.subtract).then_inc(lo_dve, 1)

            def mix(q, ks=slice(0, KT)):
                if q in (2, 3):
                    dve.wait_ge(mix_hi_done, q)
                    dve.wait_ge(mix_lo_done, q)
                elif q in (4, 5):
                    dve.wait_ge(lora1_mm, q - 3)
                for k in range(ks.start, ks.stop):
                    ins = V.scalar_tensor_tensor(mixed[:, q % 2, k, :], xx[:, k, :], pcol("rwkv_mu", KT * MIXES[q][1] + k),
                                                 xt[:, k, :], ALU.mult, ALU.add)
                ins.then_inc(mixed_ready, 1)

            def mix_low(n, q, dst, high, k=slice(0, KT)):
                dve.wait_ge(mix_hi_done, n + 1 + (k.stop == KT))
                V.tensor_tensor(dst[:, k, :], mixed[:, q % 2, k, :], high[:, k, :].bitcast(F32),
                                ALU.subtract).then_inc(mix_lo_done, 1)

            dve.wait_ge(par_loaded, 16)
            halves = (slice(0, KT // 2), slice(KT // 2, KT))
            for n, k in enumerate(halves):
                dve.wait_ge(xt_loaded[n], 16)
                V.tensor_tensor(xx[:, k, 1:T], xt[:, k, 0:T - 1], xt[:, k, 1:T], ALU.subtract)
                link(V.tensor_scalar(xx[:, k, 0:1], xt[:, k, 0:1], -1.0, None, ALU.mult))
                mix(0, k)
            mix_low(0, 0, rx_lo, rx_hi, halves[0])
            lo(0)
            mix_low(0, 0, rx_lo, rx_hi, halves[1])
            mix(1)
            lo(2)
            mix_low(1, 1, mix_lo, mix_hi)
            mix(2)
            lo(4)
            mix(3)
            lo(6)
            mix(4)
            dve.wait_ge(slab_done, 4)
            mix_low(2, 4, rx_lo, rx_hi)
            mix(5)
            for i in range(8, 12, 2):
                lo(i)

            dve.wait_ge(consts_loaded, 32)
            dve.wait_ge(par_loaded, 16)
            for k in range(KT):
                ins = V.tensor_scalar(rk_sel[:, k, :], rc("headsel"), pcol("rwkv_r_k", k), None, ALU.mult)
            link(ins)
            flat = lambda t: t.rearrange("p a b -> p (a b)")

            def decays(g):
                dve.wait_ge(aux_taken, aux_at(g, A_W) + 1)
                link(V.tensor_tensor_scan(flat(cum), rc("reset"), flat(sw), 0.0, ALU.mult, ALU.add))
                link(V.tensor_copy(smid[:, :], cum[:, :, P // 2 - 1]))
                last = cum[:, :, :].rearrange("p (a t) c -> p a t c", t=TT)[:, :, 1, P - 1]
                mid = smid[:, :].rearrange("p (a t) -> p a t", t=TT)
                link(V.tensor_tensor(sdec[:, g, :], cum[:, :, :].rearrange("p (a t) c -> p a t c", t=TT)[:, :, 0, P - 1],
                                     mid[:, :, 0], ALU.subtract))
                link(V.tensor_tensor(sdec[:, g, :], sdec[:, g, :], mid[:, :, 1], ALU.add))
                V.tensor_tensor(cum[:, :, :], cum[:, :, :], along(smid[:, :], P), ALU.subtract).then_inc(cum_ready, 1)

            def modified_k(g):
                dve.wait_ge(aux_taken, aux_at(g, A_A) + 1)
                dve.wait_ge(aux_ready, aux_at(g, A_KK) + 1)
                for m in range(2):
                    at = slice(2 * m, 2 * m + 2)
                    ins = V.tensor_scalar(kmod[:, at, :], av[:, at, :], 1.0, pcol("rwkv_k_a", 2 * g + m),
                                          ALU.subtract, ALU.mult)
                link(ins)
                V.scalar_tensor_tensor(kmod[:, :, :], kmod[:, :, :], 1.0, k_fm[:, 4 * g:4 * g + 4, :],
                                       ALU.add, ALU.mult).then_inc(kmod_ready, 1)

            def normalized_k(g, m):
                at = slice(2 * m, 2 * m + 2)
                dve.wait_ge(aux_taken, aux_at(g, A_KK) + 1)
                link(V.tensor_scalar(norm_k[:, at, :], norm_k[:, at, :], 1e-12, None, ALU.max))
                link(V.reciprocal(norm_k[:, at, :], norm_k[:, at, :]))
                V.tensor_tensor(kk[:, at, :], kk[:, at, :], norm_k[:, at, :], ALU.mult).then_inc(kk_ready, 1)

            def a_tilde(g):
                dve.wait_ge(exp_done, g + 1)
                dve.wait_ge(kk_ready, 2 * g + 2)
                dve.wait_ge(kmod_ready, g + 1)
                V.scalar_tensor_tensor(k_fm[:, 4 * g:4 * g + 4, :], kk[:, :, :], -1.0, cprev[:, :, :],
                                       ALU.mult, ALU.mult).then_inc(a_ready, 1)

            def y_mean(g):
                dve.wait_ge(aux_taken, aux_at(g, A_Y) + 1)
                link(V.tensor_reduce(ymean[:, :], y_sb[:, :, :], AX_X, ALU.add))
                V.tensor_scalar(ymean[:, :], ymean[:, :], 1.0 / HD, None, ALU.mult).then_inc(ymean_ready, 1)

            def y_variance(g):
                dve.wait_ge(ysq_ready, g + 1)
                V.tensor_reduce(yvar[:, :], y_sq[:, :, :], AX_X, ALU.add).then_inc(yvar_ready, 1)

            def y_scale(g):
                dve.wait_ge(ysd_ready, g + 1)
                V.reciprocal(yrs[:, :], ysd[:, :]).then_inc(yrs_ready, 1)

            def mix_out_low(g):
                dve.wait_ge(aux_taken, aux_at(g, A_YT) + 1)
                V.tensor_tensor(mix_lo[:, 2 * g:2 * g + 2, :], y_fm[:, :, :], mix_hi[:, 2 * g:2 * g + 2, :].bitcast(F32),
                                ALU.subtract).then_inc(rwkv_lo_done, 1)

            def last_outputs():
                y_mean(3)
                dve.wait_ge(ymean_ready, 4)
                link(V.tensor_tensor(y_sb[:, :, :], y_sb[:, :, :], along(ymean[:, :], HD), ALU.subtract))
                V.tensor_tensor(y_sq[:, :, :], y_sb[:, :, :], y_sb[:, :, :], ALU.mult).then_inc(ysq_ready, 1)
                y_variance(3)
                y2 = y_sb[:, :, :].rearrange("p (t h) c -> p t (h c)", t=TT)
                dve.wait_ge(gate_lora_loaded, 256)
                y_scale(3)
                dve.wait_ge(yrs_ready, 4)
                link(V.tensor_tensor(y_sb[:, :, :], y_sb[:, :, :], along(yrs[:, :], HD), ALU.mult))
                link(V.tensor_tensor(y2, y2, over(gn_g[:, :], TT), ALU.mult))
                link(V.tensor_tensor(y2, y2, over(gn_b[:, :], TT), ALU.add))
                dve.wait_ge(bonus_ready, 1)
                link(V.tensor_tensor(y2, y2, e_pos[:, :, :].rearrange("p (t a) c -> p t (a c)", t=TT), ALU.add))
                dve.wait_ge(aux_taken, aux_at(3, A_G) + 1)
                V.tensor_tensor(y2, y2, g_sb[:, :, :], ALU.mult).then_inc(y_ready, 1)

            def take_scores(g):
                d_g, rb_g, ak_g, rk_g = d_m[g % 2], rb_m[g % 2], ak_m[g % 2], rk_m[g % 2]
                for t in range(TT):
                    dve.wait_ge(inv_ready[t], INVR * g + 1)
                    ba = ps[:, 2 + 3 * t:4 + 3 * t, :].rearrange("p b (h s c) -> p (b h) s c", h=2, s=2)
                    for b in range(2):
                        V.tensor_tensor(w_m[:, t, 2 * b:2 * b + 2], ba[:, 2 * b:2 * b + 2, 0], over(rc("level0"), 2), ALU.mult)
                        ins = V.tensor_tensor(rb_g[:, t, 2 * b:2 * b + 2], ba[:, 2 * b:2 * b + 2, 1], over(rc("incl"), 2), ALU.mult)
                    link(ins)
                    V.tensor_tensor(d_g[:, t], w_m[:, t], over(ident, 4), ALU.add).then_inc(inv_taken[t], 1)
                for t in range(TT):
                    dve.wait_ge(nt_taken[t], g + 1)
                    link(V.tensor_tensor(dt_m[:, t], nt_m[:, t], over(rc("level0T"), 4), ALU.mult))
                    link(V.tensor_tensor(dt_m[:, t], dt_m[:, t], over(ident, 4), ALU.add))
                    dve.wait_ge(inv_ready[t], INVR * g + 3)
                    ka = ps[:, 2 + 3 * t:4 + 3 * t, :].rearrange("p b (h s c) -> p (b h) s c", h=2, s=2)
                    for b in range(2):
                        V.tensor_tensor(ak_g[:, t, 2 * b:2 * b + 2], ka[:, 2 * b:2 * b + 2, 0], over(rc("strict"), 2), ALU.mult)
                        ins = V.tensor_tensor(rk_g[:, t, 2 * b:2 * b + 2], ka[:, 2 * b:2 * b + 2, 1], over(rc("incl"), 2), ALU.mult)
                    ins.then_inc(inv_taken[t], 1)

            def take_half_level(g, slot):
                n, d_g = slot // 2 + 1, d_m[g % 2]
                b4 = lambda b: ps[:, b, :].rearrange("p (h c) -> p h c", h=4)
                for t in range(TT):
                    dve.wait_ge(inv_ready[t], INVR * g + 3 + slot + 1)
                    if slot % 2 == 0:
                        V.tensor_tensor(w_m[:, t], b4(2 + 3 * t), over(rc(f"level{n}"), 4), ALU.mult).then_inc(inv_taken[t], 1)
                    else:
                        if n < NL - 1:
                            V.tensor_tensor(dt_m[:, t], b4(4 + 3 * t), dt_m[:, t], ALU.add)
                        V.tensor_tensor(d_g[:, t], b4(3 + 3 * t), d_g[:, t], ALU.add).then_inc(inv_taken[t], 1)

            dve.wait_ge(aux_taken, 1)
            decays(0)
            modified_k(0)
            normalized_k(0, 0)
            normalized_k(0, 1)
            a_tilde(0)
            for i in range(12, 15, 2):
                lo(i)
            for g in range(4):
                take_scores(g)
                for slot in range(12):
                    take_half_level(g, slot)
                    if slot == 4 and g > 1:
                        mix_out_low(g - 2)
                    if g < 3:
                        if slot == 0:
                            decays(g + 1)
                        elif slot == 2:
                            modified_k(g + 1)
                        elif slot in (4, 5):
                            normalized_k(g + 1, slot - 4)
                        elif slot == 6:
                            a_tilde(g + 1)
                    if g:
                        if slot == 7:
                            y_mean(g - 1)
                        elif slot == 8:
                            y_variance(g - 1)
                        elif slot == 9:
                            y_scale(g - 1)
            mix_out_low(2)
            last_outputs()
            for i in range(2):
                lo(first["rwkv_o"] + i + WS)
            mix_out_low(3)
            def after(i, r=0, per=0):
                lo(i + WS, r, per)

            def add_product(src, scale, t, n, last_slab, product, base=0):
                if t and n:
                    dve.wait_ge(slab_done, last_slab + 1)
                else:
                    dve.wait_ge(bank_done, 3 * (product - 1) + 2 * t + n + 1)
                at = src[:, t, 512 * n:512 * n + 512]
                return V.scalar_tensor_tensor(at, at, scale, ps[:, base + 2 * t + n, :], ALU.mult, ALU.add)

            def norm_tokens(q, src, scale=None, last_slab=None, product=None):
                name, g_at, b_at, e, mean = NORMS[q]

                def add(t, n):
                    return add_product(src, scale, t, n, last_slab, product, 0 if q else 4)

                def half_statistics(t, n):
                    return V.bn_stats(stats[:, t, n, :], src[:, t, 512 * n:512 * n + 512])

                def mean_variance(t):
                    V.bn_aggr(mv[:, t, :], stats[:, t, :, :].rearrange("p a b -> p (a b)")).then_inc(stat_ready, 1)

                def scales(t):
                    dve.wait_ge(sd_ready, 2 * q + t + 1)
                    ins = V.reciprocal(rstd[:, t:t + 1], sd[:, t:t + 1])
                    if mean:
                        link(ins)
                        ins = V.scalar_tensor_tensor(shift[:, t:t + 1], mv[:, t, 0:1], -1.0, rstd[:, t:t + 1],
                                                     ALU.mult, ALU.mult)
                    ins.then_inc(rstd_ready, 1)

                def normalized(t, at):
                    dve.wait_ge(rstd_ready, 2 * q + t + 1)
                    if mean:
                        return V.tensor_scalar(xn[:, t, at], src[:, t, at], mv[:, t, 0:1], rstd[:, t:t + 1],
                                               ALU.subtract, ALU.mult)
                    return V.tensor_scalar(xn[:, t, at], src[:, t, at], rstd[:, t:t + 1], None, ALU.mult)

                if mean:
                    add(0, 0)
                    link(add(0, 1))
                    half_statistics(0, 0)
                    link(half_statistics(0, 1))
                    mean_variance(0)
                    link(add(1, 0))
                    half_statistics(1, 0)
                    scales(0)
                    link(add(1, 1))
                    link(half_statistics(1, 1))
                    mean_variance(1)
                else:
                    if scale is not None:
                        for t in range(TT):
                            add(t, 0)
                            add(t, 1).then_inc(stat_ready, 1)
                    scales(0)
                    if q != 8:
                        normalized(0, slice(0, C)).then_inc(xn0_ready, 1)
                scales(1)
                if q in (3, 8):
                    return
                ins = normalized(1, slice(512, C))
                ins.then_inc(xn_dve, 1)

            def feature_major(q, i):
                name, g_at, b_at, e, mean = NORMS[q]
                dve.wait_ge(tr_ready, 4 * FM_NORMS.index(q) + i + 1)
                for m in range(2):
                    k = 2 * i + m
                    z = ps[:, 4 + i, T * m:T * m + T]
                    if b_at:
                        ins = V.tensor_scalar(x_fm[:, k, :], z, pcol(g_at[0], g_at[1] + k), pcol(b_at[0], b_at[1] + k),
                                              ALU.mult, ALU.add)
                    else:
                        ins = V.tensor_scalar(x_fm[:, k, :], z, pcol(g_at[0], g_at[1] + k), None, ALU.mult)
                ins.then_inc(xfm_ready, 1)

            def low_part(q, i):
                dve.wait_ge(xhi_ready, 4 * FM_NORMS.index(q) + i + 1)
                k = slice(2 * i, 2 * i + 2)
                V.tensor_tensor(x_lo[:, k, :], x_fm[:, k, :], x_hi[:, k, :].bitcast(F32), ALU.subtract)\
                 .then_inc(xlo_ready, 1)

            def norm(q, *how):
                norm_tokens(q, *how)
                feature_major(q, 1)
                low_part(q, 0)
                feature_major(q, 2)
                for i in range(1, 4):
                    low_part(q, i)

            def scale_stream():
                dve.wait_ge(rstd_ready, 8)
                dve.wait_ge(gain_loaded, 128)
                for t in range(TT):
                    link(V.scalar_tensor_tensor(x_tm[:, t, :], x_tm[:, t, :], mv[:, t, 0:1], gain[:, 0, :],
                                                ALU.subtract, ALU.mult))
                    V.scalar_tensor_tensor(x_tm[:, t, :], x_tm[:, t, :], rstd[:, t:t + 1], gain[:, 1, :],
                                           ALU.mult, ALU.add).then_inc(stat_ready, 1)

            def ffn(name):
                s0, n, h0, per, rounds = FFN[name]
                slabs = per * (2 if name == "ff2" else 3)

                def step(j, r=0):
                    up, down = ffn_slabs(name, j)
                    if j < n:
                        dve.wait_ge(slab_done, up[-1] + 1 + r * slabs)
                        dve.wait_ge(ffn_act, h0 + j + 1 + r * per)
                        if h0 + j >= 2:
                            dve.wait_ge(hid_hi_done, h0 + j - 1 + r * per)
                        if name == "ff2":
                            V.scalar_tensor_tensor(hid[:, j % 2, :], ps[:, 4 + 2 * (j % 2), :], 0.0, act_f[:, j % 2, :],
                                                   ALU.max, ALU.mult).then_inc(ffn_taken, 1)
                        else:
                            V.tensor_tensor(hid[:, j % 2, :], act_f[:, j % 2, :], ps[:, 5 + 2 * (j % 2), :],
                                            ALU.mult).then_inc(ffn_taken, 1)
                        for i in up:
                            after(i, r, slabs)
                        dve.wait_ge(hid_hi_done, h0 + j + 1 + r * per)
                        V.tensor_tensor(hid_lo[:, j % 2, :], hid[:, j % 2, :], hid_hi[:, j % 2, :].bitcast(F32),
                                        ALU.subtract).then_inc(hid_ready, 1)
                    if 0 < j < n:
                        after(down, r, slabs)

                for j in range(FFN_PEEL):
                    step(j)
                with dve.Fori(0, rounds) as r:
                    for j in range(FFN_PEEL, FFN_PEEL + per):
                        step(j, r)
                for j in range(FFN_PEEL + per * rounds, n + 1):
                    step(j)

            def masked(u, s, tiles, mask):
                dve.wait_ge(scores_ready, u + 1)
                for t, c0, c1 in tiles:
                    n = 2 * (u % 4) + t
                    ins = V.tensor_tensor_reduce(out=s[:, u % 4, c0:c1], in0=ps[:, 4 + u % 4, c0:c1], in1=mask(u, t, c0, c1),
                                                 scale=1.0, scalar=-3.0e38, op0=ALU.add, op1=ALU.max,
                                                 accum_out=rs[:, n:n + 1])
                link(ins)
                n = 2 * (u % 4)
                V.tensor_scalar(mx[:, n:n + 2], rs[:, n:n + 2], -1.0, None, ALU.mult).then_inc(masked_ready, 1)

            def probs(u, s, tiles):
                dve.wait_ge(exp_ready, u + 1 - (4 if u >= U_ML else 0))
                n = 2 * (u % 4)
                link(V.reciprocal(rs[:, n:n + 2], sm[:, n:n + 2]))
                for t, c0, c1 in tiles:
                    ins = V.tensor_scalar(s[:, u % 4, c0:c1], s[:, u % 4, c0:c1], rs[:, n + t:n + t + 1], None, ALU.mult)
                ins.then_inc(p_ready, 1)

            def out_low(o, o_sb, f2):
                dve.wait_ge(o_taken, o + 1)
                V.tensor_tensor(mix_lo[:, f2, :], o_sb[:, :, :], mix_hi[:, f2, :].bitcast(F32),
                                ALU.subtract).then_inc(o_lo_done, 1)

            def causal_mask(u, t, c0, c1):
                return causal[:, c0:c1]

            after(first["rwkv_o"] + 2)
            dve.wait_ge(x_loaded, 16)
            norm(0, x_tm, ALPHA, first["rwkv_o"] + 3, 1)
            after(first["rwkv_o"] + 3)
            ffn("ffn0")
            dve.wait_ge(xtm_ready, 2)
            norm(1, x_tm, ALPHA, first["ffn0"] + 32, 2)
            after(first["ffn0"] + 32)
            dve.wait_ge(late_loaded, 80)
            cos, sin = rope_c[:, 0:T], rope_c[:, T:2 * T]
            def rope(g, n):
                src, dst, c = ((ma_q, ma_q2, HD ** -0.5), (ma_k, ma_k2, 1.0))[n]
                dve.wait_ge(rot_ready, 2 * g + n + 1)
                for m in range(2):
                    V.scalar_tensor_tensor(rt[:, m, :], ps[:, 3, T * m:T * m + T], c, sin, ALU.mult, ALU.mult)
                    ins = V.scalar_tensor_tensor(dst[:, m, :], src[:, m, :], c, cos, ALU.mult, ALU.mult)
                link(ins)
                V.tensor_tensor(dst[:, :, :], dst[:, :, :], rt[:, :, :], ALU.add).then_inc(rope_done, 1)

            for g in range(-1, 4):
                if g >= 0:
                    for u in range(4 * g, 4 * g + 4):
                        masked(U_MOBA + u, ma_s, CAUSAL, causal_mask)
                if g < 3:
                    n = first["qkv"] + 3 * (g + 1)
                    after(n)
                    rope(g + 1, 0)
                    after(n + 1)
                if g >= 0:
                    for u in range(4 * g, 4 * g + 4):
                        probs(U_MOBA + u, ma_s, CAUSAL)
                if g < 3:
                    rope(g + 1, 1)
                    after(n + 2)
                if g >= 0:
                    out_low(O_MOBA + g, ma_o, slice(2 * g, 2 * g + 2))
            for i in range(3):
                after(first["moba_o"] + i)
            dve.wait_ge(xtm_ready, 4)
            norm(2, x_tm, ALPHA, first["moba_o"] + 3, 3)
            after(first["moba_o"] + 3)
            ffn("ffn1")
            dve.wait_ge(xtm_ready, 6)
            norm_tokens(3, x_tm, ALPHA, first["ffn1"] + 32, 4)
            scale_stream()
            norm(4, x_tm)
            after(first["ffn1"] + 32)
            V.memset(conv_in[:, :, 0:3], 0.0)
            V.memset(ones_t[:, :], 1.0)
            link(V.memset(gst[:, :], 0.0))
            dve.wait_ge(late_loaded, 80)
            dve.wait_ge(gate_mm, 1)
            link(V.tensor_scalar(zf[:, :], ps[0:12, 3, 0:T], gate_bf[:, :], None, ALU.add))
            link(V.tensor_scalar(gi[0:4, :], ps[0:4, 3, T:2 * T], gate_bi[:, :], None, ALU.add))
            V.scalar_tensor_tensor(za[:, :], zf[:, :], -1.0, zf[:, :], ALU.mult, ALU.max).then_inc(gate_abs, 1)
            dve.wait_ge(gate_ln, 1)
            link(V.tensor_scalar(zf[:, :], zf[:, :], 0.0, None, ALU.min))
            link(V.tensor_tensor(zf[:, :], zf[:, :], za[:, :], ALU.subtract))
            link(V.tensor_tensor_scan(gst[0:12, :], ones_t[:, :], zf[:, :], 0.0, ALU.mult, ALU.add))
            link(V.tensor_tensor(gi[0:4, :], gi[0:4, :], gst[0:4, :], ALU.subtract))
            V.tensor_tensor_scan(gst[32:36, :], ones_t[0:4, :], gi[0:4, :], 0.0, ALU.mult, ALU.max).then_inc(gate_rows, 1)
            for j in range(4):
                after(first["ml_qk"] + j)
            dve.wait_ge(mem_loaded, 16)
            norm_tokens(5, gain)
            dve.wait_ge(p_taken, P_FIRST["ml_qk"] + 4)
            for k in range(KT):
                ins = V.tensor_scalar(conv_out[:, k, :], conv_in[:, k, 0:T], pcol("ml_conv_w_2", k), pcol("ml_conv_b_2", k),
                                      ALU.mult, ALU.add)
            link(ins)
            for n in range(1, 4):
                if n == 2:
                    for j in range(2):
                        after(first["ml_v"] + j)
                for k in range(KT):
                    ins = V.scalar_tensor_tensor(conv_out[:, k, :], conv_in[:, k, n:n + T], pcol("ml_conv_w_2", KT * n + k),
                                                 conv_out[:, k, :], ALU.mult, ALU.add)
                if n < 3:
                    link(ins)
                else:
                    ins.then_inc(conv_ready, 1)
            for i in (1, 2):
                feature_major(5, i)
            dve.wait_ge(gate_cols, 1)
            for t in range(TT):
                ins = V.tensor_tensor(em[:, 4 * t:4 * t + 4], tc[:, t, 0:4], tc[:, t, 32:36], ALU.add)
            ins.then_inc(em_ready, 1)


            def rows(u, n):
                dve.wait_ge(row_ready, n + 1)
                for t, c0, c1 in CAUSAL:
                    z = ps[:, 3, 0:c1 - c0]
                    dst = bias[:, u, c0:c1]
                    if n < 4:
                        ins = V.scalar_tensor_tensor(dst, z, tc[:, t, 32 + n:33 + n], causal[:, c0:c1], ALU.subtract, ALU.add)
                    else:
                        link(V.tensor_scalar(dst, z, -1.0, tc[:, t, n:n + 1], ALU.mult, ALU.add))
                        ins = V.tensor_tensor(dst, dst, causal[:, c0:c1], ALU.add)
                ins.then_inc(row_taken, 1)

            for j in range(2):
                after(first["ml_o"] + j)
            for j in range(4):
                rows(j, j)
                after(first["fx_qk"] + j)
                if j == 1:
                    dve.wait_ge(silu_ready, 1)
                    V.tensor_scalar(conv_out[:, 4:8, :], conv_out[:, 4:8, :], P ** -0.5, None, ALU.mult).then_inc(silu_ready, 1)
            after(first["fx_v"])
            for i in range(4):
                low_part(5, i)
            after(first["fx_v"] + 1)
            def fx_masked(g):
                dve.wait_ge(row_taken, 8 + 4 * g)
                for u in range(4):
                    masked(U_FX + 4 * g + u, se_s, CAUSAL, lambda w, t, c0, c1: bias[:, w % 4, c0:c1])

            def fx_probs(g):
                for u in range(4):
                    probs(U_FX + 4 * g + u, se_s, CAUSAL)

            after(memory_slab(0))
            for u in range(4):
                dve.wait_ge(scores_ready, U_ML + u + 1)
                dve.wait_ge(w_ready, u + 1)
                for t, c0, c1 in CAUSAL:
                    ins = V.tensor_tensor_reduce(out=se_s[:, u, c0:c1], in0=ps[:, 4 + u, c0:c1], in1=bias[:, u, c0:c1],
                                                 scale=1.0, scalar=0.0, op0=ALU.mult, op1=ALU.add,
                                                 accum_out=den[:, 4 * t + u:4 * t + u + 1])
                ins.then_inc(p_ready, 1)
            dve.wait_ge(p_ready, U_ML + 4)
            rows(0, 4)
            after(memory_slab(1))
            rows(1, 5)
            rows(2, 6)
            rows(3, 7)
            after(memory_slab(2))
            dve.wait_ge(em_ready, 2)
            link(V.scalar_tensor_tensor(den[:, :], den[:, :], -1.0, den[:, :], ALU.mult, ALU.max))
            link(V.tensor_tensor(den[:, :], den[:, :], em[:, :], ALU.max))
            link(V.reciprocal(den[:, :], den[:, :]))
            fx_masked(0)
            dve.wait_ge(o_ready, O_ML + 2)
            for t in range(TT):
                ins = V.tensor_tensor(ml_y[:, 4 * t:4 * t + 4], ps[:, t, :].rearrange("p (h c) -> p h c", h=4),
                                      along(den[:, 4 * t:4 * t + 4], P), ALU.mult)
            link(ins)
            link(V.tensor_tensor(ml_sq, ml_y, ml_y, ALU.mult))
            V.tensor_reduce(ml_rs[:, :], ml_sq, AX_X, ALU.add).then_inc(ml_var, 1)
            fx_probs(0)
            after(memory_slab(3))
            dve.wait_ge(ml_sd, 1)
            link(V.reciprocal(ml_rs[:, :], ml_rs[:, :]))
            link(V.tensor_tensor(ml_y, ml_y, along(ml_rs[:, :], P), ALU.mult))
            V.tensor_tensor(ml_y, ml_y, ml_o[:, :, :].rearrange("p t (h c) -> p (t h) c", c=P),
                            ALU.mult).then_inc(ml_ready, 1)
            out_low(O_FX, se_o, slice(4, 6))
            rows(0, 8)
            after(memory_slab(4))
            rows(1, 9)
            after(memory_slab(5))
            for b in range(2):
                dve.wait_ge(ml_tr, b + 1)
                dve.wait_ge(o_lo_done, O_FX + 1 + b)
                for m in range(2):
                    ins = V.tensor_scalar(se_o[:, m, :], ps[:, b, T * m:T * m + T], pcol("ml_norm_2", 2 * b + m), None, ALU.mult)
                ins.then_inc(ml_fm, 1)
                out_low(O_FX + 1 + b, se_o, slice(2 * b, 2 * b + 2))
            rows(2, 10)
            after(memory_slab(6))
            rows(3, 11)
            fx_masked(1)
            fx_probs(1)
            after(memory_slab(7))
            out_low(O_FX + 3, se_o, slice(6, 8))
            for i in range(3):
                after(first["mix_o"] + i)
            norm(6, x_tm, 1.0, first["mix_o"] + 3, 5)
            after(first["mix_o"] + 3)
            for j in range(4):
                after(first["x_q"] + j)
            link(V.memset(zero_m[:, :], 0.0))
            for u in range(4):
                masked(U_X + u, cr_s, FULL, lambda w, t, c0, c1: zero_m[:, :])
            for u in range(4):
                probs(U_X + u, cr_s, FULL)
            for u in range(4):
                out_low(O_X + u, cr_o, slice(2 * u, 2 * u + 2))
            for i in range(3):
                after(first["x_o"] + i)
            norm(7, x_tm, 1.0, first["x_o"] + 3, 6)
            after(first["x_o"] + 3)
            ffn("ff2")
            norm_tokens(8, x_tm, 1.0, first["ff2"] + 31, 7)
            dve.wait_ge(gain_loaded, 16 * 9)
            for t in range(TT):
                dve.wait_ge(rstd_ready, 17 + t)
                V.scalar_tensor_tensor(xn[:, t, :], x_tm[:, t, :], rstd[:, t:t + 1], gain[:, 0, :],
                                       ALU.mult, ALU.mult).then_inc(final_ready, 1)

        @block.tensor
        def _(pe):
            def three(out, hi_l, lo_l, hi_r, lo_r, start, stop):
                nc.tensor.matmul(out, hi_l, hi_r, start=start, stop=False)
                nc.tensor.matmul(out, hi_l, lo_r, start=False, stop=False)
                return nc.tensor.matmul(out, lo_l, hi_r, start=False, stop=stop)

            def wide_fm(i, hi_x, lo_x, bank, x_first=None, x_ready=xlo_ready, part=2, r=0, per=0):
                wait_slab(pe, i, r, per)
                wh, wl = wview(w_hi, i, "wide"), wview(w_lo, i, "wide")
                for m in range(2):
                    for k in range(KT):
                        f = slice(P * m, P * m + P)
                        if x_first is not None and m == 0 and k % part == 0:
                            pe.wait_ge(x_ready, x_first + k // part + 1)
                        last = three(ps[:, bank, T * m:T * m + T], wh[:, k, f], wl[:, k, f], hi_x[:, k, :], lo_x[:, k, :],
                                     k == 0, k == KT - 1)
                last.then_inc(slab_done, 1)

            def wide_tm(i, hi_x, lo_x, bank, x_first=None):
                wait_slab(pe, i)
                wh, wl = wview(w_hi, i, "wide"), wview(w_lo, i, "wide")
                for t in range(TT):
                    for k in range(KT):
                        f = slice(P * t, P * t + P)
                        last = three(ps[:, bank, T * t:T * t + T], hi_x[:, k, f], lo_x[:, k, f], wh[:, k, :], wl[:, k, :],
                                     k == 0, k == KT - 1)
                last.then_inc(slab_done, 1)

            def tall_half(i, hi_x, lo_x, start, stop, t, base=0, r=0, per=0, signal=False):
                if t == 0:
                    wait_slab(pe, i, r, per)
                wh, wl = wview(w_hi, i, "tall"), wview(w_lo, i, "tall")
                for n in range(2):
                    for k in range(2):
                        f, c = slice(P * t, P * t + P), slice(512 * n, 512 * n + 512)
                        last = three(ps[:, base + 2 * t + n, :], hi_x[:, k, f], lo_x[:, k, f], wh[:, k, c], wl[:, k, c],
                                     start and k == 0, stop and k == 1)
                    if t and n:
                        last.then_inc(slab_done, 1)
                    elif signal:
                        last.then_inc(bank_done, 1)

            def tall(i, hi_x, lo_x, start, stop, base=0, r=0, per=0):
                for t in range(TT):
                    tall_half(i, hi_x, lo_x, start, stop, t, base, r, per, signal=stop)

            mm = nc.tensor.matmul
            fence = chain(pe, pe_step)

            def lora1(w, n, parts, q):
                pe.wait_ge(mixed_ready, q + 2)
                if n == 0:
                    pe.wait_ge(lora1_loaded, 48)
                for bank, lo_c, hi_c in parts:
                    for k in range(KT):
                        last = mm(ps[0:hi_c - lo_c, bank, 0:T], w[:, k, lo_c:hi_c], mixed[:, q % 2, k, :],
                                  start=k == 0, stop=k == KT - 1)
                last.then_inc(lora1_mm, 1)

            for i in range(4):
                wide_fm(i, rx_hi, rx_lo, i % 4, None if i else 0, mix_lo_done, KT // 2)
            lora1(w1, 0, [(4, 0, LORA)], 2)
            lora1(a1, 1, [(5, 0, LORA)], 3)
            pe.wait_ge(mix_lo_done, 3)
            for i in range(4, 8):
                pe.wait_ge(proj_taken, i - 3)
                wide_fm(i, mix_hi, mix_lo, i % 4)
            lora1(g1, 2, [(6, 0, P), (7, P, GLORA)], 5)
            pe.wait_ge(mix_lo_done, 4)

            def aux_bank(g, k):
                n = aux_at(g, k)
                if n >= 2:
                    pe.wait_ge(aux_taken, n - 1)
                return ps[:, n % 2, :]

            def tok(t):
                return slice(P * t, P * t + P)

            def head(h):
                return slice(HD * (h % 2), HD * (h % 2) + HD), h // 2

            def step(g, k):
                z = aux_bank(g, k)
                d_g, rb_g, ak_g, rk_g = d_m[g % 2], rb_m[g % 2], ak_m[g % 2], rk_m[g % 2]
                v = lambda t, h: v_tm[:, t, 256 * g + HD * h:256 * g + HD * h + HD]
                t = int(k in (A_U1, A_SA1))
                if k in (A_W, A_A):
                    pe.wait_ge(lora2_loaded, 32 * (g + 1))
                    w, src = ((w2, tanh_w), (a2, lora_a))[k == A_A]
                    for m in range(2):
                        last = mm(z[:, T * m:T * m + T], w[:, P * m:P * m + P], src[:, :], start=True, stop=True)
                elif k == A_KK:
                    pe.wait_ge(kk2_ready, g + 1)
                    last = mm(z, rc("headones"), kmod[:, :, :].rearrange("p a b -> p (a b)"), start=True, stop=True)
                elif k == A_BON:
                    pe.wait_ge(rkr_ready, g + 1)
                    for t in range(TT):
                        for m in range(2):
                            last = mm(z[:, 4 * t + 2 * m:4 * t + 2 * m + 2], sw[:, 2 * m + t, :], rk_sel[:, 2 * g + m, :],
                                      start=True, stop=True)
                elif k == A_BK:
                    pe.wait_ge(prep_ready, g + 1)
                    for s, src in ((0, b_t), (1, k_t)):
                        for m in range(2):
                            last = nc.tensor.transpose(z[:, P * (2 * s + m):P * (2 * s + m) + P], src[:, 2 * m, :], ident)
                elif k == A_G:
                    pe.wait_ge(gate_lora_loaded, 64 * (g + 1))
                    for t in range(TT):
                        mm(z[:, T * t:T * t + T], sig_g[:, tok(t)], g2[:, :], start=True, stop=False)
                        last = mm(z[:, T * t:T * t + T], sig_g2[:, tok(t)], g2b[:, :], start=False, stop=True)
                elif k in (A_U0, A_U1):
                    for s, h in enumerate(HEADS):
                        q, m = head(h)
                        o = z[:, HD * h:HD * h + HD]
                        if t:
                            if s == 0:
                                pe.wait_ge(aux_taken, aux_at(g, A_ST) + 1)
                            if s == 2:
                                fence(last)
                            mm(o, ar[q, 2 * g + m, t, 0, :], state[q, m, :], start=True, stop=False)
                        last = mm(o, ak_g[:, t, s], v(t, h), start=not t, stop=True)
                elif k in (A_SA0, A_SA1):
                    pe.wait_ge(aux_taken, aux_at(g, A_U1 if t else A_U0) + 1)
                    pe.wait_ge(inv_taken[t], INV * (g + 1))
                    for s, h in enumerate(HEADS):
                        last = mm(z[:, HD * h:HD * h + HD], d_g[:, t, s], u_m[:, HD * h:HD * h + HD], start=True, stop=True)
                elif k == A_ST:
                    pe.wait_ge(aux_taken, aux_at(g, A_SA0) + 1)
                    for h in range(4):
                        q, m = head(h)
                        o = z[q, HD * m:HD * m + HD]
                        mm(o, bk_tm[:, g % 2, 0, m, q], sa_m[:, 0, HD * h:HD * h + HD], start=True, stop=False)
                        last = mm(o, bk_tm[:, g % 2, 1, m, q], v(0, h), start=False, stop=True)
                elif k == A_Y:
                    pe.wait_ge(aux_taken, aux_at(g, A_SA1) + 1)
                    for t in range(TT):
                        for s, h in enumerate(HEADS):
                            q, m = head(h)
                            if t and s in (0, 2):
                                fence(last)
                            o = z[:, 256 * t + HD * h:256 * t + HD * h + HD]
                            if t:
                                mm(o, ar[q, 2 * g + m, t, 1, :], state[q, m, :], start=True, stop=False)
                            mm(o, rb_g[:, t, s], sa_m[:, t, HD * h:HD * h + HD], start=not t, stop=False)
                            last = mm(o, rk_g[:, t, s], v(t, h), start=False, stop=True)
                else:
                    pe.wait_ge(y_ready, g + 1)
                    y2 = y_sb[:, :, :].rearrange("p (t h) c -> p t (h c)", t=TT)
                    for m in range(2):
                        for t in range(TT):
                            last = nc.tensor.transpose(z[:, T * m + P * t:T * m + P * t + P], y2[:, t, P * m:P * m + P], ident)
                last.then_inc(aux_ready, 1)

            for i in range(8, 12):
                pe.wait_ge(proj_taken, i - 1)
                wide_tm(i, rx_hi, rx_lo, v_bank(i))
                if i == 8:
                    pe.wait_ge(proj_taken, 6)
                    pe.wait_ge(lora1_out, 4)
                    pe.wait_ge(consts_loaded, 32)
                    for k in (A_W, A_A, A_KK):
                        step(0, k)
                elif i == 10:
                    step(0, A_BON)
            pe.wait_ge(lora1_out, 4)
            step(0, A_BK)
            for g in range(4):
                pe.wait_ge(a_ready, g + 1)
                pe.wait_ge(prep_ready, g + 1)
                if g == 0:
                    pe.wait_ge(proj_taken, 12)
                for t in range(TT):
                    if g:
                        pe.wait_ge(inv_taken[t], INV * g)
                    for s, h in enumerate(HEADS):
                        q, m = head(h)
                        last = mm(ps[:, 2 + 3 * t + s // 2, 256 * (s % 2):256 * (s % 2) + 256], b_t[q, 2 * m + t, :],
                                  ar[q, 2 * g + m, t, :, :].rearrange("p s c -> p (s c)"), start=True, stop=True)
                    last.then_inc(inv_ready[t], 1)
                for half in range(2):
                    for t in range(TT):
                        for s in (2 * half, 2 * half + 1):
                            q, m = head(HEADS[s])
                            last = mm(ps[:, 4 + 3 * t, P * s:P * s + P], ar[q, 2 * g + m, t, 0, :], b_t[q, 2 * m + t, :],
                                      start=True, stop=True)
                        if half:
                            last.then_inc(inv_ready[t], 1)
                    if not half:
                        fence(last)
                for t in range(TT):
                    pe.wait_ge(inv_taken[t], INV * g + 1)
                    for s, h in enumerate(HEADS):
                        q, m = head(h)
                        last = mm(ps[:, 2 + 3 * t + s // 2, 256 * (s % 2):256 * (s % 2) + 256], k_t[q, 2 * m + t, :],
                                  ar[q, 2 * g + m, t, :, :].rearrange("p s c -> p (s c)"), start=True, stop=True)
                    last.then_inc(inv_ready[t], 1)
                for slot in range(12):
                    n = slot // 2 + 1
                    for t in range(TT):
                        pe.wait_ge(inv_taken[t], INV * g + 2 + slot)
                        if slot == 0:
                            pe.wait_ge(nt_taken[t], g + 1)
                        for h in range(4):
                            if slot % 2 == 0:
                                last = mm(ps[:, 2 + 3 * t, P * h:P * h + P], nt_m[:, t, h], d_m[g % 2][:, t, h],
                                          start=True, stop=True)
                            else:
                                if n < NL - 1:
                                    mm(ps[:, 4 + 3 * t, P * h:P * h + P], w_m[:, t, h], dt_m[:, t, h], start=True, stop=True)
                                last = mm(ps[:, 3 + 3 * t, P * h:P * h + P], dt_m[:, t, h], w_m[:, t, h],
                                          start=True, stop=True)
                        last.then_inc(inv_ready[t], 1)
                        if t == 0:
                            for m, k in slot_steps(g, slot):
                                step(m, k)
            def out_part(i, t):
                tall_half(first["rwkv_o"] + i, mix_hi[:, 2 * i:2 * i + 2, :], mix_lo[:, 2 * i:2 * i + 2, :], i == 0, False, t, 4)

            halves = [(i, t) for i in range(3) for t in range(TT)]
            for n, k in tail_steps:
                step(n, k)
                if n == 3 and k in (A_ST, A_U1, A_SA1, A_Y):
                    if k == A_ST:
                        pe.wait_ge(rwkv_lo_done, 3)
                        pe.wait_ge(inv_taken[1], INV * 4)
                    for i, t in (halves if k == A_Y else halves[:1]):
                        out_part(i, t)
                    halves = halves[1:]
            pe.wait_ge(rwkv_lo_done, 4)
            tall(first["rwkv_o"] + 3, mix_hi[:, 6:8, :], mix_lo[:, 6:8, :], False, True, 4)

            def transposes(q):
                n = FM_NORMS.index(q)
                for t in range(TT):
                    if t:
                        pe.wait_ge(xn_act, n + 1)
                        pe.wait_ge(xn_dve, n + 1)
                    else:
                        pe.wait_ge(xn0_ready, n + 1)
                        if q == 0:
                            pe.wait_ge(stat_ready, 2)
                    for i in range(4):
                        for m in range(2):
                            k = 2 * i + m
                            last = nc.tensor.transpose(ps[:, 4 + i, T * m + P * t:T * m + P * t + P],
                                                       xn[:, t, P * k:P * k + P], ident)
                        if t:
                            last.then_inc(tr_ready, 1)

            def product(section, count):
                pe.wait_ge(o_taken, count)
                for i in range(4):
                    pe.wait_ge(o_lo_done, count - 3 + i if section != "mix_o" else count - (i < 3))
                    tall(first[section] + i, mix_hi[:, 2 * i:2 * i + 2, :], mix_lo[:, 2 * i:2 * i + 2, :], i == 0, i == 3)

            def ffn(name, q):
                s0, n, h0, per, rounds = FFN[name]
                slabs = per * (2 if name == "ff2" else 3)

                def step(j, r=0):
                    up, down = ffn_slabs(name, j)
                    if j < n:
                        if h0 + j >= 2:
                            pe.wait_ge(ffn_taken, h0 + j - 1 + r * per)
                        for m, i in enumerate(up):
                            wide_fm(i, x_hi, x_lo, 4 + 2 * (j % 2) + m, 4 * FM_NORMS.index(q) if j == 0 and m == 0 else None,
                                    r=r, per=slabs)
                    if j:
                        pe.wait_ge(hid_ready, h0 + j + r * per)
                        view = lambda w: w[:, (j - 1) % 2, :].rearrange("p (k n) -> p k n", k=2)
                        tall(down, view(hid_hi), view(hid_lo), j == 1, j == n, r=r, per=slabs)

                for j in range(FFN_PEEL):
                    step(j)
                with pe.Fori(0, rounds) as r:
                    for j in range(FFN_PEEL, FFN_PEEL + per):
                        step(j, r)
                for j in range(FFN_PEEL + per * rounds, n + 1):
                    step(j)

            def project(n, i, wide, x_first=None):
                if n >= 3:
                    pe.wait_ge(p_taken, max(n - 2, P_FIRST["x_q"]) if n >= P_FIRST["x_q"] else n - 2)
                wide(i, x_hi, x_lo, n % 3, x_first)

            def p_transposes(u, s, kind):
                pe.wait_ge(p_ready, u + 1)
                for n, (c0, tq, tk) in enumerate(BLOCKS[kind]):
                    at = (0 if tk == 0 else (P if kind == "causal" else T)) + P * tq if kind == "full" else P * n
                    last = nc.tensor.transpose(ps[:, 4 + u % 4, at:at + P], s[:, u % 4, c0:c0 + P], ident)
                last.then_inc(pt_ready, 1)

            transposes(0)
            ffn("ffn0", 0)
            transposes(1)
            def rotate(g, n):
                if g == 0 and n == 0:
                    pe.wait_ge(late_loaded, 80)
                if g > 1 and n == 0:
                    pe.wait_ge(o_taken, g - 1)
                if n or g:
                    pe.wait_ge(rope_done, 2 * g + n)
                pe.wait_ge(p_taken, 3 * g + n + 1)
                mm(ps[:, 3, :], rope_c[:, 2 * T:2 * T + P], (ma_q, ma_k)[n][:, :, :].rearrange("p a b -> p (a b)"),
                   start=True, stop=True).then_inc(rot_ready, 1)

            for g in range(-1, 4):
                if g >= 0:
                    pe.wait_ge(rope_done, 2 * g + 2)
                    if g:
                        pe.wait_ge(pt_taken, 4 * g)
                    for s, h in enumerate(HEADS):
                        q, m = head(h)
                        for t, c0, c1 in CAUSAL:
                            last = mm(ps[:, 4 + s, c0:c1], ma_q2[q, m, tok(t)], ma_k2[q, m, 0:c1 - c0], start=True, stop=True)
                        last.then_inc(scores_ready, 1)
                if g < 3:
                    n = 3 * (g + 1)
                    project(n, first["qkv"] + n, wide_fm, 4 if g < 0 else None)
                    project(n + 1, first["qkv"] + n + 1, wide_fm)
                    rotate(g + 1, 0)
                    project(n + 2, first["qkv"] + n + 2, wide_tm)
                    rotate(g + 1, 1)
                if g >= 0:
                    for s in range(4):
                        p_transposes(U_MOBA + 4 * g + s, ma_s, "causal")
                    if g < 3:
                        pe.wait_ge(rope_done, 2 * g + 4)
                    for s, h in enumerate(HEADS):
                        q, m = head(h)
                        pe.wait_ge(pt_taken, 4 * g + s + 1)
                        v = lambda t: ma_vv[:, g % 2, t, HD * h:HD * h + HD]
                        mm(ps[q, 3, T * m:T * m + T], v(0), ma_p[:, s, 0:T], start=True, stop=False)
                        last = mm(ps[q, 3, T * m + P:T * m + T], v(1), ma_p[:, s, T:T + P], start=False, stop=True)
                    last.then_inc(o_ready, 1)
            product("moba_o", 4)
            transposes(2)
            ffn("ffn1", 2)
            transposes(4)
            def gates():
                pe.wait_ge(xhi_ready, 16)
                pe.wait_ge(late_loaded, 80)
                for k in range(KT):
                    mm(ps[0:12, 3, 0:T], gate_w[:, k, 0:12], x_fm[:, k, :], start=k == 0, stop=k == KT - 1)
                for k in range(KT):
                    last = mm(ps[0:4, 3, T:2 * T], gate_w[:, k, 12:16], x_fm[:, k, :], start=k == 0, stop=k == KT - 1)
                last.then_inc(gate_mm, 1)

            def gate_columns():
                pe.wait_ge(gate_rows, 1)
                for t in range(TT):
                    last = nc.tensor.transpose(ps[:, 3, HD * t:HD * t + HD], gst[:, tok(t)], ident[0:HD, 0:HD])
                last.then_inc(gate_tr, 1)

            def memory_product(n):
                pe.wait_ge(p_taken, P_FIRST["x_k"] + n)
                (wide_tm if n >= 4 else wide_fm)(memory_slab(n), x_hi, x_lo, 2)

            def row(n):
                if n:
                    pe.wait_ge(row_taken, n)
                else:
                    pe.wait_ge(gate_cols, 1)
                r, src = (4, gi) if n < 4 else (12, gst)
                mm(ps[:, 3, 0:T], gsel[0:r, P * n:P * n + P], src[0:r, :], start=True, stop=True).then_inc(row_ready, 1)

            for name, n, kind in (("ml_qk", 4, wide_fm), ("ml_v", 2, wide_tm), ("ml_o", 2, wide_tm),
                                  ("fx_qk", 4, wide_fm), ("fx_v", 2, wide_tm)):
                for j in range(n):
                    project(P_FIRST[name] + j, first[name] + j, kind, 12 if name == "ml_qk" and j == 0 else None)
                    if name == "ml_qk" and j == 0:
                        gates()
                    if name == "fx_qk":
                        row(j)
                if name == "ml_v":
                    transposes(5)
                    gate_columns()
            def fx_scores(g):
                pe.wait_ge(pt_taken, U_FX + 4 * g)
                for s, h in enumerate(HEADS):
                    q, m = head(h)
                    for t, c0, c1 in CAUSAL:
                        last = mm(ps[:, 4 + s, c0:c1], fx_q[q, 2 * g + m, tok(t)], fx_k[q, 2 * g + m, 0:c1 - c0],
                                  start=True, stop=True)
                    last.then_inc(scores_ready, 1)

            def fx_outputs(g):
                for s in range(4):
                    p_transposes(U_FX + 4 * g + s, se_s, "causal")
                pe.wait_ge(row_taken, 8 + 4 * g)
                for s, h in enumerate(HEADS):
                    q, m = head(h)
                    pe.wait_ge(pt_taken, U_FX + 4 * g + s + 1)
                    v = lambda t: fx_v[:, t, 256 * g + HD * h:256 * g + HD * h + HD]
                    mm(ps[q, 3, T * m:T * m + T], v(0), se_p[:, s, 0:T], start=True, stop=False)
                    last = mm(ps[q, 3, T * m + P:T * m + T], v(1), se_p[:, s, T:T + P], start=False, stop=True)
                last.then_inc(o_ready, 1)

            def ml_transposes():
                pe.wait_ge(ml_ready, 1)
                for b in range(2):
                    for m in range(2):
                        for t in range(TT):
                            last = nc.tensor.transpose(ps[:, b, T * m + P * t:T * m + P * t + P],
                                                       ml_y[:, 4 * t + 2 * b + m, :], ident)
                    last.then_inc(ml_tr, 1)

            pe.wait_ge(silu_ready, 2)
            for u in range(4):
                for t, c0, c1 in CAUSAL:
                    last = mm(ps[:, 4 + u, c0:c1], conv_out[:, u, tok(t)], conv_out[:, 4 + u, 0:c1 - c0], start=True, stop=True)
                last.then_inc(scores_ready, 1)
            pe.wait_ge(xlo_ready, 20)
            pe.wait_ge(p_taken, P_FIRST["fx_v"] + 2)
            memory_product(0)
            memory_product(1)
            for u in range(4):
                p_transposes(U_ML + u, se_s, "causal")
            row(4)
            memory_product(2)
            row(5)
            for t in range(TT):
                for u in range(4):
                    pe.wait_ge(pt_taken, U_ML + u + 1)
                    v = lambda tk: ml_v[:, tk, P * u:P * u + P]
                    o = ps[:, t, P * u:P * u + P]
                    last = mm(o, se_p[:, u, P * t:P * t + P], v(0), start=True, stop=not t)
                    if t:
                        last = mm(o, se_p[:, u, T:T + P], v(1), start=False, stop=True)
                last.then_inc(o_ready, 1)
                row(6 + t)
            fx_scores(0)
            memory_product(3)
            fx_outputs(0)
            memory_product(4)
            pe.wait_ge(o_taken, O_FX + 1)
            row(8)
            memory_product(5)
            row(9)
            ml_transposes()
            row(10)
            memory_product(6)
            row(11)
            fx_scores(1)
            memory_product(7)
            fx_outputs(1)
            pe.wait_ge(p_taken, P_FIRST["x_q"])
            product("mix_o", 8)
            transposes(6)
            for j in range(4):
                project(P_FIRST["x_q"] + j, first["x_q"] + j, wide_fm, None if j else 20)
            pe.wait_ge(p_taken, P_FIRST["x_q"] + 4)
            for u in range(4):
                for t in range(TT):
                    for k in range(2):
                        last = mm(ps[:, 4 + u, T * t:T * t + T], xq_fm[:, 2 * u + k, tok(t)], xk_fm[:, 2 * u + k, 0:T],
                                  start=k == 0, stop=k == 1)
                last.then_inc(scores_ready, 1)
            for u in range(4):
                p_transposes(U_X + u, cr_s, "full")
            for u in range(4):
                pe.wait_ge(pt_taken, U_X + u + 1)
                for m in range(2):
                    for tk in range(TT):
                        last = mm(ps[:, u, T * m:T * m + T], gain[:, tk, T * u + P * m:T * u + P * m + P],
                                  cr_p[:, u, T * tk:T * tk + T], start=tk == 0, stop=tk == 1)
                last.then_inc(o_ready, 1)
            product("x_o", 12)
            transposes(7)
            ffn("ff2", 7)


def lay_out(inputs):
    a = {k: np.ascontiguousarray(v) for k, v in inputs.items()}
    plan, _ = weight_plan()
    slabs = np.empty((len(plan), P, SLAB), np.float32)
    for i, (kind, src, layer, r0, c0) in enumerate(plan):
        w = a[src]
        w = w.reshape((-1,) + w.shape[-2:])[layer]
        if kind == "wide":
            slabs[i] = w[:, c0:c0 + 256].reshape(KT, P, 256).transpose(1, 0, 2).reshape(P, SLAB)
        else:
            slabs[i] = w[P * r0:P * (r0 + 2)].reshape(2, P, C).transpose(1, 0, 2).reshape(P, SLAB)
    tokens = lambda x: np.ascontiguousarray(x.reshape(TT, P, C).transpose(1, 0, 2))
    features = lambda w: np.ascontiguousarray(w.reshape(-1, P, w.shape[-1]).transpose(1, 0, 2))
    cols = {}
    for name, n in PARAMS:
        cols[name] = a[name].reshape(n, P).T
    table = constants()
    out = {
        "weights": slabs,
        "x": tokens(a["x"]),
        "xT": features(np.ascontiguousarray(a["x"][0].T)),
        "mem": tokens(a["mem_2"]),
        "params": np.ascontiguousarray(np.concatenate([cols[n] for n, _ in PARAMS], axis=1)),
        "w1": features(a["rwkv_w1"][0]), "a1": features(a["rwkv_a1"][0]), "g1": features(a["rwkv_g1"][0]),
        "w2": a["rwkv_w2"][0], "a2": a["rwkv_a2"][0], "g2": a["rwkv_g2"][0],
        "gn_g": a["rwkv_gn_g"], "gn_b": a["rwkv_gn_b"],
        "mix_g": a["ln_mix_g"], "mix_b": a["ln_mix_b"], "ffn_g": a["ln_ffn_g"], "ffn_b": a["ln_ffn_b"],
        "final_g": a["ln_f_2"].reshape(1, C),
        "gate_w": features(np.concatenate([a["w_in_2"][0][:, 2052:2056], a["w_in_2"][0][:, 3592:3600],
                                           a["w_in_2"][0][:, 2048:2052]], axis=1)),
        "gate_b": np.concatenate([a["ml_b_f_2"][0], a["fx_b_f_2"][0], a["ml_b_i_2"][0]]).reshape(16, 1),
    }
    for which, names in CONST_SETS.items():
        out["const_" + which] = np.ascontiguousarray(np.concatenate([table[n] for n in names], axis=1))
    return out


def kernel(**inputs):
    import concourse.bacc as bacc
    from concourse.bass_utils import run_bass_kernel_spmd

    nc = bacc.Bacc("TRN2", target_bir_lowering=False, num_devices=1)
    arrays = lay_out(inputs)
    d = {k: nc.dram_tensor("in_" + k, v.shape, F32, kind="ExternalInput").ap() for k, v in arrays.items()}
    out = nc.dram_tensor("out", (P, TT, C), F32, kind="ExternalOutput").ap()
    build(nc, d, out)
    r = run_bass_kernel_spmd(nc, [{"in_" + k: v for k, v in arrays.items()}], core_ids=[0])
    got = r.results[0]["out"]
    return np.ascontiguousarray(got.transpose(1, 0, 2)).reshape(1, T, C)
```
